# Optimizing a Trainium2 kernel written in Bass

```python
import math
import jax, jax.numpy as jnp
from jax import lax
import numpy as np

D_MODEL = 1024
BATCH = 1
SEQ = 512
DEPTH = 1
DEC_BATCH = 8
DEC_SEQ = 4
PAST_LEN = 2048
PAGE_SIZE = 128

HEAD_DIM = 64
N_HEADS_A = 12
N_HEADS_B = 4
N_HEADS = N_HEADS_A + N_HEADS_B
WIDTH_A = N_HEADS_A * HEAD_DIM
WIDTH_B = N_HEADS_B * HEAD_DIM
DIL_PATTERNS = ((128, 1), (512, 4), (2048, 16))
MAX_WINDOW = 2048
BAND_BLOCK = 128
N_IDX_HEADS = 8
IDX_DIM = 64
TOPK_MAX = 256
Q_BLOCK = 128
N_BUCKETS = 32
REL_MAX_DIST = 2048
D_FF = 2816
D_PLE = 256
PROJ_SIZES = (WIDTH_A, WIDTH_A, WIDTH_A, WIDTH_B, HEAD_DIM, HEAD_DIM, N_IDX_HEADS * IDX_DIM, IDX_DIM, N_IDX_HEADS)
D_PROJ = sum(PROJ_SIZES)
B_ROW = 2 * HEAD_DIM + IDX_DIM
ALPHA = (2 * DEPTH) ** 0.25
BETA = (8 * DEPTH) ** -0.25
LN_EPS = 1e-5

kernel_name = "hymba_dilated_dsa_macaron_decoder_step"

def layer_norm(x, g, b):
    xf = x.astype(jnp.float32)
    mu = xf.mean(-1, keepdims=True)
    var = jnp.square(xf - mu).mean(-1, keepdims=True)
    return ((xf - mu) * lax.rsqrt(var + LN_EPS) * g + b).astype(x.dtype)

def swiglu(x, wi, wo):
    gate, up = jnp.split(x @ wi, 2, axis=-1)
    return (jax.nn.silu(gate) * up) @ wo

def t5_bucket(dist):
    dist = jnp.maximum(dist, 0)
    exact = N_BUCKETS // 2
    scaled = jnp.log(jnp.maximum(dist, 1).astype(jnp.float32) / exact) / math.log(REL_MAX_DIST / exact)
    large = exact + (scaled * (N_BUCKETS - exact)).astype(jnp.int32)
    return jnp.where(dist < exact, dist, jnp.minimum(large, N_BUCKETS - 1))

def pre_mix(x, g, b, wi, wo):
    return layer_norm(ALPHA * x + 0.5 * swiglu(x, wi, wo), g, b)

def project(h, w_in, kidx_g, kidx_b):
    offs = np.cumsum(PROJ_SIZES)[:-1].tolist()
    qa, ka, va, qb, kb, vb, qi, ki, wi = jnp.split(h @ w_in, offs, axis=-1)
    bsz, t = h.shape[:2]
    scale = HEAD_DIM ** -0.5
    qa = qa.reshape(bsz, t, N_HEADS_A, HEAD_DIM) * scale
    ka = ka.reshape(bsz, t, N_HEADS_A, HEAD_DIM)
    va = va.reshape(bsz, t, N_HEADS_A, HEAD_DIM)
    qb = qb.reshape(bsz, t, N_HEADS_B, HEAD_DIM) * scale
    qi = qi.reshape(bsz, t, N_IDX_HEADS, IDX_DIM)
    ki = layer_norm(ki, kidx_g, kidx_b)
    return qa, ka, va, qb, kb, vb, qi, ki, wi

def post_mix(h, o_a, o_b, w_out, g1, b1, g2, b2, wi2, wo2, p, ple_proj, ple_gate):
    bsz, t = h.shape[:2]
    o = jnp.concatenate([o_a.reshape(bsz, t, WIDTH_A), o_b.reshape(bsz, t, WIDTH_B)], -1).astype(h.dtype) @ w_out
    h = layer_norm(ALPHA * h + o, g1, b1)
    h = layer_norm(ALPHA * h + 0.5 * swiglu(h, wi2, wo2), g2, b2)
    return h + (p @ ple_proj) * jax.nn.sigmoid(h @ ple_gate)

def dilated_band_prompt(q, k, v, bias_a, window, dil):
    b, s, h, dh = q.shape
    n = s // dil
    nb = -(-n // BAND_BLOCK)
    pad = nb * BAND_BLOCK - n
    sub_w = window // dil

    def to_sub(a):
        rest = a.shape[2:]
        a = a.reshape(b, n, dil, *rest).swapaxes(1, 2).reshape(b * dil, n, *rest)
        a = jnp.pad(a, ((0, 0), (0, pad)) + ((0, 0),) * len(rest))
        return a.reshape(b * dil, nb, BAND_BLOCK, *rest)

    def from_sub(a):
        rest = a.shape[3:]
        a = a.reshape(b * dil, nb * BAND_BLOCK, *rest)[:, :n]
        return a.reshape(b, dil, n, *rest).swapaxes(1, 2).reshape(b, s, *rest)

    def with_prev(a):
        prev = jnp.pad(a, ((0, 0), (1, 0), (0, 0), (0, 0), (0, 0)))[:, :-1]
        return jnp.concatenate([prev, a], axis=2)

    qs, ks, vs = to_sub(q), with_prev(to_sub(k)), with_prev(to_sub(v))
    i = jnp.arange(BAND_BLOCK)[:, None]
    j = jnp.arange(2 * BAND_BLOCK)[None, :]
    delta = i - j + BAND_BLOCK
    in_band = (delta >= 0) & (delta <= sub_w)
    has_key = (jnp.arange(nb)[:, None, None] > 0) | (j >= BAND_BLOCK)[None]
    valid = in_band[None] & has_key
    bias = bias_a[t5_bucket(delta * dil)].transpose(2, 0, 1)
    logits = jnp.einsum('znqhd,znkhd->znhqk', qs, ks).astype(jnp.float32) + bias[None, None]
    logits = jnp.where(valid[None, :, None], logits, -jnp.inf)
    m = logits.max(-1, keepdims=True)
    pr = jnp.exp(logits - m)
    l = pr.sum(-1, keepdims=True)
    o = jnp.einsum('znhqk,znkhd->znqhd', pr / l, vs.astype(jnp.float32))
    lse = (m + jnp.log(l))[..., 0].swapaxes(2, 3)
    return from_sub(o), from_sub(lse)

def dilated_gather_step(q, k_all, v_all, bias_a, window, dil, w_buf):
    t = q.shape[1]
    steps = jnp.arange(window // dil + 1) * dil
    idx = w_buf + jnp.arange(t)[:, None] - steps[None]
    valid = idx >= 0
    idx_c = jnp.maximum(idx, 0)
    kg, vg = k_all[:, idx_c], v_all[:, idx_c]
    bias = bias_a[t5_bucket(steps)].T
    logits = jnp.einsum('bthd,btjhd->bthj', q, kg).astype(jnp.float32) + bias[None, None]
    logits = jnp.where(valid[None, :, None, :], logits, -jnp.inf)
    m = logits.max(-1, keepdims=True)
    pr = jnp.exp(logits - m)
    l = pr.sum(-1, keepdims=True)
    o = jnp.einsum('bthj,btjhd->bthd', pr / l, vg.astype(jnp.float32))
    return o, (m + jnp.log(l))[..., 0]

def combine_dilations(outs, lses):
    w = jax.nn.softmax(jnp.stack(lses), axis=0)[..., None]
    return (w * jnp.stack(outs)).sum(0)

def indexer_scores(qi, wi, ki):
    s = jax.nn.relu(jnp.einsum('bthd,bsd->bths', qi, ki).astype(jnp.float32))
    return jnp.einsum('bths,bth->bts', s, wi.astype(jnp.float32)) * (IDX_DIM ** -0.5 * N_IDX_HEADS ** -0.5)

def sparse_attend(q, kg, vg, idx, pos_q, bias_b):
    dist = pos_q[None, :, None] - idx
    bias = bias_b[t5_bucket(dist)].transpose(0, 1, 3, 2)
    logits = jnp.einsum('bthd,btkd->bthk', q, kg).astype(jnp.float32) + bias
    logits = jnp.where((dist >= 0)[:, :, None, :], logits, -jnp.inf)
    p = jax.nn.softmax(logits, axis=-1)
    return jnp.einsum('bthk,btkd->bthd', p, vg.astype(jnp.float32))

_row_gather = jax.vmap(lambda a, i: a[i])

def dsa_prompt(qb, kb, vb, qi, wi, ki, bias_b):
    b, s = qb.shape[:2]
    k_sel = min(TOPK_MAX, s // 4)
    nblk = s // Q_BLOCK
    blocks = lambda a: a.reshape(b, nblk, Q_BLOCK, *a.shape[2:]).swapaxes(0, 1)
    key_pos = jnp.arange(s)

    def one_block(args):
        q_blk, qi_blk, wi_blk, start = args
        pos_q = start + jnp.arange(Q_BLOCK)
        score = indexer_scores(qi_blk, wi_blk, ki)
        score = jnp.where(key_pos[None, None, :] <= pos_q[None, :, None], score, -jnp.inf)
        _, idx = lax.top_k(score, k_sel)
        return sparse_attend(q_blk, _row_gather(kb, idx), _row_gather(vb, idx), idx, pos_q, bias_b)

    starts = jnp.arange(nblk, dtype=jnp.int32) * Q_BLOCK
    out = lax.map(one_block, (blocks(qb), blocks(qi), blocks(wi), starts))
    return out.swapaxes(0, 1).reshape(b, s, N_HEADS_B, HEAD_DIM)

def dsa_step(qb, kb, vb, qi, wi, ki, cache_l, page_table, bias_b):
    bd, t = qb.shape[:2]
    past = page_table.shape[1] * PAGE_SIZE
    total = past + t
    k_sel = min(TOPK_MAX, total // 4)
    ki_past = cache_l[page_table, :, 2 * HEAD_DIM:].reshape(bd, past, IDX_DIM)
    ki_all = jnp.concatenate([ki_past.astype(ki.dtype), ki], axis=1)
    pos_q = past + jnp.arange(t)
    score = indexer_scores(qi, wi, ki_all)
    score = jnp.where(jnp.arange(total)[None, None, :] <= pos_q[None, :, None], score, -jnp.inf)
    _, idx = lax.top_k(score, k_sel)
    pidx = jnp.minimum(idx, past - 1)
    phys = _row_gather(page_table, pidx // PAGE_SIZE)
    rows_past = cache_l[phys, pidx % PAGE_SIZE, :2 * HEAD_DIM]
    kv_new = jnp.concatenate([kb, vb], axis=-1)
    rows_new = _row_gather(kv_new, jnp.clip(idx - past, 0, t - 1))
    rows = jnp.where((idx < past)[..., None], rows_past.astype(kv_new.dtype), rows_new)
    return sparse_attend(qb, rows[..., :HEAD_DIM], rows[..., HEAD_DIM:], idx, pos_q, bias_b)

def setup_inputs(seed: int = 0) -> dict:
    key = jax.random.key(seed)
    ks = jax.random.split(key, 24)
    n_pages = PAST_LEN // PAGE_SIZE
    n_used = DEC_BATCH * n_pages
    n_pool = n_used + max(1, n_used // 4)
    w_buf = min(MAX_WINDOW, PAST_LEN)
    nrm = lambda k, shape, scale: jax.random.normal(k, shape, jnp.float32) * scale
    page_table = jax.random.permutation(ks[6], n_pool)[:n_used].reshape(DEC_BATCH, n_pages).astype(jnp.int32)
    return {
        "x_prompt": nrm(ks[0], (BATCH, SEQ, D_MODEL), 1.0),
        "x_sample": nrm(ks[1], (DEC_BATCH, DEC_SEQ, D_MODEL), 1.0),
        "cache_a_kv": nrm(ks[2], (DEPTH, DEC_BATCH, w_buf, 2, N_HEADS_A, HEAD_DIM), 1.0),
        "cache_b": nrm(ks[3], (DEPTH, n_pool, PAGE_SIZE, B_ROW), 1.0),
        "page_table": page_table,
        "p_prompt": nrm(ks[4], (DEPTH, BATCH, SEQ, D_PLE), 1.0),
        "p_sample": nrm(ks[5], (DEPTH, DEC_BATCH, DEC_SEQ, D_PLE), 1.0),
        "ln_g": 1.0 + nrm(ks[7], (DEPTH, 3, D_MODEL), 0.02),
        "ln_b": nrm(ks[8], (DEPTH, 3, D_MODEL), 0.02),
        "ffn1_wi": nrm(ks[9], (DEPTH, D_MODEL, 2 * D_FF), D_MODEL ** -0.5),
        "ffn1_wo": nrm(ks[10], (DEPTH, D_FF, D_MODEL), BETA * D_FF ** -0.5),
        "w_in": nrm(ks[11], (DEPTH, D_MODEL, D_PROJ), D_MODEL ** -0.5),
        "kidx_ln_g": 1.0 + nrm(ks[12], (DEPTH, IDX_DIM), 0.02),
        "kidx_ln_b": nrm(ks[13], (DEPTH, IDX_DIM), 0.02),
        "w_out": nrm(ks[14], (DEPTH, D_MODEL, D_MODEL), BETA * D_MODEL ** -0.5),
        "ffn2_wi": nrm(ks[15], (DEPTH, D_MODEL, 2 * D_FF), D_MODEL ** -0.5),
        "ffn2_wo": nrm(ks[16], (DEPTH, D_FF, D_MODEL), BETA * D_FF ** -0.5),
        "ple_proj": nrm(ks[17], (DEPTH, D_PLE, D_MODEL), D_PLE ** -0.5),
        "ple_gate": nrm(ks[18], (DEPTH, D_MODEL, D_MODEL), D_MODEL ** -0.5),
        "rel_bias": nrm(ks[19], (N_BUCKETS, N_HEADS), 0.5),
    }

def reference(x_prompt, x_sample, cache_a_kv, cache_b, page_table, p_prompt, p_sample,
              ln_g, ln_b, ffn1_wi, ffn1_wo, w_in, kidx_ln_g, kidx_ln_b, w_out,
              ffn2_wi, ffn2_wo, ple_proj, ple_gate, rel_bias):
    bias_a = rel_bias[:, :N_HEADS_A]
    bias_b = rel_bias[:, N_HEADS_A:]
    xp, xs = x_prompt, x_sample
    a_prompt, a_sample, b_prompt, b_sample = [], [], [], []
    for i in range(DEPTH):
        hp = pre_mix(xp, ln_g[i, 0], ln_b[i, 0], ffn1_wi[i], ffn1_wo[i])
        qa, ka, va, qb, kb, vb, qi, ki, wi = project(hp, w_in[i], kidx_ln_g[i], kidx_ln_b[i])
        outs, lses = [], []
        for window, dil in DIL_PATTERNS:
            o, l = dilated_band_prompt(qa, ka, va, bias_a, window, dil)
            outs.append(o)
            lses.append(l)
        o_a = combine_dilations(outs, lses)
        o_b = dsa_prompt(qb, kb, vb, qi, wi, ki, bias_b)
        xp = post_mix(hp, o_a, o_b, w_out[i], ln_g[i, 1], ln_b[i, 1], ln_g[i, 2], ln_b[i, 2],
                      ffn2_wi[i], ffn2_wo[i], p_prompt[i], ple_proj[i], ple_gate[i])
        s = hp.shape[1]
        a_prompt.append(jnp.stack([ka, va], axis=2)[:, s - min(MAX_WINDOW, s):])
        b_prompt.append(jnp.concatenate([kb, vb, ki], axis=-1))

        hs = pre_mix(xs, ln_g[i, 0], ln_b[i, 0], ffn1_wi[i], ffn1_wo[i])
        qa, ka, va, qb, kb, vb, qi, ki, wi = project(hs, w_in[i], kidx_ln_g[i], kidx_ln_b[i])
        t = hs.shape[1]
        buf = cache_a_kv[i]
        w_buf = buf.shape[1]
        kv_all = jnp.concatenate([buf.astype(ka.dtype), jnp.stack([ka, va], axis=2)], axis=1)
        outs, lses = [], []
        for window, dil in DIL_PATTERNS:
            o, l = dilated_gather_step(qa, kv_all[:, :, 0], kv_all[:, :, 1], bias_a, window, dil, w_buf)
            outs.append(o)
            lses.append(l)
        o_a = combine_dilations(outs, lses)
        o_b = dsa_step(qb, kb, vb, qi, wi, ki, cache_b[i], page_table, bias_b)
        xs = post_mix(hs, o_a, o_b, w_out[i], ln_g[i, 1], ln_b[i, 1], ln_g[i, 2], ln_b[i, 2],
                      ffn2_wi[i], ffn2_wo[i], p_sample[i], ple_proj[i], ple_gate[i])
        a_sample.append(kv_all[:, w_buf + t - min(MAX_WINDOW, w_buf + t):])
        b_sample.append(jnp.concatenate([kb, vb, ki], axis=-1))
    return (xp, xs, jnp.stack(a_prompt), jnp.stack(a_sample), jnp.stack(b_prompt), jnp.stack(b_sample))


_drawn_inputs = setup_inputs


def setup_inputs(seed=0):
    import zlib

    import numpy as np

    out = dict(_drawn_inputs(seed))
    spreads = {}
    factors = {}
    for name, (base, spread) in spreads.items():
        noise = np.random.default_rng([zlib.crc32(name.encode()), seed]).standard_normal(out[name].shape)
        drawn = base * np.exp(spread * noise) if base else spread * noise
        out[name] = __import__('jax').numpy.asarray(drawn.astype(out[name].dtype))
    for name, factor in factors.items():
        out[name] = (out[name] * factor).astype(out[name].dtype)
    return out
```

```python
from contextlib import ExitStack
from math import log

import concourse.bass as bass
import numpy as np
from concourse import mybir

F32 = mybir.dt.float32
F32R = mybir.dt.float32r
I32 = mybir.dt.int32
ACT = mybir.ActivationFunctionType
ALU = mybir.AluOpType
AX = mybir.AxisListType

D_MODEL, SEQ, DEC_BATCH, DEC_SEQ, PAST, PAGE = 1024, 512, 8, 4, 2048, 128
HD, HEADS_A, HEADS_B, IDX_HEADS = 64, 12, 4, 8
D_FF, D_PLE, BUCKETS, REL_MAX = 2816, 256, 32, 2048
ROW_B = 3 * HD
WIDTH_A = HEADS_A * HD
ALPHA = 2.0 ** 0.25
LN_EPS = 1e-5
PATTERNS = ((128, 1), (512, 4), (2048, 16))
TOPK_PROMPT, TOPK_DEC = 128, 256
IDX_SCALE = HD ** -0.5 * IDX_HEADS ** -0.5
NEG = -1.0e30
TAKEN = -3.0e38
TAKEN_LIMIT = -2.0e38

NDEC = DEC_BATCH * DEC_SEQ
T = SEQ + NDEC
HALF = T // 2
HALVES = ((0, HALF), (HALF, T))
KD = D_MODEL // 128
KF = D_FF // 128
KP = D_PLE // 128
UNIT_TILES = KF // 2
QB_BLOCKS = SEQ // 128
PAGES = PAST // PAGE

C_QA, C_QB, C_QI, C_IDX, C_KV, C_KA, C_VA, N_PROJ = 0, 6, 8, 12, 13, 14, 20, 26

KEY_BLOCKS_A, BLK_NEW = 7, 23
STRIDED_BLOCKS = 3

STAGES = (("wi1", 44, 8), ("wo1", 16, 11), ("w_in", 26, 8), ("w_out", 8, 8),
          ("wi2", 44, 8), ("wo2", 16, 11), ("gate", 8, 10))
FIRST = {}
_u = 0
for _n, _c, _t in STAGES:
    FIRST[_n] = _u
    _u += _c
N_UNITS = _u
STAGE_TILES = {name: tiles for name, _, tiles in STAGES}
RAW_SLOTS, SPLIT_SLOTS = 4, 2
COPY_ROWS = 28
N_COPIES = (PAST - DEC_SEQ) // COPY_ROWS


def tiles_of(u):
    for name, count, tiles in STAGES:
        if u < FIRST[name] + count:
            return tiles
    raise ValueError(u)


def spread(ap, axis, n):
    a = ap.unsqueeze(axis)
    shape = list(a.shape)
    shape[axis] = n
    return a.broadcast_to(shape)


class Steps:

    def __init__(self, eng, sem):
        self.eng, self.sem, self.n = eng, sem, 0

    def done(self, instruction):
        instruction.then_inc(self.sem, 1)
        self.n += 1
        self.eng.wait_ge(self.sem, self.n)


def build_program(nc, x_t, p_t, cache_a, cache_b, page_table, ln, kidx_g, kidx_b, w, rel_bias,
                  rel_rows, consts, onehots, toeplitz, y_t, kv_a_t, a_sample, kv_b_t, ki_b):
    ctx = ExitStack()
    with ctx:
        SBUF_FROM, SBUF_TO = 16512, 229344
        place = {"at": SBUF_FROM}

        def sb(name, shape, dt=F32, at=None):
            size = int(np.prod(shape[1:])) * 4
            if at is None:
                at = place["at"]
                place["at"] += (size + 31) // 32 * 32
                assert place["at"] <= SBUF_TO, (name, place["at"])
            return nc.alloc_sbuf_tensor_at(name, list(shape), dt, offset=at)

        XH = sb("x_high", [128, KD, T], F32R)
        XL = sb("x_rest", [128, KD, T], F32R)
        RAW = sb("w_raw", [128, RAW_SLOTS, UNIT_TILES, 128])
        split_at = place["at"]
        WH = sb("w_high", [128, SPLIT_SLOTS, UNIT_TILES, 128], F32R)
        WL = sb("w_rest", [128, SPLIT_SLOTS, UNIT_TILES, 128], F32R)
        h_at = place["at"]
        HH = sb("hidden_high", [128, KF, T], F32R)
        HL = sb("hidden_rest", [128, KF, T], F32R)
        h_end = y_at = place["at"]
        Y = sb("y", [128, KD, T])
        CP = sb("consts_sb", [128, 444])
        BIAS_A = sb("bias_a_t", [128, KEY_BLOCKS_A, HEADS_A, 4])
        BIAS_B = sb("bias_b_t", [128, PAGES, HEADS_B, 4])
        BIAS_N = sb("bias_new_t", [32, 16, 4])
        LN = sb("ln_sb", [128, 6, KD])
        KIDX_GB = sb("kidx_gb", [128, 2, HD])
        ONES = sb("ones", [128, 128])
        PAGE_IDS = sb("page_ids", [1, DEC_BATCH * PAGES], I32)
        SMALL = sb("small", [128, 64])
        e_at = place["at"]

        IDENT = CP[:, 0:128]
        LNC_A = CP[:, 128:156].rearrange("p (k t) -> p k t", t=4)
        MASK_NEW_A = CP[0:32, 156:188].rearrange("p (b t) -> p b t", t=4)
        MASK_NEW_IX = CP[0:32, 188:220]
        SEL_HEAD = CP[64:72, 220:348]
        WMASK = CP[:, 348:412].rearrange("p (k c) -> p k c", k=2)

        SG = sb("silu_gate", [128, 2, T], at=y_at)
        HF = sb("hidden", [128, 2, T], at=y_at + 2 * T * 4)
        P_RAW = sb("p_raw", [128, KP, T], at=y_at + 4 * T * 4)
        SUM = sb("sum_acc", [128, T], at=e_at)
        PH = sb("p_high", [128, KP, T], F32R, at=e_at + T * 4)
        PL = sb("p_rest", [128, KP, T], F32R, at=e_at + 3 * T * 4)
        OH = sb("onehots_sb", [128, 24, 128], at=h_at)
        TP = sb("toeplitz_sb", [34, 640], at=h_at + 12288)
        RELC = sb("rel_sb", [34, 16], at=h_at + 16384)
        RELREP = sb("rel_rep", [128, 16], at=h_at + 16512)
        RELT = sb("rel_t", [128, 16, 4], at=h_at + 16640)
        REV = sb("rev_sb", [16, 640], at=h_at + 17408)
        ln_at = h_at + 70016
        MEAN = sb("mean", [128, T], at=ln_at)
        RSTD = sb("rstd", [128, T], at=ln_at + T * 4)
        SQ = sb("squares", [128, 2, T], at=ln_at + 2 * T * 4)
        XN = sb("x_new", [128, 2, T], at=ln_at + 4 * T * 4)
        PROJ = sb("proj", [128, N_PROJ, T], at=h_at)
        vp_at = h_at + N_PROJ * T * 4
        VP = sb("v_prompt", [128, QB_BLOCKS, WIDTH_A], at=vp_at)
        wk_at = vp_at + QB_BLOCKS * WIDTH_A * 4
        TOE = sb("bias_toeplitz", [128, 2, SEQ], at=wk_at)
        LP = sb("logits", [128, 3, SEQ], at=wk_at + 4096)
        PTS = sb("probs_t", [128, 2, SEQ], at=wk_at + 10240)
        MSK = sb("topk_work", [128, 3, SEQ], at=wk_at + 14336)
        TM = sb("bias_masked", [128, 2, SEQ], at=wk_at + 20480)
        KIT = sb("kidx_t", [128, T], at=wk_at + 24576)
        assert wk_at + 24576 + T * 4 <= h_end
        KI0 = sb("kidx_wi_tok", [128, 5, 72], at=wk_at + 20480)
        KIN = sb("kidx_norm", [128, 5, 128], at=wk_at + 20480 + 1440)
        RL = sb("idx_relu", [128, 2, SEQ], at=wk_at + 10240)
        KIPT = sb("kidx_pages_t", [128, 2, 4, 128], at=wk_at + 4096)
        RLD = sb("idx_relu_dec", [128, 2, 2, 128], at=wk_at + 8192)
        KNEW = sb("k_a_new_tok", [NDEC, WIDTH_A], at=y_at)
        QIB = sb("q_idx_blocks", [128, 4, 64], at=y_at + 3072)
        WB = sb("w_idx_blocks", [128, 2, 32], at=y_at + 4096)
        OT = sb("attn_out_t", [128, KD, T], at=y_at)
        OH_ = sb("attn_out_high", [128, KD, T], F32R, at=h_at)
        OL_ = sb("attn_out_rest", [128, KD, T], F32R, at=h_at + KD * T * 4)
        SC = sb("idx_scores", [NDEC, PAST + NDEC], at=e_at)
        KB2 = sb("k_b_high_half", [128, T], at=e_at + 8320)
        VBT = sb("kv_b_tok", [128, QB_BLOCKS, 128], at=e_at + 10496)
        VBN = sb("kv_b_new_tok", [NDEC, 128], at=e_at + 12544)
        assert e_at + 13056 <= SBUF_TO, e_at + 13056 - SBUF_TO
        AR = sb("cache_a_ring", [128, 3, WIDTH_A], at=split_at)
        PG = sb("cache_b_ring", [128, 4, DEC_BATCH, HD], at=split_at + 9216)
        QBLKA = sb("q_a_blocks", [128, 6, DEC_BATCH, 8], at=split_at + 17408)
        VNEW = sb("v_a_new_tok", [NDEC, WIDTH_A], at=split_at + 18944)
        QBLKB = sb("q_b_blocks", [128, 4, 32], at=split_at + 22016)
        assert split_at + 22528 <= h_at
        KTA = sb("k_a_t", [128, 2, WIDTH_A], at=h_at + C_QI * T * 4)
        KTB = sb("k_b_t", [128, 2, 512], at=h_at + C_QI * T * 4)
        STA = sb("logits_a_t", [128, 8, 384], at=h_at + C_VA * T * 4)
        STB = sb("logits_b_t", [128, 17, 128], at=vp_at)
        SELT = sb("taken_t", [128, 17, 32], at=vp_at + 8704)
        MX = sb("dec_max", [128, 384], at=wk_at + 4096)
        DIAG = sb("dec_diag", [128, 3, 128], at=wk_at + 4096 + 1536)
        RD = sb("dec_rden", [128, 384], at=wk_at + 4096 + 4608)
        NMA = sb("bias_new_a", [32, DEC_BATCH, HEADS_A, 4], at=wk_at)

        BANK = [ctx.enter_context(nc.psum_tensor(f"bank{i}", [128, 512], F32)) for i in range(8)]
        REV_DRAM = nc.dram_tensor("rev_bias", [16, 128, 640], F32, kind="Internal").ap()

        names = """setup_in ids_in x_in ln_in ones_done relt_done tables_ps rev_in rev_out
            xh_ready x_ready hi_ready lo_ready unit_used
            silu_done h_done hh_done hl_done y_part y_full sum_done
            mean_ps mean_sb centred squared sq_used var_sb std_sb zed xh_ln
            p_in p_ready gate_sig y_final
            proj_a proj_d kiw_ps ki_var ki_std kin_done kit_ps kit_sb tr_ps tr_a tr_d qblocks_done
            ix_ps ix_relu ix_acc wsel_ps wsel_done kp_t kp_sb kp_sc kp_relu kp_sum kp_row ix_causal
            topk_prompt_done sc_ps logits_done exp_done probs_done pt_ps pt_sb pv_done o_sb tm_done
            new_rows_out proj_out copy_done
            ka_t ka_sb_a ka_sb_d ka_sc ka_logits
            mxa_done mxa_t diaga_done maxa_all suba_done expa_done dena_ps va_used va_all oa_done
            topk_dec_done taken_t taken_sb kb_t kb_sb kb_sc kb_logits
            mxb_done mxb_t diagb_done maxb_all subb_done expb_done denb_ps vb_used vb_all ob_done
            oh_ready o_ready dve_step""".split()
        S = {n: ctx.enter_context(nc.semaphore(n)) for n in names}
        raw_loaded = [ctx.enter_context(nc.semaphore(f"raw_loaded{i}")) for i in range(RAW_SLOTS)]
        toe_in = [ctx.enter_context(nc.semaphore(f"toe_in{i}")) for i in range(2)]
        ar_in = [ctx.enter_context(nc.semaphore(f"ar_in{i}")) for i in range(3)]
        pg_in = [ctx.enter_context(nc.semaphore(f"pg_in{i}")) for i in range(4)]
        y_out = [ctx.enter_context(nc.semaphore(f"y_out{i}")) for i in range(2)]

        block = ctx.enter_context(nc.Block())
        UP_ITERS = KF // 2
        N_STEPS = 4 * (HEADS_A + HEADS_B)

        def raw_slot(u0, j):
            return (u0 + j) % RAW_SLOTS

        def half(t, k, n):
            a, b = HALVES[n]
            return t[:, k, a:b]

        def tr_copies(g):
            bank = BANK[2 + g % 6]
            if g < 6:
                return [(VP[:, :, :].rearrange("p a n -> p (a n)")[:, 512 * g:512 * g + 512], bank[:, :])]
            if g == 6:
                return [(VBT[:, :, :].rearrange("p a n -> p (a n)"), bank[:, :])]
            if g == 7:
                return [(KNEW[:, 0:512], bank[0:32, :])]
            if g == 8:
                return [(KNEW[:, 512:768], bank[0:32, 0:256]), (VNEW[:, 0:256], bank[0:32, 256:512])]
            if g == 9:
                return [(VNEW[:, 256:768], bank[0:32, :])]
            return [(VBN[:, 0:HD], bank[0:32, HD:128]), (VBN[:, HD:128], bank[0:32, HD:128])]

        @block.sync
        def _(sp):
            def cache_copy(q):
                sp.dma_start(
                    a_sample[:, bass.ds(q * COPY_ROWS, COPY_ROWS), :].rearrange("b r n -> r b n"),
                    cache_a[:, bass.ds(q * COPY_ROWS + DEC_SEQ, COPY_ROWS), :].rearrange("b r n -> r b n"),
                ).then_inc(S["copy_done"], 16)

            def load_unit(name, i, j, free=True):
                u0, n_tiles = FIRST[name], STAGE_TILES[name]
                slot = raw_slot(u0, j)
                if free:
                    sp.wait_ge(S["lo_ready"], u0 + i * 4 + j - 3)
                sp.dma_start(RAW[:, slot, 0:n_tiles, :],
                             w[name][bass.ds(i * 4 + j, 1)].rearrange("o p t n -> (o p) t n")
                             ).then_inc(raw_loaded[slot], 16)

            def load_stage(name, first, iters, copies=0, copy0=0):
                with sp.Fori(first, iters) as i:
                    for j in range(4):
                        load_unit(name, i, j)
                        if j < copies:
                            cache_copy(i * copies + (j + copy0))

            sp.dma_start(RELC[0:32, :], rel_bias).then_inc(S["setup_in"], 16)
            sp.dma_start(RELC[32:34, :], rel_rows).then_inc(S["setup_in"], 16)
            for t in range(4):
                sp.dma_start(RELREP[32 * t:32 * t + 32, :], rel_bias).then_inc(S["setup_in"], 16)
            sp.dma_start(CP[:], consts).then_inc(S["setup_in"], 16)
            sp.dma_start(TP[:], toeplitz).then_inc(S["setup_in"], 16)
            sp.dma_start(OH[:], onehots).then_inc(S["setup_in"], 16)
            for j in range(2):
                load_unit("wi1", 0, j, free=False)
            sp.dma_start(Y[:], x_t).then_inc(S["x_in"], 16)
            for j in range(2, 4):
                load_unit("wi1", 0, j, free=False)
            sp.dma_start(LN[:], ln).then_inc(S["ln_in"], 16)
            sp.dma_start(KIDX_GB[:, 0, :], kidx_g.partition_broadcast(128)).then_inc(S["ln_in"], 16)
            sp.dma_start(KIDX_GB[:, 1, :], kidx_b.partition_broadcast(128)).then_inc(S["ln_in"], 16)
            sp.dma_start(PAGE_IDS[:], page_table.rearrange("b g -> (b g)").unsqueeze(0)).then_inc(S["ids_in"], 16)
            sp.wait_ge(S["rev_in"], 1)
            sp.dma_start(REV_DRAM, spread(REV[:], 1, 128)).then_inc(S["rev_out"], 16)
            load_stage("wi1", 1, UP_ITERS, copies=2, copy0=-2)
            load_stage("wo1", 0, 4, copies=2, copy0=20)
            load_stage("w_in", 0, 6, copies=2, copy0=28)
            for j in range(2):
                load_unit("w_in", 6, j)
            for j in range(4):
                load_unit("w_out", 0, j)

            sp.wait_ge(S["proj_a"], N_PROJ)
            sp.wait_ge(S["proj_d"], N_PROJ)
            sp.dma_start(kv_a_t.rearrange("c p n -> p c n"), PROJ[:, C_KA:C_KA + 12, 0:SEQ]).then_inc(S["proj_out"], 16)
            sp.dma_start(kv_b_t, PROJ[:, C_KV, :]).then_inc(S["proj_out"], 16)

            def load_pages(which, g, n):
                if n >= 4:
                    sem, base = ((S["kp_t"], 0), (S["kb_t"], PAGES), (S["vb_used"], 2 * PAGES))[(n - 4) // PAGES]
                    sp.wait_ge(sem, n - 3 - base)
                for b in range(DEC_BATCH):
                    page = sp.value_load(PAGE_IDS[0:1, b * PAGES + g:b * PAGES + g + 1],
                                         min_val=0, max_val=cache_b.shape[0] - 1)
                    sp.dma_start(PG[:, n % 4, b, :],
                                 cache_b[bass.ds(page, 1), :, which * HD:(which + 1) * HD].rearrange("o p n -> (o p) n")
                                 ).then_inc(pg_in[n % 4], 16)

            sp.wait_ge(S["ids_in"], 16)
            for g in range(4):
                load_pages(2, g, g)
            sp.wait_ge(S["tr_a"], 6)
            sp.wait_ge(S["tr_d"], 5)
            for b in range(DEC_BATCH):
                for kv, t in ((0, KNEW), (1, VNEW)):
                    sp.dma_start(a_sample[b, PAST - DEC_SEQ:PAST, kv * WIDTH_A:(kv + 1) * WIDTH_A],
                                 t[4 * b:4 * b + 4, :]).then_inc(S["new_rows_out"], 16)
            sp.wait_ge(S["kin_done"], 1)
            sp.dma_start(ki_b, KIN[:, :, 0:HD]).then_inc(S["proj_out"], 16)
            for g in range(4, PAGES):
                load_pages(2, g, g)
            for q in range(40, 52):
                cache_copy(q)

            def load_rows(n, kv, b, k):
                if n >= 3:
                    if n - 3 < 56:
                        sp.wait_ge(S["ka_t"], n - 2)
                    else:
                        sp.wait_ge(S["va_used"], n - 2 - 56)
                cols = slice(kv * WIDTH_A, (kv + 1) * WIDTH_A)
                if k < STRIDED_BLOCKS:
                    src = cache_a[b, 512 * k:512 * k + 512, cols].rearrange("(j r) n -> j r n", r=16)[:, 0:4, :]
                else:
                    r0 = PAST - 512 + 128 * (k - STRIDED_BLOCKS)
                    src = cache_a[b, r0:r0 + 128, cols]
                sp.dma_start(AR[:, n % 3, :], src).then_inc(ar_in[n % 3], 16)

            for n in range(56):
                load_rows(n, 0, n % 8, n // 8)
            for n in range(56):
                load_rows(56 + n, 1, n // 7, n % 7)
            for g in range(PAGES):
                load_pages(0, g, PAGES + g)
            for g in range(PAGES):
                load_pages(1, g, 2 * PAGES + g)

            for j in range(4):
                load_unit("w_out", 1, j)
            load_stage("wi2", 0, UP_ITERS, copies=1, copy0=52)
            sp.dma_start(P_RAW[:], p_t).then_inc(S["p_in"], 16)
            load_stage("wo2", 0, 4, copies=2, copy0=63)
            for q in range(71, N_COPIES):
                cache_copy(q)
            load_stage("gate", 0, 2)
            for m in range(KD):
                sp.wait_ge(S["y_final"], m + 1)
                sp.dma_start(y_t[m], HF[:, m % 2, :]).then_inc(y_out[m % 2], 16)
            for s in y_out:
                sp.wait_ge(s, 16 * KD // 2)
            sp.wait_ge(S["proj_out"], 48)
            sp.wait_ge(S["new_rows_out"], 16 * 2 * DEC_BATCH)
            sp.wait_ge(S["copy_done"], 16 * N_COPIES)

        @block.gpsimd
        def _(pool):
            def rest(name, i, j):
                u0, tiles = FIRST[name], STAGE_TILES[name]
                slot, s = raw_slot(u0, j), (u0 + j) % 2
                pool.wait_ge(S["hi_ready"], u0 + i * 4 + j + 1)
                nc.gpsimd.tensor_tensor(WL[:, s, 0:tiles, :], RAW[:, slot, 0:tiles, :],
                                        WH[:, s, 0:tiles, :].bitcast(F32), ALU.subtract
                                        ).then_inc(S["lo_ready"], 1)

            def rests(name, first, iters):
                with pool.Fori(first, iters) as i:
                    for j in range(4):
                        rest(name, i, j)

            def x_rest(k, new):
                nc.gpsimd.tensor_tensor(XL[:, k, :], new, XH[:, k, :].bitcast(F32), ALU.subtract
                                        ).then_inc(S["x_ready"], 1)

            def ln_rest(which, nxt):
                for j in range(2):
                    rest(nxt, 0, j)
                for m in range(KD):
                    pool.wait_ge(S["xh_ln"], KD * which + m + 1)
                    x_rest(m, XN[:, m % 2, :])
                for j in range(2, 4):
                    rest(nxt, 0, j)

            nc.gpsimd.memset(ONES[:], 1.0 / D_MODEL).then_inc(S["ones_done"], 1)
            for k in range(KD):
                pool.wait_ge(S["xh_ready"], k + 1)
                x_rest(k, Y[:, k, :])
            rests("wi1", 0, UP_ITERS)
            rests("wo1", 0, 4)
            ln_rest(0, "w_in")
            rests("w_in", 1, 6)
            for j in range(2):
                rest("w_in", 6, j)

            for i in range(1, QB_BLOCKS):
                pool.wait_ge(S["ix_acc"], IDX_HEADS * i)
                d = MSK[:, i - 1, 128 * i:128 * i + 128]
                nc.gpsimd.affine_select(out=d, in_=d, compare_op=ALU.is_ge, fill=NEG, base=0,
                                        pattern=[[-1, 128]], channel_multiplier=1
                                        ).then_inc(S["ix_causal"], 1)
            pool.wait_ge(S["rev_out"], 16)
            for h in range(HEADS_A + HEADS_B):
                if h >= 2:
                    pool.wait_ge(S["logits_done"], 4 * (h - 1))
                row = bass.AP(REV_DRAM.tensor, 640 * 128 * h + 127, [[639, 128], [1, SEQ]])
                pool.dma_start(TOE[:, h % 2, :], row).then_inc(toe_in[h % 2], 16)
                if h >= HEADS_A:
                    if h == HEADS_A:
                        pool.wait_ge(S["topk_prompt_done"], 1)
                        pool.wait_ge(S["proj_out"], 48)
                    pool.wait_ge(toe_in[h % 2], 16 * (h // 2 + 1))
                    for i in range(1, QB_BLOCKS):
                        n = 3 * (h - HEADS_A) + i - 1
                        if n >= 2:
                            hh, ii = HEADS_A + (n - 2) // 3, (n - 2) % 3 + 1
                            pool.wait_ge(S["logits_done"], 4 * hh + ii + 1)
                        nk = 128 * (i + 1)
                        nc.gpsimd.tensor_tensor(TM[:, n % 2, 0:nk], TOE[:, h % 2, SEQ - nk:SEQ],
                                                MSK[:, i - 1, 0:nk], ALU.add).then_inc(S["tm_done"], 1)

            for c in range(KD):
                pool.wait_ge(S["oh_ready"], c + 1)
                nc.gpsimd.tensor_tensor(OL_[:, c, :], OT[:, c, :], OH_[:, c, :].bitcast(F32), ALU.subtract
                                        ).then_inc(S["o_ready"], 1)
            rests("w_out", 0, 2)
            ln_rest(1, "wi2")
            rests("wi2", 1, UP_ITERS)
            rests("wo2", 0, 4)
            ln_rest(2, "gate")
            rests("gate", 1, 2)

        @block.scalar
        def _(act):
            def high(u0, i, j, tiles):
                slot, s = raw_slot(u0, j), (u0 + j) % 2
                act.wait_ge(raw_loaded[slot], (i + (u0 + j) // 4) * 16 + 16)
                if not (isinstance(i, int) and u0 + 4 * i + j < 2):
                    act.wait_ge(S["unit_used"], u0 + i * 4 + j - 1)
                nc.scalar.activation(WH[:, s, 0:tiles, :], RAW[:, slot, 0:tiles, :], ACT.Copy
                                     ).then_inc(S["hi_ready"], 1)

            def high_of(u):
                high(u % 4, u // 4, 0, tiles_of(u))

            def up_stage(which):
                name = ("wi1", "wi2")[which]
                u0 = FIRST[name]

                def pair(i, split):
                    for s in range(2):
                        for j in (2 * s + 2, 2 * s + 3):
                            split(i, j)
                        if not (isinstance(i, int) and i == 0 and which == 0):
                            act.wait_ge(S["h_done"], 22 * which + i * 2 + s - 1)
                        act.wait_ge(S["unit_used"], u0 + i * 4 + 2 * s + 1)
                        for n in range(2):
                            last = nc.scalar.activation(half(SG, s, n), BANK[4 * s + n][:, 0:HALF], ACT.Silu)
                        last.then_inc(S["silu_done"], 1)

                pair(0, lambda i, j: high(u0, i, j, 8))
                with act.Fori(1, UP_ITERS - 1) as i:
                    pair(i, lambda i, j: high(u0, i, j, 8))
                pair(UP_ITERS - 1, lambda i, j: high_of(u0 + 4 * i + j))

            def layer_norm(which):
                act.wait_ge(S["mean_ps"], which + 1)
                for n, (a, b) in enumerate(HALVES):
                    last = nc.scalar.activation(MEAN[:, a:b], BANK[4 + n][:, 0:HALF], ACT.Copy)
                last.then_inc(S["mean_sb"], 1)
                for m in range(KD):
                    act.wait_ge(S["centred"], KD * which + m + 1)
                    if m >= 2 or which:
                        act.wait_ge(S["sq_used"], KD * which + m - 1)
                    nc.scalar.activation(SQ[:, m % 2, :], Y[:, m, :], ACT.Square).then_inc(S["squared"], 1)
                act.wait_ge(S["var_sb"], which + 1)
                nc.scalar.activation(RSTD[:], RSTD[:], ACT.Sqrt).then_inc(S["std_sb"], 1)
                if which == 0:
                    act.wait_ge(S["ln_in"], 48)
                for m in range(KD):
                    act.wait_ge(S["zed"], KD * which + m + 1)
                    if m >= 2 or which:
                        act.wait_ge(S["x_ready"], KD * (which + 1) + m - 1)
                    g, b = LN[:, 2 * which, m:m + 1], LN[:, 2 * which + 1, m:m + 1]
                    nc.scalar.activation(XN[:, m % 2, :], Y[:, m, :], ACT.Identity, bias=b, scale=g)
                    nc.scalar.activation(XH[:, m, :], Y[:, m, :], ACT.Identity, bias=b, scale=g
                                         ).then_inc(S["xh_ln"], 1)

            high_of(0)
            high_of(1)
            up_stage(0)
            for m in range(KD):
                high_of(FIRST["wo1"] + 2 * m + 2)
                high_of(FIRST["wo1"] + 2 * m + 3)
            layer_norm(0)

            def project(i, j, scale, split=True):
                u0 = FIRST["w_in"]
                if split:
                    high(u0, i, j + 2, 8)
                act.wait_ge(S["unit_used"], u0 + i * 4 + j + 1)
                c = i * 4 + j
                nc.scalar.activation(PROJ[:, bass.ds(c, 1), 0:HALF].rearrange("p o n -> p (o n)"),
                                     BANK[2 * j][:, 0:HALF], ACT.Copy, scale=scale
                                     ).then_inc(S["proj_a"], 1)

            with act.Fori(0, C_QI // 4) as i:
                for j in range(4):
                    project(i, j, HD ** -0.5)
            with act.Fori(C_QI // 4, 6) as i:
                for j in range(4):
                    project(i, j, 1.0)
            for j in range(2):
                project(6, j, 1.0, split=False)

            act.wait_ge(S["ki_var"], 1)
            nc.scalar.activation(SMALL[:, 10:15], SMALL[:, 10:15], ACT.Sqrt).then_inc(S["ki_std"], 1)
            for g in range(0, 11, 2):
                act.wait_ge(S["tr_ps"], g + 1)
                for dst, src in tr_copies(g):
                    last = nc.scalar.activation(dst, src, ACT.Copy)
                last.then_inc(S["tr_a"], 1)
            act.wait_ge(S["kit_ps"], 1)
            nc.scalar.activation(KIT[:, 0:SEQ], BANK[1][:, 0:SEQ], ACT.Copy)
            nc.scalar.activation(KIT[:, SEQ:T], BANK[0][:, 480:512], ACT.Copy).then_inc(S["kit_sb"], 1)
            n = 0
            for i in range(1, QB_BLOCKS):
                for h in range(IDX_HEADS):
                    act.wait_ge(S["ix_ps"], n + 1)
                    if n >= 2:
                        act.wait_ge(S["ix_acc"], n - 1)
                    nk = 128 * (i + 1)
                    nc.scalar.activation(RL[:, n % 2, 0:nk], BANK[n % 2][:, 0:nk], ACT.Relu
                                         ).then_inc(S["ix_relu"], 1)
                    n += 1

            def relu_dec(g):
                act.wait_ge(S["kp_sc"], g + 1)
                if g >= 2:
                    act.wait_ge(S["kp_sum"], g - 1)
                nk = 128 if g < PAGES else NDEC
                src = BANK[4 + g % 2][:, 0:256].rearrange("p (a k) -> p a k", a=2)[:, :, 0:nk]
                nc.scalar.activation(RLD[:, g % 2, :, 0:nk], src, ACT.Relu).then_inc(S["kp_relu"], 1)

            for g in range(PAGES + 1):
                if g < PAGES:
                    act.wait_ge(S["kp_t"], g + 1)
                    if g >= 2:
                        act.wait_ge(S["kp_sc"], g - 1)
                    nc.scalar.activation(KIPT[:, g % 2, :, :].rearrange("p a k -> p (a k)"), BANK[2 + g % 2][:, :],
                                         ACT.Copy).then_inc(S["kp_sb"], 1)
                if g >= 1:
                    relu_dec(g - 1)
            relu_dec(PAGES)

            for n in range(N_STEPS + 1):
                if n < N_STEPS:
                    nk = 128 * (n % 4 + 1)
                    act.wait_ge(S["logits_done"], n + 1)
                    l = LP[:, n % 3, 0:nk]
                    nc.scalar.activation(l, l, ACT.Exp, bias=SMALL[:, 32 + n % 4:33 + n % 4], scale=-1.0,
                                         accum_out=SMALL[:, 36 + n % 4:37 + n % 4]).then_inc(S["exp_done"], 1)
                if n >= 1:
                    k = n - 1
                    nk = 128 * (k % 4 + 1)
                    act.wait_ge(S["pt_ps"], k + 1)
                    if k >= 2:
                        act.wait_ge(S["pv_done"], k - 1)
                    nc.scalar.activation(PTS[:, k % 2, 0:nk], BANK[2 + k % 2][:, 0:nk], ACT.Copy
                                         ).then_inc(S["pt_sb"], 1)

            for n in range(56):
                act.wait_ge(S["ka_t"], n + 1)
                if n >= 2:
                    act.wait_ge(S["ka_sc"], n - 1)
                nc.scalar.activation(KTA[:, n % 2, 0:512], BANK[2 * (n % 2)][:, :], ACT.Copy
                                     ).then_inc(S["ka_sb_a"], 1)
            for k in range(8):
                act.wait_ge(S["suba_done"], k + 1)
                nc.scalar.activation(STA[:, k, :], STA[:, k, :], ACT.Exp).then_inc(S["expa_done"], 1)
            for g in range(PAGES):
                act.wait_ge(S["kb_t"], g + 1)
                if g >= 2:
                    act.wait_ge(S["kb_sc"], g - 1)
                nc.scalar.activation(KTB[:, g % 2, :], BANK[g % 2][:, :], ACT.Copy).then_inc(S["kb_sb"], 1)
            act.wait_ge(S["subb_done"], 1)
            nc.scalar.activation(STB[:], STB[:], ACT.Exp).then_inc(S["expb_done"], 1)

            act.wait_ge(S["vb_all"], 1)
            for j in range(2):
                high_of(FIRST["w_out"] + j)
            for m in range(KD):
                high_of(FIRST["w_out"] + m + 2)
            layer_norm(1)
            up_stage(1)
            for m in range(KD):
                high_of(FIRST["wo2"] + 2 * m + 2)
                high_of(FIRST["wo2"] + 2 * m + 3)
            layer_norm(2)
            for m in range(KD):
                if m < KD - 2:
                    high_of(FIRST["gate"] + m + 2)
                s = m % 2
                act.wait_ge(S["unit_used"], FIRST["gate"] + m + 1)
                if m >= 2:
                    act.wait_ge(S["y_final"], m - 1)
                for n in range(2):
                    last = nc.scalar.activation(half(SG, s, n), BANK[4 * s + n][:, 0:HALF], ACT.Sigmoid)
                last.then_inc(S["gate_sig"], 1)

        @block.vector
        def _(dve):
            own = Steps(dve, S["dve_step"])
            v = nc.vector

            own.done(v.memset(RELT[:], 0.0))
            dve.wait_ge(S["setup_in"], 16 * 9)
            for t in range(4):
                last = v.tensor_copy(RELT[32 * t:32 * t + 32, :, t], RELREP[32 * t:32 * t + 32, :])
            last.then_inc(S["relt_done"], 1)
            dve.wait_ge(S["x_in"], 16)
            for k in range(KD):
                v.tensor_copy(XH[:, k, :], Y[:, k, :]).then_inc(S["xh_ready"], 1)
            dve.wait_ge(S["tables_ps"], 1)
            v.tensor_copy(REV[:, 0:512], BANK[3][0:16, :])
            v.tensor_copy(REV[:, 512:640], BANK[4][0:16, 0:128]).then_inc(S["rev_in"], 1)
            v.tensor_tensor(BIAS_A[:], BANK[0][:, 0:336].rearrange("p (k h t) -> p k h t", k=7, t=4),
                            spread(LNC_A, 2, HEADS_A), ALU.add)
            v.tensor_copy(BIAS_B[:].rearrange("p g h t -> p (g h t)"), BANK[1][:, 0:256])
            own.done(v.tensor_copy(BIAS_N[:].rearrange("p h t -> p (h t)"), BANK[2][0:32, 0:64]))
            dve.wait_ge(S["rev_out"], 16)

            def up_stage(which):
                u0 = FIRST[("wi1", "wi2")[which]]
                with dve.Fori(0, UP_ITERS) as i:
                    for s in range(2):
                        done = i * 2 + (22 * which + s + 1)
                        c = i * 2 + s
                        dve.wait_ge(S["silu_done"], done)
                        dve.wait_ge(S["unit_used"], u0 + i * 4 + 2 * s + 2)
                        for n in range(2):
                            last = v.scalar_tensor_tensor(half(HF, s, n), half(SG, s, n), 0.5,
                                                          BANK[4 * s + 2 + n][:, 0:HALF], ALU.mult, ALU.mult)
                        last.then_inc(S["h_done"], 1)
                        dve.wait_ge(S["h_done"], done)
                        v.tensor_copy(HH[:, bass.ds(c, 1), :], HF[:, s:s + 1, :]).then_inc(S["hh_done"], 1)
                        dve.wait_ge(S["hh_done"], done)
                        v.tensor_tensor(HL[:, bass.ds(c, 1), :], HF[:, s:s + 1, :],
                                        HH[:, bass.ds(c, 1), :].bitcast(F32), ALU.subtract
                                        ).then_inc(S["hl_done"], 1)

            def down_stage(which):
                name = ("wo1", "w_out", "wo2")[which]
                u0, per = FIRST[name], (2, 1, 2)[which]
                own.done(v.memset(SUM[:], 0.0))
                with dve.Fori(0, KD // 2) as i:
                    for s in range(2):
                        done = i * 2 + (KD * which + s + 1)
                        m = i * 2 + s
                        dve.wait_ge(S["unit_used"], u0 + i * (2 * per) + per * (s + 1))
                        for n, (a, b) in enumerate(HALVES):
                            last = v.scalar_tensor_tensor(
                                Y[:, bass.ds(m, 1), a:b], XH[:, bass.ds(m, 1), a:b].bitcast(F32), ALPHA,
                                BANK[2 * s + n][:, 0:HALF].unsqueeze(1), ALU.mult, ALU.add)
                        last.then_inc(S["y_part"], 1)
                        dve.wait_ge(S["y_part"], done)
                        v.scalar_tensor_tensor(Y[:, bass.ds(m, 1), :], XL[:, bass.ds(m, 1), :].bitcast(F32), ALPHA,
                                               Y[:, bass.ds(m, 1), :], ALU.mult, ALU.add).then_inc(S["y_full"], 1)
                        dve.wait_ge(S["y_full"], done)
                        v.tensor_tensor(SUM[:].unsqueeze(1), SUM[:].unsqueeze(1), Y[:, bass.ds(m, 1), :], ALU.add
                                        ).then_inc(S["sum_done"], 1)
                        dve.wait_ge(S["sum_done"], done)

            def layer_norm(which):
                dve.wait_ge(S["mean_sb"], which + 1)
                for m in range(KD):
                    v.tensor_tensor(Y[:, m, :], Y[:, m, :], MEAN[:], ALU.subtract).then_inc(S["centred"], 1)
                dve.wait_ge(S["sq_used"], KD * (which + 1))
                for n, (a, b) in enumerate(HALVES):
                    last = v.tensor_scalar_add(RSTD[:, a:b], BANK[6 + n][:, 0:HALF], LN_EPS)
                last.then_inc(S["var_sb"], 1)
                dve.wait_ge(S["std_sb"], which + 1)
                own.done(v.reciprocal(RSTD[:], RSTD[:]))
                for m in range(KD):
                    v.tensor_tensor(Y[:, m, :], Y[:, m, :], RSTD[:], ALU.mult).then_inc(S["zed"], 1)

            up_stage(0)
            down_stage(0)
            layer_norm(0)

            def project(i, j, scale):
                dve.wait_ge(S["unit_used"], FIRST["w_in"] + i * 4 + j + 1)
                c = i * 4 + j
                v.tensor_scalar_mul(PROJ[:, bass.ds(c, 1), HALF:T], BANK[2 * j + 1][:, 0:HALF].unsqueeze(1), scale
                                    ).then_inc(S["proj_d"], 1)

            with dve.Fori(0, C_QI // 4) as i:
                for j in range(4):
                    project(i, j, HD ** -0.5)
            with dve.Fori(C_QI // 4, 6) as i:
                for j in range(4):
                    project(i, j, 1.0)
            for j in range(2):
                project(6, j, 1.0)

            own.done(v.memset(KI0[:], 0.0))
            dve.wait_ge(S["kiw_ps"], 1)
            v.tensor_copy(KI0[:, 0:4, :].rearrange("p a n -> p (a n)"), BANK[0][:, 0:288])
            own.done(v.tensor_copy(KI0[0:32, 4, :], BANK[0][0:32, 288:360]))
            for k in range(5):
                own.done(v.bn_stats(SMALL[:, 48:54], KI0[:, k, 0:HD]))
                own.done(v.bn_aggr(SMALL[:, 2 * k:2 * k + 2], SMALL[:, 48:54]))
            v.tensor_scalar_add(SMALL[:, 10:15], SMALL[:, 1:10:2], LN_EPS).then_inc(S["ki_var"], 1)
            dve.wait_ge(S["ki_std"], 1)
            own.done(v.reciprocal(SMALL[:, 10:15], SMALL[:, 10:15]))
            for k in range(5):
                own.done(v.tensor_scalar(KIN[:, k, 0:HD], KI0[:, k, 0:HD], SMALL[:, 2 * k:2 * k + 1],
                                         SMALL[:, 10 + k:11 + k], ALU.subtract, ALU.mult))
            own.done(v.tensor_tensor(KIN[:, :, 0:HD], KIN[:, :, 0:HD], spread(KIDX_GB[:, 0, :], 1, 5), ALU.mult))
            own.done(v.tensor_tensor(KIN[:, :, 0:HD], KIN[:, :, 0:HD], spread(KIDX_GB[:, 1, :], 1, 5), ALU.add))
            v.tensor_copy(KIN[:, :, HD:128], KIN[:, :, 0:HD]).then_inc(S["kin_done"], 1)
            own.done(v.tensor_scalar_mul(KI0[:, :, HD:HD + 8], KI0[:, :, HD:HD + 8], IDX_SCALE))

            for t in (QBLKA, QBLKB, QIB):
                last = v.memset(t[:], 0.0)
            own.done(last)
            for h2 in range(2):
                lo = slice(64 * h2, 64 * h2 + 64)
                v.tensor_copy(QBLKA[lo, :, :, 4 * h2:4 * h2 + 4],
                              PROJ[lo, C_QA:C_QA + 6, SEQ:T].rearrange("p c (b t) -> p c b t", t=4))
                for b2 in range(2):
                    up = slice(64 * b2, 64 * b2 + 64)
                    qi = PROJ[lo, C_QI:C_QI + 4, SEQ:T].rearrange("p c (a b t) -> p a c b t", b=2, t=4)[:, :, :, b2, :]
                    v.tensor_copy(QIB[up, :, :].rearrange("p a (b c h t) -> p a b c h t", b=2, c=4, h=2)
                                  [:, :, b2, :, h2, :], qi)
                    qb = PROJ[lo, C_QB:C_QB + 2, SEQ:T].rearrange("p c (a b t) -> p a c b t", b=2, t=4)[:, :, :, b2, :]
                    v.tensor_copy(QBLKB[up, :, :].rearrange("p a (b c h t) -> p a b c h t", b=2, c=2, h=2)
                                  [:, :, b2, :, h2, :], qb)
            v.tensor_copy(KB2[0:64, SEQ:T], PROJ[0:64, C_KV, SEQ:T])
            v.tensor_copy(KB2[64:128, :], PROJ[0:64, C_KV, :]).then_inc(S["qblocks_done"], 1)
            for g in range(1, 11, 2):
                dve.wait_ge(S["tr_ps"], g + 1)
                for dst, src in tr_copies(g):
                    last = v.tensor_copy(dst, src)
                last.then_inc(S["tr_d"], 1)
            dve.wait_ge(S["wsel_ps"], 1)
            v.tensor_tensor(WB[:], spread(BANK[7][:, 0:32], 1, 2), WMASK, ALU.mult).then_inc(S["wsel_done"], 1)

            n = 0
            for i in range(1, QB_BLOCKS):
                nk = 128 * (i + 1)
                for h in range(IDX_HEADS):
                    dve.wait_ge(S["ix_relu"], n + 1)
                    weight = KI0[:, i, HD + h:HD + h + 1]
                    if h == 0:
                        last = v.tensor_scalar_mul(MSK[:, i - 1, 0:nk], RL[:, n % 2, 0:nk], weight)
                    else:
                        dve.wait_ge(S["ix_acc"], n)
                        last = v.scalar_tensor_tensor(MSK[:, i - 1, 0:nk], RL[:, n % 2, 0:nk], weight,
                                                      MSK[:, i - 1, 0:nk], ALU.mult, ALU.add)
                    last.then_inc(S["ix_acc"], 1)
                    n += 1
            for g in range(PAGES + 1):
                dve.wait_ge(S["kp_sum"], g + 1)
                if g < PAGES:
                    last = v.tensor_copy(SC[:, 128 * g:128 * g + 128], BANK[6 + g % 2][0:32, 0:128])
                else:
                    last = v.tensor_tensor(SC[:, PAST:PAST + NDEC], BANK[6 + g % 2][0:32, 0:NDEC], MASK_NEW_IX, ALU.add)
                last.then_inc(S["kp_row"], 1)
            dve.wait_ge(S["kp_row"], PAGES + 1)

            def take_eight(scores, top):
                own.done(v.max(top, scores))
                own.done(v.match_replace(scores, top, scores, TAKEN))

            def taken_to_mask(scores):
                return v.tensor_scalar(scores, scores, TAKEN_LIMIT, NEG, ALU.is_ge, ALU.mult)

            def normalise(n):
                dve.wait_ge(S["exp_done"], n + 1)
                c = n % 4
                own.done(v.reciprocal(SMALL[:, 40 + c:41 + c], SMALL[:, 36 + c:37 + c]))
                l = LP[:, n % 3, 0:128 * (c + 1)]
                v.tensor_scalar_mul(l, l, SMALL[:, 40 + c:41 + c]).then_inc(S["probs_done"], 1)

            def take_out(q):
                dve.wait_ge(S["pv_done"], 8 * q + 8)
                v.tensor_copy(OT[:, q, 0:SEQ], BANK[4 + q % 2][:, :]).then_inc(S["o_sb"], 1)

            dve.wait_ge(S["new_rows_out"], 16 * 2 * DEC_BATCH)
            dve.wait_ge(S["ix_causal"], 3)
            rounds = 0
            for n in range(N_STEPS):
                h, i = n // 4, n % 4
                nk = 128 * (i + 1)
                dve.wait_ge(S["sc_ps"], n + 1)
                if n >= 3:
                    dve.wait_ge(S["pt_ps"], n - 2)
                if h < HEADS_A or i == 0:
                    dve.wait_ge(toe_in[h % 2], 16 * (h // 2 + 1))
                    bias = TOE[:, h % 2, SEQ - nk:SEQ]
                else:
                    t = 3 * (h - HEADS_A) + i - 1
                    dve.wait_ge(S["tm_done"], t + 1)
                    bias = TM[:, t % 2, 0:nk]
                v.tensor_tensor_reduce(out=LP[:, n % 3, 0:nk], in0=BANK[n % 2][:, 0:nk], in1=bias, scale=-1.0,
                                       scalar=3.0e38, op0=ALU.add, op1=ALU.min,
                                       accum_out=SMALL[:, 32 + i:33 + i]).then_inc(S["logits_done"], 1)
                if n >= 1:
                    normalise(n - 1)
                if n >= 10 and (n - 10) % 8 == 0:
                    take_out((n - 10) // 8)
                if n < 48:
                    b = n % 3
                    take_eight(MSK[:, b, 0:128 * (b + 2)], SMALL[:, 16:24])
                    if n == 47:
                        for b in range(3):
                            last = taken_to_mask(MSK[:, b, 0:128 * (b + 2)])
                        last.then_inc(S["topk_prompt_done"], 1)
                else:
                    take_eight(SC[:], SMALL[0:32, 24:32])
                    rounds += 1
            normalise(N_STEPS - 1)
            take_out(7)

            v.tensor_tensor(NMA[:], spread(BIAS_N[:, 0:HEADS_A, :], 1, DEC_BATCH),
                            spread(MASK_NEW_A, 2, HEADS_A), ALU.add)
            own.done(v.memset(STA[:, 7, :], NEG))

            def logits_a(k):
                v.tensor_tensor(STA[:, k, :].rearrange("p (b c) -> p b c", b=8),
                                BANK[4 + k % 2][:, 0:384].rearrange("p (b c) -> p b c", b=8),
                                spread(BIAS_A[:, k].rearrange("p h t -> p (h t)"), 1, 8), ALU.add
                                ).then_inc(S["ka_logits"], 1)

            for n in range(56):
                k, b = n // 8, n % 8
                dve.wait_ge(S["ka_t"], n + 1)
                if n >= 2:
                    dve.wait_ge(S["ka_sc"], n - 1)
                v.tensor_copy(KTA[:, n % 2, 512:768], BANK[2 * (n % 2) + 1][:, 0:256]).then_inc(S["ka_sb_d"], 1)
                if b == 1 and k >= 1:
                    dve.wait_ge(S["ka_sc"], 8 * k)
                    logits_a(k - 1)
                if rounds < TOPK_DEC // 8 and n % 3 == 0:
                    take_eight(SC[:], SMALL[0:32, 24:32])
                    rounds += 1
            dve.wait_ge(S["ka_sc"], 57)
            logits_a(6)
            v.tensor_tensor(STA[0:32, 7, :], BANK[6][0:32, 0:384], NMA[:].rearrange("p b h t -> p (b h t)"), ALU.add
                            ).then_inc(S["ka_logits"], 1)
            dve.wait_ge(S["ka_logits"], 8)
            while rounds < TOPK_DEC // 8:
                take_eight(SC[:], SMALL[0:32, 24:32])
                rounds += 1
            taken_to_mask(SC[:]).then_inc(S["topk_dec_done"], 1)

            v.tensor_reduce(MX[:], STA[:].rearrange("p k c -> p c k"), AX.X, ALU.max).then_inc(S["mxa_done"], 1)
            dve.wait_ge(S["mxa_t"], 1)
            own.done(v.tensor_reduce(SMALL[:, 44:47], BANK[2][:, 0:384].rearrange("p (g c) -> p g c", g=3), AX.X, ALU.max))
            for gdx in range(3):
                last = v.tensor_scalar(DIAG[:, gdx, :], IDENT, SMALL[:, 44 + gdx:45 + gdx], float(D_MODEL), ALU.mult, ALU.mult)
            last.then_inc(S["diaga_done"], 1)
            dve.wait_ge(S["maxa_all"], 1)
            for k in range(8):
                v.tensor_tensor(STA[:, k, :], STA[:, k, :], BANK[1][:, 0:384], ALU.subtract).then_inc(S["suba_done"], 1)
            dve.wait_ge(S["dena_ps"], 1)
            own.done(v.reciprocal(RD[:], BANK[3][:, 0:384]))
            own.done(v.tensor_scalar_mul(RD[:], RD[:], 1.0 / D_MODEL))
            dve.wait_ge(S["va_all"], 1)
            for h2 in range(2):
                lo = slice(64 * h2, 64 * h2 + 64)

                def cut(t):
                    return t.rearrange("p (b c h t) -> p c b h t", b=8, c=6, h=2)[:, :, :, h2, :]
                last = v.tensor_tensor(OT[lo, 0:6, SEQ:T].rearrange("p c (b t) -> p c b t", t=4),
                                       cut(BANK[7][lo, 0:384]), cut(RD[lo, 0:384]), ALU.mult)
            last.then_inc(S["oa_done"], 1)

            own.done(v.memset(STB[:, 16, :], NEG))
            dve.wait_ge(S["taken_t"], 1)
            v.tensor_copy(SELT[:, 0:16, :].rearrange("p g n -> p (g n)"), BANK[6][:, :])
            v.tensor_copy(SELT[0:32, 16, :], BANK[5][0:32, 0:32]).then_inc(S["taken_sb"], 1)
            dve.wait_ge(S["taken_sb"], 1)
            for g in range(PAGES + 1):
                dve.wait_ge(S["kb_sc"], g + 1)
                parts = slice(0, 128) if g < PAGES else slice(0, 32)
                bank = BANK[4 + g % 2]
                lg = STB[parts, g, :].rearrange("p (b h t) -> p b h t", b=8, t=4)
                own.done(v.tensor_tensor(lg, bank[parts, 0:128].rearrange("p (b h t) -> p b h t", b=8, t=4),
                                         spread(SELT[parts, g, :].rearrange("p (b t) -> p b t", t=4), 2, HEADS_B), ALU.add))
                bias = BIAS_B[:, g] if g < PAGES else BIAS_N[:, HEADS_A:16, :]
                v.tensor_tensor(lg, lg, spread(bias, 1, 8), ALU.add).then_inc(S["kb_logits"], 1)
            dve.wait_ge(S["kb_logits"], PAGES + 1)
            v.tensor_reduce(MX[:, 0:128], STB[:].rearrange("p k c -> p c k"), AX.X, ALU.max).then_inc(S["mxb_done"], 1)
            dve.wait_ge(S["mxb_t"], 1)
            own.done(v.tensor_reduce(SMALL[:, 47:48], BANK[2][:, 0:128], AX.X, ALU.max))
            v.tensor_scalar(DIAG[:, 0, :], IDENT, SMALL[:, 47:48], float(D_MODEL), ALU.mult, ALU.mult
                            ).then_inc(S["diagb_done"], 1)
            dve.wait_ge(S["maxb_all"], 1)
            v.tensor_tensor(STB[:], STB[:], spread(BANK[1][:, 0:128], 1, 17), ALU.subtract).then_inc(S["subb_done"], 1)
            dve.wait_ge(S["denb_ps"], 1)
            own.done(v.reciprocal(RD[:, 0:128], BANK[3][:, 0:128]))
            own.done(v.tensor_scalar_mul(RD[:, 0:128], RD[:, 0:128], 1.0 / D_MODEL))
            dve.wait_ge(S["vb_all"], 1)
            for b2 in range(2):
                up = slice(64 * b2, 64 * b2 + 64)
                for h2 in range(2):
                    lo = slice(64 * h2, 64 * h2 + 64)

                    def cut(t):
                        return t.rearrange("p (a b c h t) -> p c a b h t", a=4, b=2, c=2, h=2)[:, :, :, b2, h2, :]
                    last = v.tensor_tensor(
                        OT[lo, 6:8, SEQ:T].rearrange("p c (a b t) -> p c a b t", b=2, t=4)[:, :, :, b2, :],
                        cut(BANK[7][up, 0:128]), cut(RD[up, 0:128]), ALU.mult)
            own.done(last)
            for c in range(KD):
                v.tensor_copy(OH_[:, c, :], OT[:, c, :]).then_inc(S["oh_ready"], 1)
            dve.wait_ge(S["o_ready"], KD)

            down_stage(1)
            layer_norm(1)
            up_stage(1)
            dve.wait_ge(S["p_in"], 16)
            own.done(v.tensor_copy(PH[:], P_RAW[:]))
            own.done(v.tensor_tensor(PL[:], P_RAW[:], PH[:].bitcast(F32), ALU.subtract))
            down_stage(2)
            layer_norm(2)
            for m in range(KD):
                s = m % 2
                dve.wait_ge(S["gate_sig"], m + 1)
                if m >= 2:
                    dve.wait_ge(y_out[s], 16 * (m // 2))
                for n in range(2):
                    last = v.tensor_tensor(half(HF, s, n), half(SG, s, n), BANK[4 * s + 2 + n][:, 0:HALF], ALU.mult)
                own.done(last)
                own.done(v.tensor_tensor(HF[:, s, :], HF[:, s, :], XH[:, m, :].bitcast(F32), ALU.add))
                v.tensor_tensor(HF[:, s, :], HF[:, s, :], XL[:, m, :].bitcast(F32), ALU.add).then_inc(S["y_final"], 1)

        @block.tensor
        def _(pe):
            mm = nc.tensor.matmul

            def tile(banks, s, j, xh, xl, start, stop):
                wh, wl = WH[:, s, j, :], WL[:, s, j, :]
                for n in range(2):
                    mm(banks[n][:, 0:HALF], wh, xh[n], start=start, stop=False)
                for n in range(2):
                    mm(banks[n][:, 0:HALF], wh, xl[n], start=False, stop=False)
                for n in range(2):
                    last = mm(banks[n][:, 0:HALF], wl, xh[n], start=False, stop=stop)
                return last

            def unit(u0, i, j, banks, high, low, k0, count, first, last_tile, ready=None):
                s = (u0 + j) % 2
                pe.wait_ge(S["lo_ready"], u0 + i * 4 + j + 1)
                for t in range(count):
                    if ready is not None:
                        pe.wait_ge(S["x_ready"], ready + t + 1)
                    k = k0 + t
                    last = tile(banks, s, t, [half(high, k, n) for n in range(2)], [half(low, k, n) for n in range(2)],
                                first and t == 0, last_tile and t == count - 1)
                return last

            def up_stage(which):
                u0 = FIRST[("wi1", "wi2")[which]]

                def pair(i, ready=None):
                    for s in range(2):
                        if not (isinstance(i, int) and i == 0 and which == 0):
                            pe.wait_ge(S["h_done"], 22 * which + i * 2 + s - 1)
                        for j in (2 * s, 2 * s + 1):
                            banks = BANK[4 * s + 2 * (j % 2):4 * s + 2 * (j % 2) + 2]
                            unit(u0, i, j, banks, XH, XL, 0, KD, True, True, ready if j == 0 else None
                                 ).then_inc(S["unit_used"], 1)

                pair(0, ready=KD * 2 * which)
                with pe.Fori(1, UP_ITERS) as i:
                    pair(i)

            def down_stage(which):
                name, order = ("wo1", "wo2")[which], (0, 2)[which]
                u0 = FIRST[name]
                pe.wait_ge(S["hl_done"], KF * (which + 1))

                def pair(i):
                    for s in range(2):
                        if not (isinstance(i, int) and i == 0 and which == 0):
                            pe.wait_ge(S["y_part"], KD * order + i * 2 + s - 1)
                        for part in range(2):
                            unit(u0, i, 2 * s + part, BANK[2 * s:2 * s + 2], HH, HL, UNIT_TILES * part, UNIT_TILES,
                                 part == 0, part == 1).then_inc(S["unit_used"], 1)

                pair(0)
                with pe.Fori(1, KD // 2) as i:
                    pair(i)

            def layer_norm(which):
                pe.wait_ge(S["sum_done"], KD * (which + 1))
                for n, (a, b) in enumerate(HALVES):
                    last = mm(BANK[4 + n][:, 0:HALF], ONES[:], SUM[:, a:b], start=True, stop=True)
                last.then_inc(S["mean_ps"], 1)
                for m in range(KD):
                    pe.wait_ge(S["squared"], KD * which + m + 1)
                    for n in range(2):
                        last = mm(BANK[6 + n][:, 0:HALF], ONES[:], half(SQ, m % 2, n), start=m == 0, stop=m == KD - 1)
                    last.then_inc(S["sq_used"], 1)

            pe.wait_ge(S["setup_in"], 16 * 9)
            mm(BANK[3][0:16, :], RELC[:], TP[:, 0:512], start=True, stop=True)
            mm(BANK[4][0:16, 0:128], RELC[:], TP[:, 512:640], start=True, stop=True)
            pe.wait_ge(S["relt_done"], 1)
            relt = RELT[:].rearrange("p h t -> p (h t)")
            for k in range(KEY_BLOCKS_A):
                mm(BANK[0][:, 48 * k:48 * k + 48], OH[:, k, :], relt[:, 0:48], start=True, stop=True)
            for g in range(PAGES):
                mm(BANK[1][:, 16 * g:16 * g + 16], OH[:, KEY_BLOCKS_A + g, :], relt[:, 48:64], start=True, stop=True)
            mm(BANK[2][0:32, 0:64], OH[:, BLK_NEW, 0:32], relt, start=True, stop=True).then_inc(S["tables_ps"], 1)
            pe.wait_ge(S["rev_in"], 1)
            pe.wait_ge(S["dve_step"], 2)
            up_stage(0)
            down_stage(0)
            layer_norm(0)

            def project(i, ready=None, count=4):
                for j in range(count):
                    if not (isinstance(i, int) and i == 0):
                        pe.wait_ge(S["proj_a"], i * 4 + j - 3)
                        pe.wait_ge(S["proj_d"], i * 4 + j - 3)
                    unit(FIRST["w_in"], i, j, BANK[2 * j:2 * j + 2], XH, XL, 0, KD, True, True,
                         ready if j == 0 else None).then_inc(S["unit_used"], 1)

            project(0, ready=KD)
            with pe.Fori(1, 6) as i:
                project(i)
            project(6, count=2)

            pe.wait_ge(S["proj_a"], N_PROJ)
            pe.wait_ge(S["proj_d"], N_PROJ)
            tr = nc.tensor.transpose
            for k in range(5):
                n = 128 if k < 4 else NDEC
                last = tr(BANK[0][0:n, 72 * k:72 * k + 72], PROJ[0:72, C_IDX, 128 * k:128 * k + n], IDENT[0:72, 0:72])
            last.then_inc(S["kiw_ps"], 1)
            for g in range(11):
                bank = BANK[2 + g % 6]
                if g >= 6:
                    pe.wait_ge(S["tr_a"] if g % 2 == 0 else S["tr_d"], (g - 6) // 2 + 1)
                for q in range(4):
                    if g < 6:
                        blk, c = (4 * g + q) // 6, (4 * g + q) % 6
                        src, n = PROJ[:, C_VA + c, 128 * blk:128 * blk + 128], 128
                    elif g == 6:
                        src, n = PROJ[:, C_KV, 128 * q:128 * q + 128], 128
                    elif g < 10:
                        src, n = PROJ[:, C_KA + 4 * (g - 7) + q, SEQ:T], NDEC
                    elif q == 0:
                        src, n = PROJ[:, C_KV, SEQ:T], NDEC
                    else:
                        break
                    last = tr(bank[0:n, 128 * q:128 * q + 128], src, IDENT)
                last.then_inc(S["tr_ps"], 1)
            pe.wait_ge(S["kin_done"], 1)
            for k in range(4):
                tr(BANK[1][:, 128 * k:128 * k + 128], KIN[:, k, :], IDENT)
            tr(BANK[0][:, 480:512], KIN[0:32, 4, :], IDENT[0:32, 0:32]).then_inc(S["kit_ps"], 1)
            pe.wait_ge(S["tr_d"], 3)
            mm(BANK[7][:, 0:32], SEL_HEAD, PROJ[64:72, C_IDX, SEQ:T], start=True, stop=True).then_inc(S["wsel_ps"], 1)
            pe.wait_ge(S["kit_sb"], 1)
            n = 0
            for i in range(1, QB_BLOCKS):
                nk = 128 * (i + 1)
                for h in range(IDX_HEADS):
                    if n >= 2:
                        pe.wait_ge(S["ix_relu"], n - 1)
                    lo = slice(64 * (h % 2), 64 * (h % 2) + 64)
                    mm(BANK[n % 2][:, 0:nk], PROJ[lo, C_QI + h // 2, 128 * i:128 * i + 128], KIT[lo, 0:nk],
                       start=True, stop=True).then_inc(S["ix_ps"], 1)
                    n += 1

            pe.wait_ge(S["wsel_done"], 1)
            pe.wait_ge(S["qblocks_done"], 1)
            pe.wait_ge(S["tr_a"], 6)
            pe.wait_ge(S["tr_d"], 5)

            def page_transposes(g, n, bank, sem):
                pe.wait_ge(pg_in[n % 4], 128 * (n // 4 + 1))
                for p in range(4):
                    last = tr(bank[:, 128 * p:128 * p + 128],
                              PG[:, n % 4, 2 * p:2 * p + 2, :].rearrange("p b n -> p (b n)"), IDENT)
                last.then_inc(sem, 1)

            def index_scores(g):
                if g < PAGES:
                    pe.wait_ge(S["kp_sb"], g + 1)
                if g >= 2:
                    pe.wait_ge(S["kp_relu"], g - 1)
                nk = 128 if g < PAGES else NDEC
                for p in range(4):
                    keys = KIPT[:, g % 2, p, :] if g < PAGES else KIT[:, SEQ:T]
                    last = mm(BANK[4 + g % 2][64 * (p % 2):64 * (p % 2) + 64, 128 * (p // 2):128 * (p // 2) + nk],
                              QIB[:, p, :], keys, start=True, stop=True)
                last.then_inc(S["kp_sc"], 1)

            def index_sum(g):
                pe.wait_ge(S["kp_relu"], g + 1)
                if g >= 2:
                    pe.wait_ge(S["kp_row"], g - 1)
                nk = 128 if g < PAGES else NDEC
                for a in range(2):
                    last = mm(BANK[6 + g % 2][0:32, 0:nk], WB[:, a, :], RLD[:, g % 2, a, 0:nk], start=a == 0, stop=a == 1)
                last.then_inc(S["kp_sum"], 1)

            for g in range(PAGES + 3):
                if g < PAGES:
                    if g >= 2:
                        pe.wait_ge(S["kp_sb"], g - 1)
                    page_transposes(g, g, BANK[2 + g % 2], S["kp_t"])
                if 1 <= g < PAGES + 2:
                    index_scores(g - 1)
                if g >= 2:
                    index_sum(g - 2)

            def scores(n):
                h, i = n // 4, n % 4
                if n >= 2:
                    pe.wait_ge(S["logits_done"], n - 1)
                nk = 128 * (i + 1)
                base = 64 * (h % 2)
                lo = slice(base, base + 64)
                if h < HEADS_A:
                    keys = PROJ[lo, C_KA + h // 2, 0:nk]
                else:
                    keys = KB2[lo, 0:nk] if base else PROJ[lo, C_KV, 0:nk]
                mm(BANK[n % 2][:, 0:nk], PROJ[lo, C_QA + h // 2, 128 * i:128 * i + 128], keys,
                   start=True, stop=True).then_inc(S["sc_ps"], 1)

            def transposed(n):
                pe.wait_ge(S["probs_done"], n + 1)
                if n >= 2:
                    pe.wait_ge(S["pt_sb"], n - 1)
                for j in range(n % 4 + 1):
                    last = tr(BANK[2 + n % 2][:, 128 * j:128 * j + 128], LP[:, n % 3, 128 * j:128 * j + 128], IDENT)
                last.then_inc(S["pt_ps"], 1)

            def values(n):
                h, i = n // 4, n % 4
                q, base = h // 2, 64 * (h % 2)
                if n % 8 == 0 and q >= 2:
                    pe.wait_ge(S["o_sb"], q - 1)
                pe.wait_ge(S["pt_sb"], n + 1)
                for j in range(i + 1):
                    val = VP[:, j, 64 * h:64 * h + 64] if h < HEADS_A else VBT[:, j, HD:128]
                    last = mm(BANK[4 + q % 2][base:base + 64, 128 * i:128 * i + 128], val,
                              PTS[:, n % 2, 128 * j:128 * j + 128], start=j == 0, stop=j == i)
                last.then_inc(S["pv_done"], 1)

            pe.wait_ge(S["kp_row"], PAGES + 1)
            pe.wait_ge(S["ix_relu"], 24)
            for n in range(N_STEPS + 2):
                if n < N_STEPS:
                    scores(n)
                if 1 <= n < N_STEPS + 1:
                    transposed(n - 1)
                if n >= 2:
                    values(n - 2)

            pe.wait_ge(S["o_sb"], 8)

            def key_scores_a(n):
                k, b = n // 8, n % 8
                pe.wait_ge(S["ka_sb_a"], n + 1)
                pe.wait_ge(S["ka_sb_d"], n + 1)
                if b == 0 and k >= 2:
                    pe.wait_ge(S["ka_logits"], k - 1)
                for c in range(6):
                    last = mm(BANK[4 + k % 2][:, 48 * b + 8 * c:48 * b + 8 * c + 8], KTA[:, n % 2, 128 * c:128 * c + 128],
                              QBLKA[:, c, b, :], start=True, stop=True)
                last.then_inc(S["ka_sc"], 1)

            for n in range(57):
                if n < 56:
                    pe.wait_ge(ar_in[n % 3], 16 * (n // 3 + 1))
                    if n >= 2:
                        pe.wait_ge(S["ka_sb_a"], n - 1)
                        pe.wait_ge(S["ka_sb_d"], n - 1)
                    for c in range(6):
                        last = tr(BANK[2 * (n % 2) + c // 4][:, 128 * (c % 4):128 * (c % 4) + 128],
                                  AR[:, n % 3, 128 * c:128 * c + 128], IDENT)
                    last.then_inc(S["ka_t"], 1)
                if n >= 1:
                    key_scores_a(n - 1)
            for c in range(6):
                out = BANK[6][0:32, 0:384].rearrange("p (b c n) -> p b c n", b=8, c=6)[:, :, c, :]
                last = mm(out, PROJ[:, C_KA + c, SEQ:T], QBLKA[:, c, :, :], start=True, stop=True)
            last.then_inc(S["ka_sc"], 1)
            pe.wait_ge(S["mxa_done"], 1)
            for q in range(3):
                last = tr(BANK[2][:, 128 * q:128 * q + 128], MX[:, 128 * q:128 * q + 128], IDENT)
            last.then_inc(S["mxa_t"], 1)
            pe.wait_ge(S["topk_dec_done"], 1)
            for g in range(PAGES):
                tr(BANK[6][:, 32 * g:32 * g + 32], SC[:, 128 * g:128 * g + 128], IDENT[0:32, 0:32])
            tr(BANK[5][0:32, 0:32], SC[:, PAST:PAST + NDEC], IDENT[0:32, 0:32]).then_inc(S["taken_t"], 1)
            pe.wait_ge(S["diaga_done"], 1)
            mm(BANK[1][:, 0:384], ONES[:], DIAG[:].rearrange("p a n -> p (a n)"), start=True, stop=True
               ).then_inc(S["maxa_all"], 1)
            for k in range(8):
                pe.wait_ge(S["expa_done"], k + 1)
                last = mm(BANK[3][:, 0:384], ONES[:], STA[:, k, :], start=k == 0, stop=k == 7)
            last.then_inc(S["dena_ps"], 1)
            for b in range(DEC_BATCH):
                for k in range(8):
                    n = 56 + 7 * b + k
                    if k < 7:
                        pe.wait_ge(ar_in[n % 3], 16 * (n // 3 + 1))
                    for c in range(6):
                        col = 48 * b + 8 * c
                        val = AR[:, n % 3, 128 * c:128 * c + 128] if k < 7 else VNEW[:, 128 * c:128 * c + 128]
                        probs = STA[:, k, col:col + 8] if k < 7 else STA[0:32, 7, col:col + 8]
                        last = mm(BANK[7][:, col:col + 8], val, probs, start=k == 0 and c == 0,
                                  stop=k == 7 and c == 5, skip_group_check=True)
                    if k < 7:
                        last.then_inc(S["va_used"], 1)
                    elif b == DEC_BATCH - 1:
                        last.then_inc(S["va_all"], 1)

            def key_scores_b(g):
                if g >= 2:
                    pe.wait_ge(S["kb_logits"], g - 1)
                if g < PAGES:
                    pe.wait_ge(S["kb_sb"], g + 1)
                    for p in range(4):
                        last = mm(BANK[4 + g % 2][:, 32 * p:32 * p + 32], KTB[:, g % 2, 128 * p:128 * p + 128],
                                  QBLKB[:, p, :], start=True, stop=True)
                    last.then_inc(S["kb_sc"], 1)

            pe.wait_ge(S["oa_done"], 1)
            for g in range(PAGES + 1):
                if g < PAGES:
                    n = PAGES + g
                    if g >= 2:
                        pe.wait_ge(S["kb_sb"], g - 1)
                    page_transposes(g, n, BANK[g % 2], S["kb_t"])
                if g >= 1:
                    if g == 1:
                        pe.wait_ge(S["taken_sb"], 1)
                    key_scores_b(g - 1)
            pe.wait_ge(S["kb_logits"], PAGES - 1)
            mm(BANK[4][0:32, 0:128], KB2[:, SEQ:T], QBLKB[:].rearrange("p a n -> p (a n)"), start=True, stop=True
               ).then_inc(S["kb_sc"], 1)
            pe.wait_ge(S["mxb_done"], 1)
            tr(BANK[2][:, 0:128], MX[:, 0:128], IDENT).then_inc(S["mxb_t"], 1)
            pe.wait_ge(S["diagb_done"], 1)
            mm(BANK[1][:, 0:128], ONES[:], DIAG[:, 0, :], start=True, stop=True).then_inc(S["maxb_all"], 1)
            pe.wait_ge(S["expb_done"], 1)
            for g in range(17):
                last = mm(BANK[3][:, 0:128], ONES[:], STB[:, g, :], start=g == 0, stop=g == 16)
            last.then_inc(S["denb_ps"], 1)
            for g in range(17):
                n = 2 * PAGES + g
                if g < PAGES:
                    pe.wait_ge(pg_in[n % 4], 128 * (n // 4 + 1))
                for p in range(4):
                    val = PG[:, n % 4, 2 * p:2 * p + 2, :].rearrange("p b n -> p (b n)") if g < PAGES else VBN[:]
                    probs = STB[:, g, 32 * p:32 * p + 32] if g < PAGES else STB[0:32, 16, 32 * p:32 * p + 32]
                    last = mm(BANK[7][:, 32 * p:32 * p + 32], val, probs, start=g == 0 and p == 0,
                              stop=g == 16 and p == 3, skip_group_check=True)
                last.then_inc(S["vb_used"] if g < PAGES else S["vb_all"], 1)

            u0 = FIRST["w_out"]
            pe.wait_ge(S["o_ready"], KD)
            for i in range(2):
                for j in range(4):
                    s = j % 2
                    pe.wait_ge(S["y_part"], KD + i * 4 + j - 1) 
                    unit(u0, i, j, BANK[2 * s:2 * s + 2], OH_, OL_, 0, KD, True, True).then_inc(S["unit_used"], 1)
            layer_norm(1)
            up_stage(1)
            down_stage(1)
            layer_norm(2)
            u0 = FIRST["gate"]
            for m in range(KD):
                s = m % 2
                if m >= 2:
                    pe.wait_ge(S["y_final"], m - 1)
                unit(u0, 0, m, BANK[4 * s:4 * s + 2], XH, XL, 0, KD, True, True, KD * 3 if m == 0 else None)
                for t in range(KP):
                    last = tile(BANK[4 * s + 2:4 * s + 4], (u0 + m) % 2, KD + t, [half(PH, t, n) for n in range(2)],
                                [half(PL, t, n) for n in range(2)], t == 0, t == KP - 1)
                last.then_inc(S["unit_used"], 1)


def bucket(d):
    d = np.maximum(d, 0)
    exact = BUCKETS // 2
    scaled = np.log(np.maximum(d, 1) / exact) / log(REL_MAX / exact)
    large = exact + np.floor(scaled * (BUCKETS - exact) + 1e-9).astype(int)
    return np.where(d < exact, d, np.minimum(large, BUCKETS - 1))


def log_count(d):
    count = sum(((d >= 0) & (d <= window) & (d % dil == 0)).astype(int) for window, dil in PATTERNS)
    return np.where(count > 0, np.log(np.maximum(count, 1)), NEG)


def shape_constants():
    consts = np.zeros((128, 444), np.float32)
    consts[:, 0:128] = np.eye(128)
    p = np.arange(128)
    rows = [16 * (32 * k + p // 4) + p % 4 for k in range(STRIDED_BLOCKS)]
    rows += [PAST - 512 + 128 * k + p for k in range(4)]
    t = np.arange(4)
    for k, r in enumerate(rows):
        consts[:, 128 + 4 * k:132 + 4 * k] = log_count(PAST + t[None, :] - r[:, None])
    kb, kt = np.arange(32) // 4, np.arange(32) % 4
    own = kb[:, None] == kb[None, :]
    consts[0:32, 156:188] = np.where(own, log_count(kt[None, :] - kt[:, None]), NEG)
    consts[0:32, 188:220] = np.where(own & (kt[None, :] <= kt[:, None]), 0.0, NEG)
    consts[64:72, 220:348] = (p % 32 // 4)[None, :] == np.arange(8)[:, None]
    for a in range(2):
        q = np.arange(32)
        consts[:, 348 + 32 * a:380 + 32 * a] = IDX_SCALE * (
            (q // 4 == 4 * a + p[:, None] // 32) & (q % 4 == p[:, None] % 4))
    onehots = np.zeros((128, 24, 128), np.float32)
    keys = rows + [128 * g + p for g in range(PAGES)]
    for k, r in enumerate(keys):
        for step in range(4):
            onehots[32 * step + bucket(PAST + step - r), k, p] = 1.0
    for step in range(4):
        onehots[32 * step + bucket(step - kt), BLK_NEW, np.arange(32)] = 1.0
    toeplitz = np.zeros((34, 640), np.float32)
    d = 511 - np.arange(640)
    toeplitz[bucket(d), np.arange(640)] = 1.0
    toeplitz[32] = log_count(d)
    toeplitz[33] = np.where(d >= 0, 0.0, NEG)
    rel_rows = np.zeros((2, 16), np.float32)
    rel_rows[0, :HEADS_A] = 1.0
    rel_rows[1, HEADS_A:] = 1.0
    return consts, onehots, toeplitz, rel_rows


def kernel(x_prompt, x_sample, cache_a_kv, cache_b, page_table, p_prompt, p_sample, ln_g, ln_b,
           ffn1_wi, ffn1_wo, w_in, kidx_ln_g, kidx_ln_b, w_out, ffn2_wi, ffn2_wo, ple_proj, ple_gate,
           rel_bias):
    import concourse.bacc as bacc
    from concourse.bass_utils import run_bass_kernel_spmd

    def features(a, b, chunks):
        both = np.concatenate([np.asarray(a).reshape(SEQ, -1), np.asarray(b).reshape(NDEC, -1)])
        return np.ascontiguousarray(both.T.reshape(chunks, 128, T).transpose(1, 0, 2))

    def units(a, tiles, count, parts=1):
        a = np.asarray(a).reshape(parts, tiles, 128, count, 128)
        return a.transpose(3, 0, 2, 1, 4).reshape(count * parts, 128, tiles, 128)

    def up_units(a):
        u = units(a, KD, 2 * KF)
        return np.ascontiguousarray(u.reshape(2, KF, 128, KD, 128).transpose(1, 0, 2, 3, 4)).reshape(2 * KF, 128, KD, 128)

    wa, wb, wi_ = WIDTH_A, HEADS_B * HD, IDX_HEADS * HD
    w_in0 = np.asarray(w_in)[0]
    at = np.cumsum([0, wa, wa, wa, wb, HD, HD, wi_, HD, IDX_HEADS])
    qa, ka, va, qb, kb, vb, qi, ki, wi = (w_in0[:, at[n]:at[n + 1]] for n in range(9))
    pad = np.zeros((D_MODEL, 128 - HD - IDX_HEADS), w_in0.dtype)
    w_proj = np.concatenate([qa, qb, qi, ki, wi, pad, kb, vb, ka, va], axis=1)
    gate = units(np.asarray(ple_gate)[0], KD, KD)
    ple = units(np.asarray(ple_proj)[0], KP, KD)
    w = {
        "wi1": up_units(np.asarray(ffn1_wi)[0]),
        "wo1": units(np.asarray(ffn1_wo)[0], UNIT_TILES, KD, 2),
        "w_in": units(w_proj, KD, N_PROJ),
        "w_out": units(np.asarray(w_out)[0], KD, KD),
        "wi2": up_units(np.asarray(ffn2_wi)[0]),
        "wo2": units(np.asarray(ffn2_wo)[0], UNIT_TILES, KD, 2),
        "gate": np.concatenate([gate, ple], axis=2),
    }
    ln = np.stack([np.asarray(ln_g)[0], np.asarray(ln_b)[0]], axis=1).reshape(6, KD, 128).transpose(2, 0, 1)
    consts, onehots, toeplitz, rel_rows = shape_constants()
    n_pool = np.asarray(cache_b).shape[1]
    arrays = {
        "x_t": features(x_prompt, x_sample, KD),
        "p_t": features(p_prompt, p_sample, KP),
        "cache_a": np.asarray(cache_a_kv).reshape(DEC_BATCH, PAST, 2 * WIDTH_A),
        "cache_b": np.asarray(cache_b).reshape(n_pool, PAGE, ROW_B),
        "page_table": np.asarray(page_table),
        "ln": ln,
        "kidx_g": np.asarray(kidx_ln_g)[0],
        "kidx_b": np.asarray(kidx_ln_b)[0],
        "rel_bias": np.asarray(rel_bias),
        "rel_rows": rel_rows, "consts": consts, "onehots": onehots, "toeplitz": toeplitz,
    }
    arrays.update({"w_" + name: a for name, a in w.items()})
    arrays = {name: np.ascontiguousarray(a) for name, a in arrays.items()}
    outs = {
        "y_t": (KD, 128, T), "kv_a_t": (12, 128, SEQ), "a_sample": (DEC_BATCH, PAST, 2 * WIDTH_A),
        "kv_b_t": (128, T), "ki_b": (128, 5, HD),
    }
    nc = bacc.Bacc("TRN2", target_bir_lowering=False, num_devices=1)
    ins = {name: nc.dram_tensor("in_" + name, a.shape, mybir.dt.from_np(a.dtype), kind="ExternalInput").ap()
           for name, a in arrays.items()}
    res = {name: nc.dram_tensor("out_" + name, shape, F32, kind="ExternalOutput").ap() for name, shape in outs.items()}
    weights = {name: ins.pop("w_" + name) for name in w}
    build_program(nc, w=weights, **ins, **res)
    r = run_bass_kernel_spmd(nc, [{"in_" + name: a for name, a in arrays.items()}], core_ids=[0]).results[0]

    y = r["out_y_t"].transpose(2, 0, 1).reshape(T, D_MODEL)
    kv = r["out_kv_a_t"].reshape(2, HEADS_A, HD, SEQ).transpose(3, 0, 1, 2)
    row_b = np.concatenate([r["out_kv_b_t"].T, r["out_ki_b"].transpose(1, 0, 2).reshape(640, HD)[:T]], axis=1)
    return (
        y[:SEQ].reshape(1, SEQ, D_MODEL), y[SEQ:].reshape(DEC_BATCH, DEC_SEQ, D_MODEL),
        kv.reshape(1, 1, SEQ, 2, HEADS_A, HD),
        r["out_a_sample"].reshape(1, DEC_BATCH, PAST, 2, HEADS_A, HD),
        row_b[:SEQ].reshape(1, 1, SEQ, ROW_B), row_b[SEQ:].reshape(1, DEC_BATCH, DEC_SEQ, ROW_B),
    )
```

```python
from contextlib import ExitStack
from math import log

import concourse.bass as bass
import numpy as np
from concourse import mybir

F32 = mybir.dt.float32
F32R = mybir.dt.float32r
I32 = mybir.dt.int32
ACT = mybir.ActivationFunctionType
ALU = mybir.AluOpType
AX = mybir.AxisListType

D_MODEL, SEQ, DEC_BATCH, DEC_SEQ, PAST, PAGE = 1024, 512, 8, 4, 2048, 128
HD, HEADS_A, HEADS_B, IDX_HEADS = 64, 12, 4, 8
D_FF, D_PLE, BUCKETS, REL_MAX = 2816, 256, 32, 2048
ROW_B = 3 * HD
WIDTH_A = HEADS_A * HD
ALPHA = 2.0 ** 0.25
LN_EPS = 1e-5
PATTERNS = ((128, 1), (512, 4), (2048, 16))
TOPK_PROMPT, TOPK_DEC = 128, 256
IDX_SCALE = HD ** -0.5 * IDX_HEADS ** -0.5
NEG = -1.0e30
TAKEN = -3.0e38
TAKEN_LIMIT = -2.0e38

NDEC = DEC_BATCH * DEC_SEQ
T = SEQ + NDEC
HALF = T // 2
HALVES = ((0, HALF), (HALF, T))
KD = D_MODEL // 128
KF = D_FF // 128
KP = D_PLE // 128
UNIT_TILES = KF // 2
QB_BLOCKS = SEQ // 128
PAGES = PAST // PAGE

C_QI, C_IDX, C_KV, C_KA, C_VA, C_QA, C_QB, N_PROJ = 0, 4, 5, 6, 12, 18, 24, 26

KEY_BLOCKS_A, BLK_NEW = 7, 23
KEYS_A = 128 * KEY_BLOCKS_A
ALL_A = KEYS_A + DEC_BATCH * DEC_SEQ
STRIDED_BLOCKS = 3

STAGES = (("wi1", 44, 8), ("wo1", 16, 11), ("w_in", 26, 8), ("w_out", 8, 8),
          ("wi2", 44, 8), ("wo2", 16, 11), ("gate", 8, 10))
FIRST = {}
_u = 0
for _n, _c, _t in STAGES:
    FIRST[_n] = _u
    _u += _c
N_UNITS = _u
STAGE_TILES = {name: tiles for name, _, tiles in STAGES}
RAW_SLOTS, SPLIT_SLOTS = 4, 2
COPY_ROWS = 28
N_COPIES = (PAST - DEC_SEQ) // COPY_ROWS


def tiles_of(u):
    for name, count, tiles in STAGES:
        if u < FIRST[name] + count:
            return tiles
    raise ValueError(u)


def spread(ap, axis, n):
    a = ap.unsqueeze(axis)
    shape = list(a.shape)
    shape[axis] = n
    return a.broadcast_to(shape)


class Steps:

    def __init__(self, eng, sem):
        self.eng, self.sem, self.n = eng, sem, 0

    def done(self, instruction):
        instruction.then_inc(self.sem, 1)
        self.n += 1
        self.eng.wait_ge(self.sem, self.n)


def build_program(nc, x_t, p_t, cache_a, cache_b, page_table, ln, kidx_g, kidx_b, w, rel_bias,
                  rel_rows, consts, onehots, patterns, mask_new, toeplitz, y_t, kv_a_t, a_sample, kv_b_t, ki_b):
    ctx = ExitStack()
    with ctx:
        SBUF_FROM, SBUF_TO = 16512, 229344
        place = {"at": SBUF_FROM}

        def sb(name, shape, dt=F32, at=None):
            size = int(np.prod(shape[1:])) * 4
            if at is None:
                at = place["at"]
                place["at"] += (size + 31) // 32 * 32
                assert place["at"] <= SBUF_TO, (name, place["at"])
            return nc.alloc_sbuf_tensor_at(name, list(shape), dt, offset=at)

        XH = sb("x_high", [128, KD, T], F32R)
        XL = sb("x_rest", [128, KD, T], F32R)
        RAW = sb("w_raw", [128, RAW_SLOTS, UNIT_TILES, 128])
        split_at = place["at"]
        WH = sb("w_high", [128, SPLIT_SLOTS, UNIT_TILES, 128], F32R)
        WL = sb("w_rest", [128, SPLIT_SLOTS, UNIT_TILES, 128], F32R)
        h_at = place["at"]
        HH = sb("hidden_high", [128, KF, T], F32R)
        HL = sb("hidden_rest", [128, KF, T], F32R)
        h_end = y_at = place["at"]
        Y = sb("y", [128, KD, T])
        CP = sb("consts_sb", [128, 352])
        BIAS_A = sb("bias_a", [128, KEYS_A])
        BIAS_N = sb("bias_a_new", [128, 4, NDEC])
        RELB = sb("rel_b", [128, DEC_BATCH, HEADS_B, 4])
        LN = sb("ln_sb", [128, 6, KD])
        KIDX_GB = sb("kidx_gb", [128, 2, HD])
        ONES = sb("ones", [128, 128])
        PAGE_IDS = sb("page_ids", [1, DEC_BATCH * PAGES], I32)
        SMALL = sb("small", [128, 96])
        e_at = place["at"]

        IDENT = CP[:, 0:128]
        MASK_NEW_IX = CP[0:32, 128:160]
        SEL_HEAD = CP[64:72, 160:288]
        SEL_QUERY = CP[0:32, 160:288]
        WMASK = CP[:, 288:352].rearrange("p (k c) -> p k c", k=2)

        SG = sb("silu_gate", [128, 2, T], at=y_at)
        HF = sb("hidden", [128, 2, T], at=y_at + 2 * T * 4)
        P_RAW = sb("p_raw", [128, KP, T], at=y_at + 4 * T * 4)
        SUM = sb("sum_acc", [128, T], at=e_at)
        PH = sb("p_high", [128, KP, T], F32R, at=e_at + T * 4)
        PL = sb("p_rest", [128, KP, T], F32R, at=e_at + 3 * T * 4)
        OH = sb("onehots_sb", [128, 24, 128], at=h_at)
        TP = sb("toeplitz_sb", [34, 640], at=h_at + 12288)
        RELC = sb("rel_sb", [34, 16], at=h_at + 16384)
        RELREP = sb("rel_rep", [128, 16], at=h_at + 16512)
        RELA = sb("rel_a", [128, 2, 16, 4], at=h_at + 16640)
        LNC = sb("patterns_sb", [4, 1024], at=h_at + 20480)
        MNEW = sb("mask_new_sb", [128, 4, NDEC], at=h_at + 24576)
        REV = sb("rev_sb", [16, 640], at=h_at + 25088)
        ln_at = h_at + 70016
        MEAN = sb("mean", [128, T], at=ln_at)
        RSTD = sb("rstd", [128, T], at=ln_at + T * 4)
        SQ = sb("squares", [128, 2, T], at=ln_at + 2 * T * 4)
        XN = sb("x_new", [128, 2, T], at=ln_at + 4 * T * 4)
        PROJ = sb("proj", [128, N_PROJ, T], at=h_at)
        vp_at = h_at + N_PROJ * T * 4
        VP = sb("v_prompt", [128, QB_BLOCKS, WIDTH_A], at=vp_at)
        wk_at = vp_at + QB_BLOCKS * WIDTH_A * 4
        TOE = sb("bias_toeplitz", [128, 2, SEQ], at=wk_at)
        LP = sb("logits", [128, 3, SEQ], at=wk_at + 4096)
        PTS = sb("probs_t", [128, 2, SEQ], at=wk_at + 10240)
        MSK = sb("topk_work", [128, 3, SEQ], at=wk_at + 14336)
        TM = sb("bias_masked", [128, 2, SEQ], at=wk_at + 20480)
        KIT = sb("kidx_t", [128, T], at=wk_at + 24576)
        assert wk_at + 24576 + T * 4 <= h_end
        KI0 = sb("kidx_wi_tok", [128, 5, 72], at=wk_at + 20480)
        KIN = sb("kidx_norm", [128, 5, 128], at=wk_at + 20480 + 1440)
        RL = sb("idx_relu", [128, 2, SEQ], at=wk_at + 10240)
        KIPT = sb("kidx_pages_t", [128, 2, 4, 128], at=wk_at + 4096)
        RLD = sb("idx_relu_dec", [128, 2, 2, 128], at=wk_at + 8192)
        KNEW = sb("k_a_new_tok", [NDEC, WIDTH_A], at=y_at)
        VNEW = sb("v_a_new_tok", [NDEC, WIDTH_A], at=y_at + 3072)
        QIB = sb("q_idx_blocks", [128, 4, 64], at=y_at + 6144)
        WB = sb("w_idx_blocks", [128, 2, 32], at=y_at + 7168)
        PG = sb("idx_pages_ring", [128, 4, DEC_BATCH, HD], at=y_at + 7680)
        OT = sb("attn_out_t", [128, KD, T], at=y_at)
        OH_ = sb("attn_out_high", [128, KD, T], F32R, at=h_at)
        OL_ = sb("attn_out_rest", [128, KD, T], F32R, at=h_at + KD * T * 4)
        SC = sb("idx_scores", [NDEC, PAST + NDEC], at=e_at)
        KB2 = sb("k_b_high_half", [128, T], at=e_at + 8320)
        assert e_at + 10496 <= SBUF_TO and e_at + 5 * T * 4 <= SBUF_TO, SBUF_TO - e_at
        AR = sb("cache_a_ring", [128, 4, WIDTH_A], at=split_at)
        KTA = sb("k_a_t", [128, 2, WIDTH_A], at=split_at + 12288)
        KTB = sb("k_b_t", [128, 2, 512], at=split_at + 12288)
        KC = sb("k_b_pages", [128, 2, DEC_BATCH, HD], at=split_at + 16384)
        PTA = sb("probs_a_t", [128, 2, 8, 128], at=split_at + 12288)
        VBT = sb("kv_b_tok", [128, QB_BLOCKS, 128], at=split_at + 18432)
        VBN = sb("kv_b_new_tok", [NDEC, 128], at=split_at + 20480)
        assert split_at + 20992 <= h_at
        raw_at = SBUF_FROM + 2 * KD * T * 4
        QBLKA = sb("q_a_blocks", [128, 6, DEC_BATCH * 48 + 16], at=raw_at)
        QBLKB = sb("q_b_blocks", [128, 4, 32], at=raw_at + 9600)
        KNT = sb("k_a_new_t", [128, 6, NDEC], at=raw_at + 10112)
        OHB = sb("onehots_b", [128, 17, 128], at=raw_at + 11264)
        PTB = sb("probs_b_t", [128, 17, 128], at=raw_at + 11264)
        KVP = sb("kv_b_pages", [128, DEC_BATCH * PAGES, 128], at=h_at)
        STA = sb("logits_a", [128, 4, ALL_A], at=h_at + 65536)
        STB = sb("logits_b", [128, PAST + NDEC], at=h_at + 65536 + 14848)
        OA = sb("out_a", [128, WIDTH_A], at=h_at + 65536 + 23168)
        OB = sb("out_b", [128, 128], at=h_at + 65536 + 26240)
        VN2 = sb("v_a_new", [NDEC, WIDTH_A], at=h_at + 65536 + 26752)
        assert h_at + 65536 + 26752 + 3072 <= h_end
        SM_MINS, SM_MIN, SM_DEN, SM_BMAX, SM_BSUM = 64, 76, 80, 84, 90

        BANK = [ctx.enter_context(nc.psum_tensor(f"bank{i}", [128, 512], F32)) for i in range(8)]
        REV_DRAM = nc.dram_tensor("rev_bias", [16, 128, 640], F32, kind="Internal").ap()

        names = """setup_in ids_in ln_in ones_done relt_done tables_ps rev_in rev_out
            xh_ready x_ready hi_ready lo_ready unit_used
            silu_done h_done hh_done hl_done y_part y_full sum_done
            mean_ps mean_sb centred squared sq_used var_sb std_sb zed xn_done xh_ln
            p_in p_ready gate_sig y_final
            proj_a proj_d kiw_ps ki_var ki_std kin_done kit_ps kit_sb kb2_done tr_ps tr_a tr_d qblocks_done
            ix_ps ix_relu ix_acc wsel_ps wsel_done kp_t kp_sb kp_sc kp_relu kp_sum kp_row ix_causal
            topk_prompt_done sc_ps logits_done exp_done probs_done pt_ps pt_sb pv_done o_sb tm_done
            new_rows_out proj_out copy_done
            oh_in kv_b_new_in q_free vnew_in
            ka_t ka_sb ka_sc ka_logits expa_done
            topk_dec_done kc_ready kb_t kb_sb kb_sc b_logits b_max b_exp b_den
            pt_ps2 pt_a pt_d vb_all ob_sb oa_sb ob_t va_used va_pair ot_done o_tail o_tail_rest
            oh_ready o_ready dve_step""".split()
        S = {n: ctx.enter_context(nc.semaphore(n)) for n in names}
        raw_loaded = [ctx.enter_context(nc.semaphore(f"raw_loaded{i}")) for i in range(RAW_SLOTS)]
        toe_in = [ctx.enter_context(nc.semaphore(f"toe_in{i}")) for i in range(2)]
        ar_in = [ctx.enter_context(nc.semaphore(f"ar_in{i}")) for i in range(4)]
        pg_in = [ctx.enter_context(nc.semaphore(f"pg_in{i}")) for i in range(4)]
        kv_in = [ctx.enter_context(nc.semaphore(f"kv_in{i}")) for i in range(8)]
        x_in = [ctx.enter_context(nc.semaphore(f"x_in{i}")) for i in range(2)]
        y_out = [ctx.enter_context(nc.semaphore(f"y_out{i}")) for i in range(2)]

        block = ctx.enter_context(nc.Block())
        UP_ITERS = KF // 2
        SCORE_BANK = [BANK[0], BANK[1], BANK[6], BANK[7]]
        N_STEPS = 4 * (HEADS_A + HEADS_B)

        def raw_slot(u0, j):
            return (u0 + j) % RAW_SLOTS

        def half(t, k, n):
            a, b = HALVES[n]
            return t[:, k, a:b]

        def tr_copies(g):
            bank = BANK[2 + g % 6]
            if g < 6:
                return [(VP[:, :, :].rearrange("p a n -> p (a n)")[:, 512 * g:512 * g + 512], bank[:, :])]
            if g == 6:
                return [(VBT[:, :, :].rearrange("p a n -> p (a n)"), bank[:, :])]
            if g == 7:
                return [(KNEW[:, 0:512], bank[0:32, :])]
            if g == 8:
                return [(KNEW[:, 512:768], bank[0:32, 0:256]), (VNEW[:, 0:256], bank[0:32, 256:512])]
            if g == 9:
                return [(VNEW[:, 256:768], bank[0:32, :])]
            return [(VBN[:, 0:HD], bank[0:32, HD:128]), (VBN[:, HD:128], bank[0:32, HD:128])]

        IDX_FROM, N_PT = 9, 13
        PT_DONE_A = [(9 + 2 * a + 1) // 2 for a in range(3)]
        PT_DONE_D = [(9 + 2 * a) // 2 for a in range(3)]

        def pt_group(i):
            if 2 <= i < 7:
                return "b", i - 2, 0
            j = i if i < 2 else i - 5
            return "a", j // 2, j % 2

        def pt_copies(i):
            which, q, part = pt_group(i)
            bank = BANK[5 + i % 2]
            if which == "b":
                if q == 4:
                    return [(PTB[0:32, 16, :], bank[0:32, 0:128])]
                return [(PTB[:, 4 * q:4 * q + 4, :].rearrange("p g n -> p (g n)"), bank[:, :])]
            if part == 0:
                return [(PTA[:, q % 2, 0:4, :].rearrange("p g n -> p (g n)"), bank[:, :])]
            return [(PTA[:, q % 2, 4:7, :].rearrange("p g n -> p (g n)"), bank[:, 0:384]),
                    (PTA[0:32, q % 2, 7, :], bank[0:32, 384:512])]

        def load_kv_page(eng, q):
            g, b = q // DEC_BATCH, q % DEC_BATCH
            page = eng.value_load(PAGE_IDS[0:1, b * PAGES + g:b * PAGES + g + 1], min_val=0, max_val=cache_b.shape[0] - 1)
            eng.dma_start(KVP[:, q, :], cache_b[bass.ds(page, 1), :, 0:2 * HD].rearrange("o p n -> (o p) n")
                          ).then_inc(kv_in[g // 4 + 4 * (q % 2)], 16)

        @block.sync
        def _(sp):
            def cache_copy(q):
                sp.dma_start(
                    a_sample[:, bass.ds(q * COPY_ROWS, COPY_ROWS), :].rearrange("b r n -> r b n"),
                    cache_a[:, bass.ds(q * COPY_ROWS + DEC_SEQ, COPY_ROWS), :].rearrange("b r n -> r b n"),
                ).then_inc(S["copy_done"], 16)

            def load_unit(name, i, j, free=True):
                u0, n_tiles = FIRST[name], STAGE_TILES[name]
                slot = raw_slot(u0, j)
                if free:
                    sp.wait_ge(S["lo_ready"], u0 + i * 4 + j - 3)
                sp.dma_start(RAW[:, slot, 0:n_tiles, :],
                             w[name][bass.ds(i * 4 + j, 1)].rearrange("o p t n -> (o p) t n")
                             ).then_inc(raw_loaded[slot], 16)

            def load_stage(name, first, iters, copies=0, copy0=0):
                with sp.Fori(first, iters) as i:
                    for j in range(4):
                        load_unit(name, i, j)
                        if j < copies:
                            cache_copy(i * copies + (j + copy0))

            load_unit("wi1", 0, 0, free=False)
            for k in range(0, KD, 4):
                sp.dma_start(Y[:, k:k + 4, :], x_t[:, k:k + 4, :]).then_inc(x_in[k // 4], 16)
            sp.dma_start(RELC[0:32, :], rel_bias).then_inc(S["setup_in"], 16)
            sp.dma_start(RELC[32:34, :], rel_rows).then_inc(S["setup_in"], 16)
            for t in range(4):
                sp.dma_start(RELREP[32 * t:32 * t + 32, :], rel_bias).then_inc(S["setup_in"], 16)
            sp.dma_start(CP[:], consts).then_inc(S["setup_in"], 16)
            sp.dma_start(TP[:], toeplitz).then_inc(S["setup_in"], 16)
            sp.dma_start(OH[:], onehots).then_inc(S["setup_in"], 16)
            sp.dma_start(LNC[:], patterns).then_inc(S["setup_in"], 16)
            sp.dma_start(MNEW[:], mask_new).then_inc(S["setup_in"], 16)
            for j in range(1, 4):
                load_unit("wi1", 0, j, free=False)
            sp.dma_start(LN[:], ln).then_inc(S["ln_in"], 16)
            sp.dma_start(KIDX_GB[:, 0, :], kidx_g.partition_broadcast(128)).then_inc(S["ln_in"], 16)
            sp.dma_start(KIDX_GB[:, 1, :], kidx_b.partition_broadcast(128)).then_inc(S["ln_in"], 16)
            sp.dma_start(PAGE_IDS[:], page_table.rearrange("b g -> (b g)").unsqueeze(0)).then_inc(S["ids_in"], 16)
            sp.wait_ge(S["rev_in"], 1)
            sp.dma_start(REV_DRAM, spread(REV[:], 1, 128)).then_inc(S["rev_out"], 16)
            load_stage("wi1", 1, UP_ITERS, copies=2, copy0=-2)
            load_stage("wo1", 0, 4, copies=3, copy0=20)

            def load_idx_pages(g):
                if g == 0:
                    sp.wait_ge(S["ids_in"], 16)
                    sp.wait_ge(S["x_ready"], 2 * KD)
                if g >= 4:
                    sp.wait_ge(S["kp_t"], g - 3)
                for b in range(DEC_BATCH):
                    page = sp.value_load(PAGE_IDS[0:1, b * PAGES + g:b * PAGES + g + 1],
                                         min_val=0, max_val=cache_b.shape[0] - 1)
                    sp.dma_start(PG[:, g % 4, b, :],
                                 cache_b[bass.ds(page, 1), :, 2 * HD:3 * HD].rearrange("o p n -> (o p) n")
                                 ).then_inc(pg_in[g % 4], 16)

            for c in range(N_PROJ):
                load_unit("w_in", c // 4, c % 4)
                if 4 <= c < 8:
                    load_idx_pages(c - 4)
                elif 11 <= c < 7 + PAGES:
                    load_idx_pages(c - 7)
                if c == 3:
                    for q in range(32, 36):
                        cache_copy(q)
                elif 8 <= c < 11:
                    cache_copy(28 + c)
            sp.dma_start(ki_b, KIN[:, :, 0:HD]).then_inc(S["proj_out"], 16)
            sp.wait_ge(S["proj_a"], N_PROJ)
            sp.wait_ge(S["proj_d"], N_PROJ)
            sp.dma_start(kv_a_t.rearrange("c p n -> p c n"), PROJ[:, C_KA:C_KA + 12, 0:SEQ]).then_inc(S["proj_out"], 16)
            sp.dma_start(kv_b_t, PROJ[:, C_KV, :]).then_inc(S["proj_out"], 16)

            def load_rows(n, kv, b, k):
                if n >= 4:
                    if n - 4 < 56:
                        sp.wait_ge(S["ka_t"], n - 3)
                    else:
                        sp.wait_ge(S["va_used"], n - 3 - 56)
                cols = slice(kv * WIDTH_A, (kv + 1) * WIDTH_A)
                if k < STRIDED_BLOCKS:
                    src = cache_a[b, 512 * k:512 * k + 512, cols].rearrange("(j r) n -> j r n", r=16)[:, 0:4, :]
                else:
                    r0 = PAST - 512 + 128 * (k - STRIDED_BLOCKS)
                    src = cache_a[b, r0:r0 + 128, cols]
                sp.dma_start(AR[:, n % 4, :], src).then_inc(ar_in[n % 4], 16)

            for n in range(4):
                load_rows(n, 0, n // 7, n % 7)
            sp.wait_ge(S["lo_ready"], FIRST["w_out"])
            sp.dma_start(OHB[:], onehots[:, KEY_BLOCKS_A:24, :]).then_inc(S["oh_in"], 16)
            sp.wait_ge(S["tr_a"], 6)
            sp.wait_ge(S["tr_d"], 5)
            for b in range(DEC_BATCH):
                for kv, t in ((0, KNEW), (1, VNEW)):
                    sp.dma_start(a_sample[b, PAST - DEC_SEQ:PAST, kv * WIDTH_A:(kv + 1) * WIDTH_A],
                                 t[4 * b:4 * b + 4, :]).then_inc(S["new_rows_out"], 16)
            sp.wait_ge(S["proj_out"], 48)
            sp.wait_ge(S["new_rows_out"], 16 * 2 * DEC_BATCH)
            sp.wait_ge(S["o_sb"], 8)
            sp.dma_start(VN2[:], a_sample[:, PAST - DEC_SEQ:PAST, WIDTH_A:2 * WIDTH_A]).then_inc(S["vnew_in"], 16)
            page_at = 0
            for n in range(4, 56):
                load_rows(n, 0, n // 7, n % 7)
                while page_at < min(64, (5 * (n - 3) + 3) // 4):
                    load_kv_page(sp, 2 * page_at)
                    page_at += 1
            for n in range(4):
                load_rows(56 + n, 1, n // 7, n % 7)
            sp.wait_ge(S["b_logits"], 1)
            for j in (2, 3):
                load_unit("w_out", 0, j, free=False)
            sp.wait_ge(S["vb_all"], 1)
            for j in (0, 1):
                load_unit("w_out", 0, j, free=False)
            for n in range(4, 56):
                load_rows(56 + n, 1, n // 7, n % 7)

            for j in range(4):
                load_unit("w_out", 1, j)
            load_stage("wi2", 0, UP_ITERS, copies=2, copy0=39)
            sp.dma_start(P_RAW[:], p_t).then_inc(S["p_in"], 16)
            load_stage("wo2", 0, 4, copies=3, copy0=61)
            load_stage("gate", 0, 2)
            for m in range(KD):
                sp.wait_ge(S["y_final"], m + 1)
                sp.dma_start(y_t[m], HF[:, m % 2, :]).then_inc(y_out[m % 2], 16)
            for s in y_out:
                sp.wait_ge(s, 16 * KD // 2)
            sp.wait_ge(S["proj_out"], 48)
            sp.wait_ge(S["new_rows_out"], 16 * 2 * DEC_BATCH)
            sp.wait_ge(S["copy_done"], 16 * N_COPIES)

        @block.gpsimd
        def _(pool):
            def rest(name, i, j):
                u0, tiles = FIRST[name], STAGE_TILES[name]
                slot, s = raw_slot(u0, j), (u0 + j) % 2
                pool.wait_ge(S["hi_ready"], u0 + i * 4 + j + 1)
                nc.gpsimd.tensor_tensor(WL[:, s, 0:tiles, :], RAW[:, slot, 0:tiles, :],
                                        WH[:, s, 0:tiles, :].bitcast(F32), ALU.subtract
                                        ).then_inc(S["lo_ready"], 1)

            def rests(name, first, iters):
                with pool.Fori(first, iters) as i:
                    for j in range(4):
                        rest(name, i, j)

            def x_rest(k, new):
                nc.gpsimd.tensor_tensor(XL[:, k, :], new, XH[:, k, :].bitcast(F32), ALU.subtract
                                        ).then_inc(S["x_ready"], 1)

            def ln_rest(which, nxt):
                for j in range(2):
                    rest(nxt, 0, j)
                for m in range(KD):
                    pool.wait_ge(S["xh_ln"], KD * which + m + 1)
                    pool.wait_ge(S["xn_done"], KD * which + m + 1)
                    x_rest(m, XN[:, m % 2, :])
                for j in range(2, 4):
                    rest(nxt, 0, j)

            nc.gpsimd.memset(ONES[:], 1.0 / D_MODEL).then_inc(S["ones_done"], 1)
            for k in range(KD):
                pool.wait_ge(S["xh_ready"], k + 1)
                x_rest(k, Y[:, k, :])
            rests("wi1", 0, UP_ITERS)
            rests("wo1", 0, 4)
            ln_rest(0, "w_in")
            def causal():
                for i in range(1, QB_BLOCKS):
                    pool.wait_ge(S["ix_acc"], IDX_HEADS * i)
                    d = MSK[:, i - 1, 128 * i:128 * i + 128]
                    nc.gpsimd.affine_select(out=d, in_=d, compare_op=ALU.is_ge, fill=NEG, base=0,
                                            pattern=[[-1, 128]], channel_multiplier=1
                                            ).then_inc(S["ix_causal"], 1)

            for c in range(4, N_PROJ):
                rest("w_in", c // 4, c % 4)
                if c == 18:
                    causal()

            pool.wait_ge(S["rev_out"], 16)
            for h in range(HEADS_A + HEADS_B):
                if h >= 2:
                    pool.wait_ge(S["logits_done"], 4 * (h - 1))
                row = bass.AP(REV_DRAM.tensor, 640 * 128 * h + 127, [[639, 128], [1, SEQ]])
                pool.dma_start(TOE[:, h % 2, :], row).then_inc(toe_in[h % 2], 16)
                if h >= HEADS_A:
                    if h == HEADS_A:
                        pool.wait_ge(S["topk_prompt_done"], 1)
                        pool.wait_ge(S["proj_out"], 48)
                    pool.wait_ge(toe_in[h % 2], 16 * (h // 2 + 1))
                    for i in range(1, QB_BLOCKS):
                        n = 3 * (h - HEADS_A) + i - 1
                        if n >= 2:
                            hh, ii = HEADS_A + (n - 2) // 3, (n - 2) % 3 + 1
                            pool.wait_ge(S["logits_done"], 4 * hh + ii + 1)
                        nk = 128 * (i + 1)
                        nc.gpsimd.tensor_tensor(TM[:, n % 2, 0:nk], TOE[:, h % 2, SEQ - nk:SEQ],
                                                MSK[:, i - 1, 0:nk], ALU.add).then_inc(S["tm_done"], 1)

            pool.wait_ge(S["ids_in"], 16)
            pool.wait_ge(S["proj_out"], 48)
            pool.wait_ge(S["o_sb"], 8)
            for q in range(1, DEC_BATCH * PAGES, 2):
                load_kv_page(pool, q)
            pool.wait_ge(S["ka_sc"], 56)
            for g in range(PAGES):
                if g % 4 == 0:
                    for queue in range(2):
                        pool.wait_ge(kv_in[g // 4 + 4 * queue], 16 * 2 * DEC_BATCH)
                if g >= 2:
                    pool.wait_ge(S["kb_t"], g - 1)
                nc.gpsimd.tensor_copy(KC[:, g % 2, :, :], KVP[:, DEC_BATCH * g:DEC_BATCH * g + DEC_BATCH, 0:HD]
                                      ).then_inc(S["kc_ready"], 1)

            for c in range(KD):
                pool.wait_ge(S["oh_ready"], c + 1)
                nc.gpsimd.tensor_tensor(OL_[:, c, 0:SEQ], OT[:, c, 0:SEQ], OH_[:, c, 0:SEQ].bitcast(F32), ALU.subtract
                                        ).then_inc(S["o_ready"], 1)
            pool.wait_ge(S["o_tail"], 1)
            nc.gpsimd.tensor_tensor(OL_[:, :, SEQ:T], OT[:, :, SEQ:T], OH_[:, :, SEQ:T].bitcast(F32), ALU.subtract
                                    ).then_inc(S["o_ready"], 1)
            rests("w_out", 0, 2)
            ln_rest(1, "wi2")
            rests("wi2", 1, UP_ITERS)
            rests("wo2", 0, 4)
            ln_rest(2, "gate")
            rests("gate", 1, 2)

        @block.scalar
        def _(act):
            def high(u0, i, j, tiles):
                slot, s = raw_slot(u0, j), (u0 + j) % 2
                act.wait_ge(raw_loaded[slot], (i + (u0 + j) // 4) * 16 + 16)
                if not (isinstance(i, int) and u0 + 4 * i + j < 2):
                    act.wait_ge(S["unit_used"], u0 + i * 4 + j - 1)
                nc.scalar.activation(WH[:, s, 0:tiles, :], RAW[:, slot, 0:tiles, :], ACT.Copy
                                     ).then_inc(S["hi_ready"], 1)

            def high_of(u):
                high(u % 4, u // 4, 0, tiles_of(u))

            def up_stage(which):
                name = ("wi1", "wi2")[which]
                u0 = FIRST[name]

                def pair(i, split):
                    for s in range(2):
                        for j in (2 * s + 2, 2 * s + 3):
                            split(i, j)
                        if not (isinstance(i, int) and i == 0 and which == 0):
                            act.wait_ge(S["h_done"], 22 * which + i * 2 + s - 1)
                        act.wait_ge(S["unit_used"], u0 + i * 4 + 2 * s + 1)
                        for n in range(2):
                            last = nc.scalar.activation(half(SG, s, n), BANK[4 * s + n][:, 0:HALF], ACT.Silu)
                        last.then_inc(S["silu_done"], 1)

                pair(0, lambda i, j: high(u0, i, j, 8))
                with act.Fori(1, UP_ITERS - 1) as i:
                    pair(i, lambda i, j: high(u0, i, j, 8))
                pair(UP_ITERS - 1, lambda i, j: high_of(u0 + 4 * i + j))

            def layer_norm(which):
                act.wait_ge(S["mean_ps"], which + 1)
                for n, (a, b) in enumerate(HALVES):
                    last = nc.scalar.activation(MEAN[:, a:b], BANK[4 + n][:, 0:HALF], ACT.Copy)
                last.then_inc(S["mean_sb"], 1)
                for m in range(KD):
                    act.wait_ge(S["centred"], KD * which + m + 1)
                    if m >= 2 or which:
                        act.wait_ge(S["sq_used"], KD * which + m - 1)
                    nc.scalar.activation(SQ[:, m % 2, :], Y[:, m, :], ACT.Square).then_inc(S["squared"], 1)
                act.wait_ge(S["var_sb"], which + 1)
                nc.scalar.activation(RSTD[:], RSTD[:], ACT.Sqrt).then_inc(S["std_sb"], 1)
                if which == 0:
                    act.wait_ge(S["ln_in"], 48)
                for m in range(KD):
                    act.wait_ge(S["zed"], KD * which + m + 1)
                    g, b = LN[:, 2 * which, m:m + 1], LN[:, 2 * which + 1, m:m + 1]
                    nc.scalar.activation(XH[:, m, :], Y[:, m, :], ACT.Identity, bias=b, scale=g
                                         ).then_inc(S["xh_ln"], 1)

            high_of(0)
            high_of(1)
            up_stage(0)
            for m in range(KD):
                high_of(FIRST["wo1"] + 2 * m + 2)
                high_of(FIRST["wo1"] + 2 * m + 3)
            layer_norm(0)

            def project(c):
                u0 = FIRST["w_in"]
                if c + 2 < N_PROJ:
                    high(u0, (c + 2) // 4, (c + 2) % 4, 8)
                act.wait_ge(S["unit_used"], u0 + c + 1)
                nc.scalar.activation(PROJ[:, c, 0:HALF], BANK[2 * (c % 2)][:, 0:HALF], ACT.Copy,
                                     scale=HD ** -0.5 if c >= C_QA else 1.0).then_inc(S["proj_a"], 1)

            def relu_prompt(n):
                nk = 128 * (n // IDX_HEADS + 2)
                act.wait_ge(S["ix_ps"], n + 1)
                if n >= 2:
                    act.wait_ge(S["ix_acc"], n - 1)
                nc.scalar.activation(RL[:, n % 2, 0:nk], BANK[5][:, 0:nk], ACT.Relu).then_inc(S["ix_relu"], 1)

            def relu_dec(g):
                act.wait_ge(S["kp_sc"], g + 1)
                if g >= 2:
                    act.wait_ge(S["kp_sum"], g - 1)
                nk = 128 if g < PAGES else NDEC
                src = BANK[6][:, 0:256].rearrange("p (a k) -> p a k", a=2)[:, :, 0:nk]
                nc.scalar.activation(RLD[:, g % 2, :, 0:nk], src, ACT.Relu).then_inc(S["kp_relu"], 1)

            for c in range(7):
                project(c)
            act.wait_ge(S["ki_var"], 1)
            nc.scalar.activation(SMALL[:, 10:15], SMALL[:, 10:15], ACT.Sqrt).then_inc(S["ki_std"], 1)
            for c in range(7, IDX_FROM):
                project(c)
            act.wait_ge(S["kit_ps"], 1)
            nc.scalar.activation(KIT[:, 0:SEQ], BANK[5][:, 0:SEQ], ACT.Copy)
            nc.scalar.activation(KIT[:, SEQ:T], BANK[6][:, 0:32], ACT.Copy).then_inc(S["kit_sb"], 1)
            for s in range(PAGES + 3):
                if s < PAGES:
                    act.wait_ge(S["kp_t"], s + 1)
                    if s >= 2:
                        act.wait_ge(S["kp_sc"], s - 1)
                    nc.scalar.activation(KIPT[:, s % 2, :, :].rearrange("p a k -> p (a k)"), BANK[4][:, :],
                                         ACT.Copy).then_inc(S["kp_sb"], 1)
                if s < 8:
                    relu_prompt(3 * s)
                if 1 <= s < PAGES + 2:
                    relu_dec(s - 1)
                if s < 8:
                    relu_prompt(3 * s + 1)
                    relu_prompt(3 * s + 2)
                if IDX_FROM + s < N_PROJ:
                    project(IDX_FROM + s)
            for g in range(0, 11, 2):
                act.wait_ge(S["tr_ps"], g + 1)
                for dst, src in tr_copies(g):
                    last = nc.scalar.activation(dst, src, ACT.Copy)
                last.then_inc(S["tr_a"], 1)

            for n in range(N_STEPS + 2):
                if n < N_STEPS:
                    nk = 128 * (n % 4 + 1)
                    act.wait_ge(S["logits_done"], n + 1)
                    l = LP[:, n % 3, 0:nk]
                    nc.scalar.activation(l, l, ACT.Exp, bias=SMALL[:, 32 + n % 4:33 + n % 4], scale=-1.0,
                                         accum_out=SMALL[:, 36 + n % 4:37 + n % 4]).then_inc(S["exp_done"], 1)
                if n >= 2:
                    k = n - 2
                    nk = 128 * (k % 4 + 1)
                    act.wait_ge(S["pt_ps"], k + 1)
                    if k >= 2:
                        act.wait_ge(S["pv_done"], k - 1)
                    nc.scalar.activation(PTS[:, k % 2, 0:nk], BANK[2 + k % 2][:, 0:nk], ACT.Copy
                                         ).then_inc(S["pt_sb"], 1)

            def exp_a(a):
                act.wait_ge(S["ka_logits"], a + 1)
                nc.scalar.activation(STA[:, a, :], STA[:, a, :], ACT.Exp, bias=SMALL[:, SM_MIN + a:SM_MIN + a + 1],
                                     scale=-1.0, accum_out=SMALL[:, SM_DEN + a:SM_DEN + a + 1]
                                     ).then_inc(S["expa_done"], 1)

            for n in range(56):
                act.wait_ge(S["ka_t"], n + 1)
                if n >= 2:
                    act.wait_ge(S["ka_sc"], n - 1)
                b0 = 2 * (n % 2)
                nc.scalar.activation(KTA[:, n % 2, 0:512], BANK[b0][:, :], ACT.Copy)
                nc.scalar.activation(KTA[:, n % 2, 512:768], BANK[b0 + 1][:, 0:256], ACT.Copy
                                     ).then_inc(S["ka_sb"], 1)
                if n >= 20 and (n - 20) % 14 == 0:
                    exp_a((n - 20) // 14)
            for g in range(PAGES):
                act.wait_ge(S["kb_t"], g + 1)
                if g >= 2:
                    act.wait_ge(S["kb_sc"], g - 1)
                nc.scalar.activation(KTB[:, g % 2, :], BANK[5 + g % 2][:, :], ACT.Copy).then_inc(S["kb_sb"], 1)
                if g == 2:
                    exp_a(3)
            act.wait_ge(S["b_max"], 1)
            for j in range(5):
                nk = 512 if j < 4 else NDEC
                last = nc.scalar.activation(STB[:, 512 * j:512 * j + nk], BANK[j][:, 0:nk], ACT.Exp,
                                            bias=SMALL[:, SM_BMAX + 5:SM_BMAX + 6], scale=1.0,
                                            accum_out=SMALL[:, SM_BSUM + j:SM_BSUM + j + 1])
            last.then_inc(S["b_exp"], 1)
            for i in range(0, N_PT, 2):
                act.wait_ge(S["pt_ps2"], i + 1)
                for dst, src in pt_copies(i):
                    last = nc.scalar.activation(dst, src, ACT.Copy)
                last.then_inc(S["pt_a"], 1)

            act.wait_ge(S["va_pair"], 4)
            act.wait_ge(S["vb_all"], 1)
            for j in range(2):
                high_of(FIRST["w_out"] + j)
            for m in range(KD):
                high_of(FIRST["w_out"] + m + 2)
            layer_norm(1)
            up_stage(1)
            for m in range(KD):
                high_of(FIRST["wo2"] + 2 * m + 2)
                high_of(FIRST["wo2"] + 2 * m + 3)
            layer_norm(2)
            for m in range(KD):
                if m < KD - 2:
                    high_of(FIRST["gate"] + m + 2)
                s = m % 2
                act.wait_ge(S["unit_used"], FIRST["gate"] + m + 1)
                if m >= 2:
                    act.wait_ge(S["y_final"], m - 1)
                for n in range(2):
                    last = nc.scalar.activation(half(SG, s, n), BANK[4 * s + n][:, 0:HALF], ACT.Sigmoid)
                last.then_inc(S["gate_sig"], 1)

        @block.vector
        def _(dve):
            own = Steps(dve, S["dve_step"])
            v = nc.vector

            for k in range(KD):
                if k % 4 == 0:
                    dve.wait_ge(x_in[k // 4], 16)
                v.tensor_copy(XH[:, k, :], Y[:, k, :]).then_inc(S["xh_ready"], 1)
            v.memset(RELA[:], 0.0)
            own.done(v.memset(RELB[:], 0.0))
            dve.wait_ge(S["setup_in"], 16 * 11)
            for t in range(4):
                rel = RELREP[32 * t:32 * t + 32, :]
                v.tensor_copy(RELA[32 * t:32 * t + 32, :, 0:HEADS_A, t], spread(rel[:, 0:HEADS_A], 1, 2))
                last = v.tensor_copy(RELB[32 * t:32 * t + 32, :, :, t], spread(rel[:, HEADS_A:16], 1, DEC_BATCH))
            last.then_inc(S["relt_done"], 1)
            dve.wait_ge(S["tables_ps"], 1)
            v.tensor_copy(REV[:, 0:512], BANK[3][0:16, :])
            v.tensor_copy(REV[:, 512:640], BANK[4][0:16, 0:128]).then_inc(S["rev_in"], 1)
            v.tensor_copy(BIAS_A[:, 0:512], BANK[0][:, :])
            v.tensor_copy(BIAS_A[:, 512:KEYS_A], BANK[1][:, 0:KEYS_A - 512])
            own.done(v.tensor_tensor(BIAS_N[:], spread(BANK[2][:, 0:32], 1, 4), MNEW[:], ALU.add))
            dve.wait_ge(S["rev_out"], 16)

            def up_stage(which):
                u0 = FIRST[("wi1", "wi2")[which]]
                with dve.Fori(0, UP_ITERS) as i:
                    for s in range(2):
                        done = i * 2 + (22 * which + s + 1)
                        c = i * 2 + s
                        dve.wait_ge(S["silu_done"], done)
                        dve.wait_ge(S["unit_used"], u0 + i * 4 + 2 * s + 2)
                        for n in range(2):
                            last = v.scalar_tensor_tensor(half(HF, s, n), half(SG, s, n), 0.5,
                                                          BANK[4 * s + 2 + n][:, 0:HALF], ALU.mult, ALU.mult)
                        last.then_inc(S["h_done"], 1)
                        dve.wait_ge(S["h_done"], done)
                        v.tensor_copy(HH[:, bass.ds(c, 1), :], HF[:, s:s + 1, :]).then_inc(S["hh_done"], 1)
                        dve.wait_ge(S["hh_done"], done)
                        v.tensor_tensor(HL[:, bass.ds(c, 1), :], HF[:, s:s + 1, :],
                                        HH[:, bass.ds(c, 1), :].bitcast(F32), ALU.subtract
                                        ).then_inc(S["hl_done"], 1)

            def down_stage(which):
                name = ("wo1", "w_out", "wo2")[which]
                u0, per = FIRST[name], (2, 1, 2)[which]
                own.done(v.memset(SUM[:], 0.0))
                with dve.Fori(0, KD // 2) as i:
                    for s in range(2):
                        done = i * 2 + (KD * which + s + 1)
                        m = i * 2 + s
                        dve.wait_ge(S["unit_used"], u0 + i * (2 * per) + per * (s + 1))
                        for n, (a, b) in enumerate(HALVES):
                            last = v.scalar_tensor_tensor(
                                Y[:, bass.ds(m, 1), a:b], XH[:, bass.ds(m, 1), a:b].bitcast(F32), ALPHA,
                                BANK[2 * s + n][:, 0:HALF].unsqueeze(1), ALU.mult, ALU.add)
                        last.then_inc(S["y_part"], 1)
                        dve.wait_ge(S["y_part"], done)
                        v.scalar_tensor_tensor(Y[:, bass.ds(m, 1), :], XL[:, bass.ds(m, 1), :].bitcast(F32), ALPHA,
                                               Y[:, bass.ds(m, 1), :], ALU.mult, ALU.add).then_inc(S["y_full"], 1)
                        dve.wait_ge(S["y_full"], done)
                        v.tensor_tensor(SUM[:].unsqueeze(1), SUM[:].unsqueeze(1), Y[:, bass.ds(m, 1), :], ALU.add
                                        ).then_inc(S["sum_done"], 1)
                        dve.wait_ge(S["sum_done"], done)

            def layer_norm(which):
                dve.wait_ge(S["mean_sb"], which + 1)
                for m in range(KD):
                    v.tensor_tensor(Y[:, m, :], Y[:, m, :], MEAN[:], ALU.subtract).then_inc(S["centred"], 1)
                dve.wait_ge(S["sq_used"], KD * (which + 1))
                for n, (a, b) in enumerate(HALVES):
                    last = v.tensor_scalar_add(RSTD[:, a:b], BANK[6 + n][:, 0:HALF], LN_EPS)
                last.then_inc(S["var_sb"], 1)
                dve.wait_ge(S["std_sb"], which + 1)
                own.done(v.reciprocal(RSTD[:], RSTD[:]))
                if which == 0:
                    dve.wait_ge(S["ln_in"], 48)
                for m in range(KD + 1):
                    if m < KD:
                        v.tensor_tensor(Y[:, m, :], Y[:, m, :], RSTD[:], ALU.mult).then_inc(S["zed"], 1)
                    if m >= 1:
                        k = m - 1
                        dve.wait_ge(S["zed"], KD * which + k + 1)
                        if k >= 2 or which:
                            dve.wait_ge(S["x_ready"], KD * (which + 1) + k - 1)
                        g, b = LN[:, 2 * which, k:k + 1], LN[:, 2 * which + 1, k:k + 1]
                        v.tensor_scalar(XN[:, k % 2, :], Y[:, k, :], g, b, ALU.mult, ALU.add).then_inc(S["xn_done"], 1)

            up_stage(0)
            down_stage(0)
            layer_norm(0)

            def project(c):
                dve.wait_ge(S["unit_used"], FIRST["w_in"] + c + 1)
                v.tensor_scalar_mul(PROJ[:, c, HALF:T], BANK[2 * (c % 2) + 1][:, 0:HALF],
                                    HD ** -0.5 if c >= C_QA else 1.0).then_inc(S["proj_d"], 1)

            for c in range(7):
                project(c)
            own.done(v.memset(KI0[:], 0.0))
            dve.wait_ge(S["kiw_ps"], 1)
            v.tensor_copy(KI0[:, 0:4, :].rearrange("p a n -> p (a n)"), BANK[4][:, 0:288])
            own.done(v.tensor_copy(KI0[0:32, 4, :], BANK[4][0:32, 288:360]))
            for k in range(5):
                last = v.bn_stats(SMALL[:, 16 + 6 * k:22 + 6 * k], KI0[:, k, 0:HD])
            own.done(last)
            for k in range(5):
                last = v.bn_aggr(SMALL[:, 2 * k:2 * k + 2], SMALL[:, 16 + 6 * k:22 + 6 * k])
            own.done(last)
            v.tensor_scalar_add(SMALL[:, 10:15], SMALL[:, 1:10:2], LN_EPS).then_inc(S["ki_var"], 1)
            dve.wait_ge(S["ki_std"], 1)
            own.done(v.reciprocal(SMALL[:, 10:15], SMALL[:, 10:15]))
            for k in range(5):
                last = v.tensor_scalar(KIN[:, k, 0:HD], KI0[:, k, 0:HD], SMALL[:, 2 * k:2 * k + 1],
                                       SMALL[:, 10 + k:11 + k], ALU.subtract, ALU.mult)
            own.done(last)
            own.done(v.tensor_tensor(KIN[:, :, 0:HD], KIN[:, :, 0:HD], spread(KIDX_GB[:, 0, :], 1, 5), ALU.mult))
            own.done(v.tensor_tensor(KIN[:, :, 0:HD], KIN[:, :, 0:HD], spread(KIDX_GB[:, 1, :], 1, 5), ALU.add))
            v.tensor_copy(KIN[:, :, HD:128], KIN[:, :, 0:HD]).then_inc(S["kin_done"], 1)
            own.done(v.tensor_scalar_mul(KI0[:, :, HD:HD + 8], KI0[:, :, HD:HD + 8], IDX_SCALE))
            own.done(v.memset(QIB[:], 0.0))
            for h2 in range(2):
                lo = slice(64 * h2, 64 * h2 + 64)
                for b2 in range(2):
                    up = slice(64 * b2, 64 * b2 + 64)
                    qi = PROJ[lo, C_QI:C_QI + 4, SEQ:T].rearrange("p c (a b t) -> p a c b t", b=2, t=4)[:, :, :, b2, :]
                    last = v.tensor_copy(QIB[up, :, :].rearrange("p a (b c h t) -> p a b c h t", b=2, c=4, h=2)
                                         [:, :, b2, :, h2, :], qi)
            last.then_inc(S["qblocks_done"], 1)
            for c in range(7, IDX_FROM):
                project(c)
            dve.wait_ge(S["wsel_ps"], 1)
            v.tensor_tensor(WB[:], spread(BANK[7][:, 0:32], 1, 2), WMASK, ALU.mult).then_inc(S["wsel_done"], 1)

            def index_sum(n):
                i, h = n // IDX_HEADS + 1, n % IDX_HEADS
                nk = 128 * (i + 1)
                dve.wait_ge(S["ix_relu"], n + 1)
                weight = KI0[:, i, HD + h:HD + h + 1]
                if h == 0:
                    last = v.tensor_scalar_mul(MSK[:, i - 1, 0:nk], RL[:, n % 2, 0:nk], weight)
                else:
                    dve.wait_ge(S["ix_acc"], n)
                    last = v.scalar_tensor_tensor(MSK[:, i - 1, 0:nk], RL[:, n % 2, 0:nk], weight,
                                                  MSK[:, i - 1, 0:nk], ALU.mult, ALU.add)
                last.then_inc(S["ix_acc"], 1)

            def index_row(g):
                dve.wait_ge(S["kp_sum"], g + 1)
                if g < PAGES:
                    last = v.tensor_copy(SC[:, 128 * g:128 * g + 128], BANK[7][0:32, 0:128])
                else:
                    last = v.tensor_tensor(SC[:, PAST:PAST + NDEC], BANK[7][0:32, 0:NDEC], MASK_NEW_IX, ALU.add)
                last.then_inc(S["kp_row"], 1)

            def take_eight(scores, top):
                own.done(v.max(top, scores))
                own.done(v.match_replace(scores, top, scores, TAKEN))

            def taken_to_mask(scores):
                return v.tensor_scalar(scores, scores, TAKEN_LIMIT, NEG, ALU.is_ge, ALU.mult)

            def prompt_round(n):
                b = n % 3
                take_eight(MSK[:, b, 0:128 * (b + 2)], SMALL[:, 16:24])
                if n == 3 * TOPK_PROMPT // 8 - 1:
                    for b in range(3):
                        last = taken_to_mask(MSK[:, b, 0:128 * (b + 2)])
                    last.then_inc(S["topk_prompt_done"], 1)

            rounds = 0
            for s in range(PAGES + 3):
                if s < 8:
                    for n in range(3 * s, 3 * s + 3):
                        index_sum(n)
                if s >= 2:
                    index_row(s - 2)
                if IDX_FROM + s < N_PROJ:
                    project(IDX_FROM + s)
                if s == 8:
                    dve.wait_ge(S["ix_causal"], 3)
                if s >= 8:
                    for _ in range(3):
                        prompt_round(rounds)
                        rounds += 1
            for g in range(1, 11, 2):
                dve.wait_ge(S["tr_ps"], g + 1)
                for dst, src in tr_copies(g):
                    last = v.tensor_copy(dst, src)
                last.then_inc(S["tr_d"], 1)
            v.tensor_copy(KB2[0:64, SEQ:T], PROJ[0:64, C_KV, SEQ:T])
            v.tensor_copy(KB2[64:128, :], PROJ[0:64, C_KV, :]).then_inc(S["kb2_done"], 1)

            def decode_queries():
                dve.wait_ge(S["lo_ready"], FIRST["w_out"])
                v.memset(QBLKA[:], 0.0)
                own.done(v.memset(QBLKB[:], 0.0))
                v.tensor_copy(KNT[:], PROJ[:, C_KA:C_KA + 6, SEQ:T])
                for h2 in range(2):
                    lo = slice(64 * h2, 64 * h2 + 64)
                    for c in range(6):
                        col = 8 * c + 4 * h2
                        v.tensor_copy(QBLKA[lo, c, 0:384].rearrange("p (b r) -> p b r", b=DEC_BATCH)[:, :, col:col + 4],
                                      PROJ[lo, C_QA + c, SEQ:T].rearrange("p (b t) -> p b t", t=4))
                    for b2 in range(2):
                        up = slice(64 * b2, 64 * b2 + 64)
                        qb = PROJ[lo, C_QB:C_QB + 2, SEQ:T].rearrange("p c (a b t) -> p a c b t", b=2, t=4)[:, :, :, b2, :]
                        last = v.tensor_copy(QBLKB[up, :, :].rearrange("p a (b c h t) -> p a b c h t", b=2, c=2, h=2)
                                             [:, :, b2, :, h2, :], qb)
                last.then_inc(S["qblocks_done"], 1)

            def normalise(n):
                dve.wait_ge(S["exp_done"], n + 1)
                c = n % 4
                own.done(v.reciprocal(SMALL[:, 40 + c:41 + c], SMALL[:, 36 + c:37 + c]))
                l = LP[:, n % 3, 0:128 * (c + 1)]
                v.tensor_scalar_mul(l, l, SMALL[:, 40 + c:41 + c]).then_inc(S["probs_done"], 1)

            def take_out(q):
                dve.wait_ge(S["pv_done"], 8 * q + 8)
                v.tensor_copy(OT[:, q, 0:SEQ], BANK[4 + q % 2][:, :]).then_inc(S["o_sb"], 1)

            dve.wait_ge(S["new_rows_out"], 16 * 2 * DEC_BATCH)
            dec_rounds = 0
            for n in range(N_STEPS):
                h, i = n // 4, n % 4
                nk = 128 * (i + 1)
                dve.wait_ge(S["sc_ps"], n + 1)
                if n >= 3:
                    dve.wait_ge(S["pt_ps"], n - 2)
                if h < HEADS_A or i == 0:
                    dve.wait_ge(toe_in[h % 2], 16 * (h // 2 + 1))
                    bias = TOE[:, h % 2, SEQ - nk:SEQ]
                else:
                    t = 3 * (h - HEADS_A) + i - 1
                    dve.wait_ge(S["tm_done"], t + 1)
                    bias = TM[:, t % 2, 0:nk]
                v.tensor_tensor_reduce(out=LP[:, n % 3, 0:nk], in0=SCORE_BANK[n % 4][:, 0:nk], in1=bias, scale=-1.0,
                                       scalar=3.0e38, op0=ALU.add, op1=ALU.min,
                                       accum_out=SMALL[:, 32 + i:33 + i]).then_inc(S["logits_done"], 1)
                if n >= 1:
                    normalise(n - 1)
                if n >= 11 and (n - 11) % 8 == 0:
                    take_out((n - 11) // 8)
                if rounds < 48:
                    prompt_round(rounds)
                    rounds += 1
                elif n % 5 == 0:
                    take_eight(SC[:], SMALL[0:32, 24:32])
                    dec_rounds += 1
                if n == 20:
                    decode_queries()
            normalise(N_STEPS - 1)
            take_out(7)

            for a in range(4):
                while dec_rounds < TOPK_DEC // 8 - 5 * (3 - a):
                    take_eight(SC[:], SMALL[0:32, 24:32])
                    dec_rounds += 1
                if a == 3:
                    taken_to_mask(SC[:]).then_inc(S["topk_dec_done"], 1)
                dve.wait_ge(S["ka_sc"], 14 * (a + 1))
                lo_bank, hi_bank = BANK[4 + 2 * (a % 2)], BANK[5 + 2 * (a % 2)]
                for j, (src, bias, c0, c1) in enumerate((
                        (lo_bank[:, :], BIAS_A[:, 0:512], 0, 512),
                        (hi_bank[:, 0:384], BIAS_A[:, 512:KEYS_A], 512, KEYS_A),
                        (hi_bank[:, 384:416], BIAS_N[:, a, :], KEYS_A, ALL_A))):
                    last = v.tensor_tensor_reduce(out=STA[:, a, c0:c1], in0=src, in1=bias, scale=-1.0,
                                                  scalar=3.0e38, op0=ALU.add, op1=ALU.min,
                                                  accum_out=SMALL[:, SM_MINS + 3 * a + j:SM_MINS + 3 * a + j + 1])
                own.done(last)
                v.tensor_reduce(SMALL[:, SM_MIN + a:SM_MIN + a + 1], SMALL[:, SM_MINS + 3 * a:SM_MINS + 3 * a + 3],
                                AX.X, ALU.min).then_inc(S["ka_logits"], 1)
            dve.wait_ge(S["expa_done"], 4)
            own.done(v.reciprocal(SMALL[:, SM_DEN:SM_DEN + 4], SMALL[:, SM_DEN:SM_DEN + 4]))
            dve.wait_ge(S["b_logits"], 1)
            for j in range(5):
                nk = 512 if j < 4 else NDEC
                last = v.tensor_reduce(SMALL[:, SM_BMAX + j:SM_BMAX + j + 1], BANK[j][:, 0:nk], AX.X, ALU.max)
            own.done(last)
            own.done(v.tensor_reduce(SMALL[:, SM_BMAX + 5:SM_BMAX + 6], SMALL[:, SM_BMAX:SM_BMAX + 5], AX.X, ALU.max))
            v.tensor_scalar_mul(SMALL[:, SM_BMAX + 5:SM_BMAX + 6], SMALL[:, SM_BMAX + 5:SM_BMAX + 6], -1.0
                                ).then_inc(S["b_max"], 1)
            dve.wait_ge(S["b_exp"], 1)
            own.done(v.tensor_reduce(SMALL[:, SM_BMAX:SM_BMAX + 1], SMALL[:, SM_BSUM:SM_BSUM + 5], AX.X, ALU.add))
            own.done(v.reciprocal(SMALL[:, SM_BMAX:SM_BMAX + 1], SMALL[:, SM_BMAX:SM_BMAX + 1]))

            def pt_out(i):
                dve.wait_ge(S["pt_ps2"], i + 1)
                for dst, src in pt_copies(i):
                    last = v.tensor_copy(dst, src)
                last.then_inc(S["pt_d"], 1)

            for i in (1, 3, 5):
                pt_out(i)
            dve.wait_ge(S["vb_all"], 1)
            v.tensor_scalar_mul(OB[:], BANK[7][:, 0:128], SMALL[:, SM_BMAX:SM_BMAX + 1]).then_inc(S["ob_sb"], 1)
            dve.wait_ge(S["ob_t"], 1)
            for b2 in range(2):
                up = slice(64 * b2, 64 * b2 + 64)
                for h2 in range(2):
                    lo = slice(64 * h2, 64 * h2 + 64)
                    last = v.tensor_copy(
                        OT[lo, 6:8, SEQ:T].rearrange("p c (a b t) -> p c a b t", b=2, t=4)[:, :, :, b2, :],
                        BANK[4][up, 0:128].rearrange("p (a b c h t) -> p c a b h t", a=4, b=2, c=2, h=2)[:, :, :, b2, h2, :])
            last.then_inc(S["ot_done"], 1)
            for c in range(KD):
                v.tensor_copy(OH_[:, c, 0:SEQ], OT[:, c, 0:SEQ]).then_inc(S["oh_ready"], 1)
            pt_out(7)
            for a in range(4):
                if a < 3:
                    if a > 0:
                        pt_out(7 + 2 * a)
                dve.wait_ge(S["va_pair"], a + 1)
                if a > 0:
                    dve.wait_ge(S["ob_t"], a + 1)
                rden = SMALL[:, SM_DEN + a:SM_DEN + a + 1]
                v.tensor_scalar_mul(OA[:, 0:384], BANK[2 * (a % 2)][:, 0:384], rden)
                v.tensor_scalar_mul(OA[:, 384:768], BANK[2 * (a % 2) + 1][:, 0:384], rden).then_inc(S["oa_sb"], 1)
                dve.wait_ge(S["ob_t"], a + 2)
                for c in range(6):
                    bank, col = (BANK[7], 128 * c) if c < 4 else (BANK[4], 128 * (c - 4))
                    for h2 in range(2):
                        lo = slice(64 * h2, 64 * h2 + 64)
                        q = 8 * c + 4 * h2
                        last = v.tensor_copy(OT[lo, c, SEQ + 8 * a:SEQ + 8 * a + 8].rearrange("p (b t) -> p b t", t=4),
                                             bank[lo, col:col + 128].rearrange("p (b r) -> p b r", b=2)[:, :, q:q + 4])
                last.then_inc(S["ot_done"], 1)
            dve.wait_ge(S["ot_done"], 5)
            v.tensor_copy(OH_[:, :, SEQ:T], OT[:, :, SEQ:T]).then_inc(S["o_tail"], 1)
            dve.wait_ge(S["o_ready"], KD + 1)

            down_stage(1)
            layer_norm(1)
            up_stage(1)
            dve.wait_ge(S["p_in"], 16)
            own.done(v.tensor_copy(PH[:], P_RAW[:]))
            own.done(v.tensor_tensor(PL[:], P_RAW[:], PH[:].bitcast(F32), ALU.subtract))
            down_stage(2)
            layer_norm(2)
            for m in range(KD):
                s = m % 2
                dve.wait_ge(S["gate_sig"], m + 1)
                if m >= 2:
                    dve.wait_ge(y_out[s], 16 * (m // 2))
                for n in range(2):
                    last = v.tensor_tensor(half(HF, s, n), half(SG, s, n), BANK[4 * s + 2 + n][:, 0:HALF], ALU.mult)
                own.done(last)
                own.done(v.tensor_tensor(HF[:, s, :], HF[:, s, :], XH[:, m, :].bitcast(F32), ALU.add))
                v.tensor_tensor(HF[:, s, :], HF[:, s, :], XL[:, m, :].bitcast(F32), ALU.add).then_inc(S["y_final"], 1)

        @block.tensor
        def _(pe):
            mm = nc.tensor.matmul

            def tile(banks, s, j, xh, xl, start, stop):
                wh, wl = WH[:, s, j, :], WL[:, s, j, :]
                for n in range(2):
                    mm(banks[n][:, 0:HALF], wh, xh[n], start=start, stop=False)
                for n in range(2):
                    mm(banks[n][:, 0:HALF], wh, xl[n], start=False, stop=False)
                for n in range(2):
                    last = mm(banks[n][:, 0:HALF], wl, xh[n], start=False, stop=stop)
                return last

            def unit(u0, i, j, banks, high, low, k0, count, first, last_tile, ready=None):
                s = (u0 + j) % 2
                pe.wait_ge(S["lo_ready"], u0 + i * 4 + j + 1)
                for t in range(count):
                    if ready is not None:
                        pe.wait_ge(S["x_ready"], ready + t + 1)
                    k = k0 + t
                    last = tile(banks, s, t, [half(high, k, n) for n in range(2)], [half(low, k, n) for n in range(2)],
                                first and t == 0, last_tile and t == count - 1)
                return last

            def up_stage(which):
                u0 = FIRST[("wi1", "wi2")[which]]

                def pair(i, ready=None):
                    for s in range(2):
                        if not (isinstance(i, int) and i == 0 and which == 0):
                            pe.wait_ge(S["h_done"], 22 * which + i * 2 + s - 1)
                        for j in (2 * s, 2 * s + 1):
                            banks = BANK[4 * s + 2 * (j % 2):4 * s + 2 * (j % 2) + 2]
                            unit(u0, i, j, banks, XH, XL, 0, KD, True, True, ready if j == 0 else None
                                 ).then_inc(S["unit_used"], 1)

                pair(0, ready=KD * 2 * which)
                with pe.Fori(1, UP_ITERS) as i:
                    pair(i)

            def down_stage(which):
                name, order = ("wo1", "wo2")[which], (0, 2)[which]
                u0 = FIRST[name]
                pe.wait_ge(S["hl_done"], KF * (which + 1))

                def pair(i):
                    for s in range(2):
                        if not (isinstance(i, int) and i == 0 and which == 0):
                            pe.wait_ge(S["y_part"], KD * order + i * 2 + s - 1)
                        for part in range(2):
                            unit(u0, i, 2 * s + part, BANK[2 * s:2 * s + 2], HH, HL, UNIT_TILES * part, UNIT_TILES,
                                 part == 0, part == 1).then_inc(S["unit_used"], 1)

                pair(0)
                with pe.Fori(1, KD // 2) as i:
                    pair(i)

            def layer_norm(which):
                pe.wait_ge(S["sum_done"], KD * (which + 1))
                for n, (a, b) in enumerate(HALVES):
                    last = mm(BANK[4 + n][:, 0:HALF], ONES[:], SUM[:, a:b], start=True, stop=True)
                last.then_inc(S["mean_ps"], 1)
                for m in range(KD):
                    pe.wait_ge(S["squared"], KD * which + m + 1)
                    for n in range(2):
                        last = mm(BANK[6 + n][:, 0:HALF], ONES[:], half(SQ, m % 2, n), start=m == 0, stop=m == KD - 1)
                    last.then_inc(S["sq_used"], 1)

            pe.wait_ge(S["setup_in"], 16 * 11)
            mm(BANK[3][0:16, :], RELC[:], TP[:, 0:512], start=True, stop=True)
            mm(BANK[4][0:16, 0:128], RELC[:], TP[:, 512:640], start=True, stop=True)
            pe.wait_ge(S["relt_done"], 1)
            rela = RELA[:].rearrange("p b h t -> p (b h t)")
            for bank, c0, c1 in ((BANK[0], 0, 512), (BANK[1], 512, KEYS_A)):
                mm(bank[:, 0:c1 - c0], rela, OH[:].rearrange("p k n -> p (k n)")[:, c0:c1], start=True, stop=False)
                mm(bank[:, 0:c1 - c0], LNC[:, KEYS_A:1024], LNC[:, c0:c1], start=False, stop=True)
            mm(BANK[2][:, 0:32], rela, OH[:, BLK_NEW, 0:32], start=True, stop=True).then_inc(S["tables_ps"], 1)
            pe.wait_ge(S["rev_in"], 1)
            pe.wait_ge(S["dve_step"], 2)
            up_stage(0)
            down_stage(0)
            layer_norm(0)

            def project(c, ready=None):
                if c >= 2:
                    pe.wait_ge(S["proj_a"], c - 1)
                    pe.wait_ge(S["proj_d"], c - 1)
                unit(FIRST["w_in"], c // 4, c % 4, BANK[2 * (c % 2):2 * (c % 2) + 2], XH, XL, 0, KD, True, True,
                     ready).then_inc(S["unit_used"], 1)

            tr = nc.tensor.transpose
            for c in range(7):
                project(c, ready=KD if c == 0 else None)
            pe.wait_ge(S["proj_a"], C_IDX + 1)
            pe.wait_ge(S["proj_d"], C_IDX + 1)
            for k in range(5):
                n = 128 if k < 4 else NDEC
                last = tr(BANK[4][0:n, 72 * k:72 * k + 72], PROJ[0:72, C_IDX, 128 * k:128 * k + n], IDENT[0:72, 0:72])
            last.then_inc(S["kiw_ps"], 1)
            mm(BANK[7][:, 0:32], SEL_HEAD, PROJ[64:72, C_IDX, SEQ:T], start=True, stop=True).then_inc(S["wsel_ps"], 1)
            for c in range(7, IDX_FROM):
                project(c)
            pe.wait_ge(S["kin_done"], 1)
            for k in range(4):
                tr(BANK[5][:, 128 * k:128 * k + 128], KIN[:, k, :], IDENT)
            tr(BANK[6][:, 0:32], KIN[0:32, 4, :], IDENT[0:32, 0:32]).then_inc(S["kit_ps"], 1)
            pe.wait_ge(S["wsel_done"], 1)
            pe.wait_ge(S["qblocks_done"], 1)
            pe.wait_ge(S["kit_sb"], 1)

            def index_prompt(n):
                i, h = n // IDX_HEADS + 1, n % IDX_HEADS
                nk = 128 * (i + 1)
                if n >= 1:
                    pe.wait_ge(S["ix_relu"], n)
                lo = slice(64 * (h % 2), 64 * (h % 2) + 64)
                mm(BANK[5][:, 0:nk], PROJ[lo, C_QI + h // 2, 128 * i:128 * i + 128], KIT[lo, 0:nk],
                   start=True, stop=True).then_inc(S["ix_ps"], 1)

            def index_transposes(g):
                pe.wait_ge(pg_in[g % 4], 128 * (g // 4 + 1))
                if g >= 1:
                    pe.wait_ge(S["kp_sb"], g)
                for p in range(4):
                    last = tr(BANK[4][:, 128 * p:128 * p + 128],
                              PG[:, g % 4, 2 * p:2 * p + 2, :].rearrange("p b n -> p (b n)"), IDENT)
                last.then_inc(S["kp_t"], 1)

            def index_scores(g):
                if g < PAGES:
                    pe.wait_ge(S["kp_sb"], g + 1)
                if g >= 1:
                    pe.wait_ge(S["kp_relu"], g)
                nk = 128 if g < PAGES else NDEC
                for p in range(4):
                    keys = KIPT[:, g % 2, p, :] if g < PAGES else KIT[:, SEQ:T]
                    last = mm(BANK[6][64 * (p % 2):64 * (p % 2) + 64, 128 * (p // 2):128 * (p // 2) + nk],
                              QIB[:, p, :], keys, start=True, stop=True)
                last.then_inc(S["kp_sc"], 1)

            def index_sum(g):
                pe.wait_ge(S["kp_relu"], g + 1)
                if g >= 1:
                    pe.wait_ge(S["kp_row"], g)
                nk = 128 if g < PAGES else NDEC
                for a in range(2):
                    last = mm(BANK[7][0:32, 0:nk], WB[:, a, :], RLD[:, g % 2, a, 0:nk], start=a == 0, stop=a == 1)
                last.then_inc(S["kp_sum"], 1)

            for s in range(PAGES + 3):
                if s < PAGES:
                    index_transposes(s)
                if s < 8:
                    index_prompt(3 * s)
                if 1 <= s < PAGES + 2:
                    index_scores(s - 1)
                if s < 8:
                    index_prompt(3 * s + 1)
                if s >= 2:
                    index_sum(s - 2)
                if s < 8:
                    index_prompt(3 * s + 2)
                if IDX_FROM + s < N_PROJ:
                    project(IDX_FROM + s)

            pe.wait_ge(S["proj_a"], N_PROJ)
            pe.wait_ge(S["proj_d"], N_PROJ)
            pe.wait_ge(S["kp_row"], PAGES + 1)
            for g in range(11):
                bank = BANK[2 + g % 6]
                if g >= 6:
                    pe.wait_ge(S["tr_a"] if g % 2 == 0 else S["tr_d"], (g - 6) // 2 + 1)
                for q in range(4):
                    if g < 6:
                        blk, c = (4 * g + q) // 6, (4 * g + q) % 6
                        src, n = PROJ[:, C_VA + c, 128 * blk:128 * blk + 128], 128
                    elif g == 6:
                        src, n = PROJ[:, C_KV, 128 * q:128 * q + 128], 128
                    elif g < 10:
                        src, n = PROJ[:, C_KA + 4 * (g - 7) + q, SEQ:T], NDEC
                    elif q == 0:
                        src, n = PROJ[:, C_KV, SEQ:T], NDEC
                    else:
                        break
                    last = tr(bank[0:n, 128 * q:128 * q + 128], src, IDENT)
                last.then_inc(S["tr_ps"], 1)
            pe.wait_ge(S["tr_a"], 6)
            pe.wait_ge(S["tr_d"], 5)
            pe.wait_ge(S["kb2_done"], 1)

            def scores(n):
                h, i = n // 4, n % 4
                if n >= 4:
                    pe.wait_ge(S["logits_done"], n - 3)
                nk = 128 * (i + 1)
                base = 64 * (h % 2)
                lo = slice(base, base + 64)
                if h < HEADS_A:
                    keys = PROJ[lo, C_KA + h // 2, 0:nk]
                else:
                    keys = KB2[lo, 0:nk] if base else PROJ[lo, C_KV, 0:nk]
                mm(SCORE_BANK[n % 4][:, 0:nk], PROJ[lo, C_QA + h // 2, 128 * i:128 * i + 128], keys,
                   start=True, stop=True).then_inc(S["sc_ps"], 1)

            def transposed(n):
                pe.wait_ge(S["probs_done"], n + 1)
                if n >= 2:
                    pe.wait_ge(S["pt_sb"], n - 1)
                for j in range(n % 4 + 1):
                    last = tr(BANK[2 + n % 2][:, 128 * j:128 * j + 128], LP[:, n % 3, 128 * j:128 * j + 128], IDENT)
                last.then_inc(S["pt_ps"], 1)

            def values(n):
                h, i = n // 4, n % 4
                q, base = h // 2, 64 * (h % 2)
                if n % 8 == 0 and q >= 2:
                    pe.wait_ge(S["o_sb"], q - 1)
                pe.wait_ge(S["pt_sb"], n + 1)
                for j in range(i + 1):
                    val = VP[:, j, 64 * h:64 * h + 64] if h < HEADS_A else VBT[:, j, HD:128]
                    last = mm(BANK[4 + q % 2][base:base + 64, 128 * i:128 * i + 128], val,
                              PTS[:, n % 2, 128 * j:128 * j + 128], start=j == 0, stop=j == i)
                last.then_inc(S["pv_done"], 1)

            for n in range(N_STEPS + 3):
                if n < N_STEPS:
                    scores(n)
                if 2 <= n < N_STEPS + 2:
                    transposed(n - 2)
                if n >= 3:
                    values(n - 3)

            pe.wait_ge(S["o_sb"], 8)
            pe.wait_ge(S["qblocks_done"], 2)

            def key_scores_a(n):
                b, k = n // 7, n % 7
                a, rows = b // 2, slice(64 * (b % 2), 64 * (b % 2) + 64)
                banks = BANK[4 + 2 * (a % 2):6 + 2 * (a % 2)]
                pe.wait_ge(S["ka_sb"], n + 1)
                if k == 0 and b % 2 == 0 and a >= 2:
                    pe.wait_ge(S["ka_logits"], a - 1)
                for c in range(6):
                    last = mm(banks[k // 4][rows, 128 * (k % 4):128 * (k % 4) + 128], QBLKA[:, c, 48 * b:48 * b + 64],
                              KTA[:, n % 2, 128 * c:128 * c + 128], start=c == 0, stop=c == 5)
                if k == 6:
                    for c in range(6):
                        last = mm(banks[1][rows, 384:416], QBLKA[:, c, 48 * b:48 * b + 64], KNT[:, c, :],
                                  start=c == 0, stop=c == 5)
                last.then_inc(S["ka_sc"], 1)

            for n in range(57):
                if n < 56:
                    pe.wait_ge(ar_in[n % 4], 16 * (n // 4 + 1))
                    if n >= 2:
                        pe.wait_ge(S["ka_sb"], n - 1)
                    for c in range(6):
                        last = tr(BANK[2 * (n % 2) + c // 4][:, 128 * (c % 4):128 * (c % 4) + 128],
                                  AR[:, n % 4, 128 * c:128 * c + 128], IDENT)
                    last.then_inc(S["ka_t"], 1)
                if n >= 1:
                    key_scores_a(n - 1)

            pe.wait_ge(S["oh_in"], 16)
            relb = RELB[:].rearrange("p b h t -> p (b h t)")
            for j in range(5):
                nk = 512 if j < 4 else NDEC
                if j == 4:
                    pe.wait_ge(S["ka_logits"], 3)
                mm(BANK[j][:, 0:nk], relb, OHB[:].rearrange("p k n -> p (k n)")[:, 512 * j:512 * j + nk],
                   start=True, stop=False, skip_group_check=True)
            mm(BANK[4][:, 0:32], QBLKB[:].rearrange("p a n -> p (a n)"), KB2[:, SEQ:T], start=False, stop=False,
               skip_group_check=True)
            for g in range(PAGES + 1):
                if g < PAGES:
                    pe.wait_ge(S["kc_ready"], g + 1)
                    if g < 2:
                        pe.wait_ge(S["ka_logits"], 3 + g)
                    else:
                        pe.wait_ge(S["kb_sb"], g - 1)
                    for p in range(4):
                        last = tr(BANK[5 + g % 2][:, 128 * p:128 * p + 128],
                                  KC[:, g % 2, 2 * p:2 * p + 2, :].rearrange("p b n -> p (b n)"), IDENT)
                    last.then_inc(S["kb_t"], 1)
                if g >= 1:
                    m = g - 1
                    pe.wait_ge(S["kb_sb"], m + 1)
                    for p in range(4):
                        last = mm(BANK[m // 4][32 * p:32 * p + 32, 128 * (m % 4):128 * (m % 4) + 128], QBLKB[:, p, :],
                                  KTB[:, m % 2, 128 * p:128 * p + 128], start=False, stop=False, skip_group_check=True)
                    last.then_inc(S["kb_sc"], 1)
            pe.wait_ge(S["topk_dec_done"], 1)
            for j in range(5):
                nk = 512 if j < 4 else NDEC
                last = mm(BANK[j][:, 0:nk], SEL_QUERY, SC[:, 512 * j:512 * j + nk], start=False, stop=True,
                          skip_group_check=True)
            last.then_inc(S["b_logits"], 1)

            def pt_transposes(i):
                which, q, part = pt_group(i)
                if i >= 2:
                    pe.wait_ge(S["pt_a"] if i % 2 == 0 else S["pt_d"], i // 2)
                if which == "a":
                    pe.wait_ge(S["expa_done"], q + 1)
                for j in range(4 if which == "a" or q < 4 else 1):
                    k = 4 * (part if which == "a" else q) + j
                    n = 128
                    if which == "a":
                        c0 = 128 * k
                        if k == 7:
                            n = NDEC
                        src = STA[:, q, c0:c0 + n]
                    else:
                        if k == 16:
                            n = NDEC
                        src = STB[:, 128 * k:128 * k + n]
                    last = tr(BANK[5 + i % 2][0:n, 128 * j:128 * j + 128], src, IDENT)
                last.then_inc(S["pt_ps2"], 1)

            pe.wait_ge(S["kb_sb"], PAGES)
            for i in range(2):
                pt_transposes(i)
            pe.wait_ge(S["b_exp"], 1)
            for i in range(2, 7):
                pt_transposes(i)
            pe.wait_ge(S["pt_a"], 4)
            pe.wait_ge(S["pt_d"], 3)
            for g in range(PAGES + 1):
                for p in range(4):
                    if g < PAGES:
                        val, probs = KVP[:, DEC_BATCH * g + 2 * p:DEC_BATCH * g + 2 * p + 2, HD:2 * HD], PTB[:, g, 32 * p:32 * p + 32]
                    else:
                        val, probs = VBN[:], PTB[0:32, g, 32 * p:32 * p + 32]
                    last = mm(BANK[7][32 * p:32 * p + 32, 0:128], probs, val, start=g == 0, stop=g == PAGES,
                              skip_group_check=True)
            last.then_inc(S["vb_all"], 1)

            pe.wait_ge(S["vnew_in"], 16)

            def out_transposes_a(a):
                pe.wait_ge(S["oa_sb"], a + 1)
                pe.wait_ge(S["ot_done"], a + 1)
                for c in range(6):
                    bank, col = (BANK[7], 128 * c) if c < 4 else (BANK[4], 128 * (c - 4))
                    last = tr(bank[:, col:col + 128], OA[:, 128 * c:128 * c + 128], IDENT)
                last.then_inc(S["ob_t"], 1)

            for a in range(4):
                if a >= 2:
                    pe.wait_ge(S["oa_sb"], a - 1)
                for b in (2 * a, 2 * a + 1):
                    rows = slice(64 * (b % 2), 64 * (b % 2) + 64)
                    for k in range(8):
                        n = 56 + 7 * b + k
                        if k < 7:
                            pe.wait_ge(ar_in[n % 4], 16 * (n // 4 + 1))
                        for q in range(2):
                            if k < 7:
                                probs, val = PTA[:, a % 2, k, rows], AR[:, n % 4, 384 * q:384 * q + 384]
                            else:
                                probs, val = PTA[0:32, a % 2, 7, rows], VN2[:, 384 * q:384 * q + 384]
                            last = mm(BANK[2 * (a % 2) + q][rows, 0:384], probs, val, start=k == 0, stop=k == 7)
                        if k < 7:
                            last.then_inc(S["va_used"], 1)
                        elif b % 2:
                            last.then_inc(S["va_pair"], 1)
                        if b % 2 == 0 and k == 1 and a < 3:
                            for i in (7 + 2 * a, 8 + 2 * a):
                                pt_transposes(i)
                        if b % 2 == 0 and k == 3:
                            if a == 0:
                                pe.wait_ge(S["ob_sb"], 1)
                                tr(BANK[4][:, 0:128], OB[:], IDENT).then_inc(S["ob_t"], 1)
                            else:
                                out_transposes_a(a - 1)
                if a < 3:
                    pe.wait_ge(S["pt_a"], PT_DONE_A[a])
                    pe.wait_ge(S["pt_d"], PT_DONE_D[a])
            out_transposes_a(3)

            u0 = FIRST["w_out"]
            pe.wait_ge(S["o_ready"], KD + 1)
            for i in range(2):
                for j in range(4):
                    s = j % 2
                    pe.wait_ge(S["y_part"], KD + i * 4 + j - 1) 
                    unit(u0, i, j, BANK[2 * s:2 * s + 2], OH_, OL_, 0, KD, True, True).then_inc(S["unit_used"], 1)
            layer_norm(1)
            up_stage(1)
            down_stage(1)
            layer_norm(2)
            u0 = FIRST["gate"]
            for m in range(KD):
                s = m % 2
                if m >= 2:
                    pe.wait_ge(S["y_final"], m - 1)
                unit(u0, 0, m, BANK[4 * s:4 * s + 2], XH, XL, 0, KD, True, True, KD * 3 if m == 0 else None)
                for t in range(KP):
                    last = tile(BANK[4 * s + 2:4 * s + 4], (u0 + m) % 2, KD + t, [half(PH, t, n) for n in range(2)],
                                [half(PL, t, n) for n in range(2)], t == 0, t == KP - 1)
                last.then_inc(S["unit_used"], 1)


def bucket(d):
    d = np.maximum(d, 0)
    exact = BUCKETS // 2
    scaled = np.log(np.maximum(d, 1) / exact) / log(REL_MAX / exact)
    large = exact + np.floor(scaled * (BUCKETS - exact) + 1e-9).astype(int)
    return np.where(d < exact, d, np.minimum(large, BUCKETS - 1))


def log_count(d):
    count = sum(((d >= 0) & (d <= window) & (d % dil == 0)).astype(int) for window, dil in PATTERNS)
    return np.where(count > 0, np.log(np.maximum(count, 1)), NEG)


def shape_constants():
    p = np.arange(128)
    rows = [16 * (32 * k + p // 4) + p % 4 for k in range(STRIDED_BLOCKS)]
    rows += [PAST - 512 + 128 * k + p for k in range(4)]
    t = np.arange(4)
    patterns = np.zeros((4, 1024), np.float32)
    patterns[:, 0:KEYS_A] = log_count(PAST + t[:, None] - np.concatenate(rows)[None, :])
    patterns[:, KEYS_A:] = (p % 4)[None, :] == t[:, None]
    kb, kt = np.arange(32) // 4, np.arange(32) % 4
    batch = 2 * np.arange(4)[None, :, None] + (p // 64)[:, None, None]
    mask_new = np.where(batch == kb, log_count((p % 4)[:, None, None] - kt), NEG).astype(np.float32)
    consts = np.zeros((128, 352), np.float32)
    consts[:, 0:128] = np.eye(128)
    own = kb[:, None] == kb[None, :]
    consts[0:32, 128:160] = np.where(own & (kt[None, :] <= kt[:, None]), 0.0, NEG)
    consts[64:72, 160:288] = (p % 32 // 4)[None, :] == np.arange(8)[:, None]
    consts[0:32, 160:288] = (4 * (p // 16) + p % 4)[None, :] == np.arange(32)[:, None]
    for a in range(2):
        q = np.arange(32)
        consts[:, 288 + 32 * a:320 + 32 * a] = IDX_SCALE * (
            (q // 4 == 4 * a + p[:, None] // 32) & (q % 4 == p[:, None] % 4))
    onehots = np.zeros((128, 24, 128), np.float32)
    keys = rows + [128 * g + p for g in range(PAGES)]
    for k, r in enumerate(keys):
        for step in range(4):
            onehots[32 * step + bucket(PAST + step - r), k, p] = 1.0
    for step in range(4):
        onehots[32 * step + bucket(step - kt), BLK_NEW, np.arange(32)] = 1.0
    toeplitz = np.zeros((34, 640), np.float32)
    d = 511 - np.arange(640)
    toeplitz[bucket(d), np.arange(640)] = 1.0
    toeplitz[32] = log_count(d)
    toeplitz[33] = np.where(d >= 0, 0.0, NEG)
    rel_rows = np.zeros((2, 16), np.float32)
    rel_rows[0, :HEADS_A] = 1.0
    rel_rows[1, HEADS_A:] = 1.0
    return consts, onehots, patterns, mask_new, toeplitz, rel_rows


def kernel(x_prompt, x_sample, cache_a_kv, cache_b, page_table, p_prompt, p_sample, ln_g, ln_b,
           ffn1_wi, ffn1_wo, w_in, kidx_ln_g, kidx_ln_b, w_out, ffn2_wi, ffn2_wo, ple_proj, ple_gate,
           rel_bias):
    import concourse.bacc as bacc
    from concourse.bass_utils import run_bass_kernel_spmd

    def features(a, b, chunks):
        both = np.concatenate([np.asarray(a).reshape(SEQ, -1), np.asarray(b).reshape(NDEC, -1)])
        return np.ascontiguousarray(both.T.reshape(chunks, 128, T).transpose(1, 0, 2))

    def units(a, tiles, count, parts=1):
        a = np.asarray(a).reshape(parts, tiles, 128, count, 128)
        return a.transpose(3, 0, 2, 1, 4).reshape(count * parts, 128, tiles, 128)

    def up_units(a):
        u = units(a, KD, 2 * KF)
        return np.ascontiguousarray(u.reshape(2, KF, 128, KD, 128).transpose(1, 0, 2, 3, 4)).reshape(2 * KF, 128, KD, 128)

    wa, wb, wi_ = WIDTH_A, HEADS_B * HD, IDX_HEADS * HD
    w_in0 = np.asarray(w_in)[0]
    at = np.cumsum([0, wa, wa, wa, wb, HD, HD, wi_, HD, IDX_HEADS])
    qa, ka, va, qb, kb, vb, qi, ki, wi = (w_in0[:, at[n]:at[n + 1]] for n in range(9))
    pad = np.zeros((D_MODEL, 128 - HD - IDX_HEADS), w_in0.dtype)
    w_proj = np.concatenate([qi, ki, wi, pad, kb, vb, ka, va, qa, qb], axis=1)
    gate = units(np.asarray(ple_gate)[0], KD, KD)
    ple = units(np.asarray(ple_proj)[0], KP, KD)
    w = {
        "wi1": up_units(np.asarray(ffn1_wi)[0]),
        "wo1": units(np.asarray(ffn1_wo)[0], UNIT_TILES, KD, 2),
        "w_in": units(w_proj, KD, N_PROJ),
        "w_out": units(np.asarray(w_out)[0], KD, KD),
        "wi2": up_units(np.asarray(ffn2_wi)[0]),
        "wo2": units(np.asarray(ffn2_wo)[0], UNIT_TILES, KD, 2),
        "gate": np.concatenate([gate, ple], axis=2),
    }
    ln = np.stack([np.asarray(ln_g)[0], np.asarray(ln_b)[0]], axis=1).reshape(6, KD, 128).transpose(2, 0, 1)
    consts, onehots, patterns, mask_new, toeplitz, rel_rows = shape_constants()
    n_pool = np.asarray(cache_b).shape[1]
    arrays = {
        "x_t": features(x_prompt, x_sample, KD),
        "p_t": features(p_prompt, p_sample, KP),
        "cache_a": np.asarray(cache_a_kv).reshape(DEC_BATCH, PAST, 2 * WIDTH_A),
        "cache_b": np.asarray(cache_b).reshape(n_pool, PAGE, ROW_B),
        "page_table": np.asarray(page_table),
        "ln": ln,
        "kidx_g": np.asarray(kidx_ln_g)[0],
        "kidx_b": np.asarray(kidx_ln_b)[0],
        "rel_bias": np.asarray(rel_bias),
        "rel_rows": rel_rows, "consts": consts, "onehots": onehots,
        "patterns": patterns, "mask_new": mask_new, "toeplitz": toeplitz,
    }
    arrays.update({"w_" + name: a for name, a in w.items()})
    arrays = {name: np.ascontiguousarray(a) for name, a in arrays.items()}
    outs = {
        "y_t": (KD, 128, T), "kv_a_t": (12, 128, SEQ), "a_sample": (DEC_BATCH, PAST, 2 * WIDTH_A),
        "kv_b_t": (128, T), "ki_b": (128, 5, HD),
    }
    nc = bacc.Bacc("TRN2", target_bir_lowering=False, num_devices=1)
    ins = {name: nc.dram_tensor("in_" + name, a.shape, mybir.dt.from_np(a.dtype), kind="ExternalInput").ap()
           for name, a in arrays.items()}
    res = {name: nc.dram_tensor("out_" + name, shape, F32, kind="ExternalOutput").ap() for name, shape in outs.items()}
    weights = {name: ins.pop("w_" + name) for name in w}
    build_program(nc, w=weights, **ins, **res)
    r = run_bass_kernel_spmd(nc, [{"in_" + name: a for name, a in arrays.items()}], core_ids=[0]).results[0]

    y = r["out_y_t"].transpose(2, 0, 1).reshape(T, D_MODEL)
    kv = r["out_kv_a_t"].reshape(2, HEADS_A, HD, SEQ).transpose(3, 0, 1, 2)
    row_b = np.concatenate([r["out_kv_b_t"].T, r["out_ki_b"].transpose(1, 0, 2).reshape(640, HD)[:T]], axis=1)
    return (
        y[:SEQ].reshape(1, SEQ, D_MODEL), y[SEQ:].reshape(DEC_BATCH, DEC_SEQ, D_MODEL),
        kv.reshape(1, 1, SEQ, 2, HEADS_A, HD),
        r["out_a_sample"].reshape(1, DEC_BATCH, PAST, 2, HEADS_A, HD),
        row_b[:SEQ].reshape(1, 1, SEQ, ROW_B), row_b[SEQ:].reshape(1, DEC_BATCH, DEC_SEQ, ROW_B),
    )
```

```python
from contextlib import ExitStack
from math import log

import concourse.bass as bass
import numpy as np
from concourse import mybir

F32 = mybir.dt.float32
F32R = mybir.dt.float32r
I32 = mybir.dt.int32
ACT = mybir.ActivationFunctionType
ALU = mybir.AluOpType
AX = mybir.AxisListType

D_MODEL, SEQ, DEC_BATCH, DEC_SEQ, PAST, PAGE = 1024, 512, 8, 4, 2048, 128
HD, HEADS_A, HEADS_B, IDX_HEADS = 64, 12, 4, 8
D_FF, D_PLE, BUCKETS, REL_MAX = 2816, 256, 32, 2048
ROW_B = 3 * HD
WIDTH_A = HEADS_A * HD
ALPHA = 2.0 ** 0.25
LN_EPS = 1e-5
PATTERNS = ((128, 1), (512, 4), (2048, 16))
TOPK_PROMPT, TOPK_DEC = 128, 256
IDX_SCALE = HD ** -0.5 * IDX_HEADS ** -0.5
NEG = -1.0e30
TAKEN = -3.0e38
TAKEN_LIMIT = -2.0e38

NDEC = DEC_BATCH * DEC_SEQ
T = SEQ + NDEC
HALF = T // 2
HALVES = ((0, HALF), (HALF, T))
KD = D_MODEL // 128
KF = D_FF // 128
KP = D_PLE // 128
UNIT_TILES = KF // 2
QB_BLOCKS = SEQ // 128
PAGES = PAST // PAGE

C_QI, C_IDX, C_KV, C_KA, C_VA, C_QA, C_QB, N_PROJ = 0, 4, 5, 6, 12, 18, 24, 26

KEY_BLOCKS_A, BLK_NEW = 7, 23
KEYS_A = 128 * KEY_BLOCKS_A
ALL_A = KEYS_A + DEC_BATCH * DEC_SEQ
STRIDED_BLOCKS = 3

STAGES = (("wi1", 44, 8), ("wo1", 16, 11), ("w_in", 26, 8), ("w_out", 8, 8),
          ("wi2", 44, 8), ("wo2", 16, 11), ("gate", 8, 10))
FIRST = {}
_u = 0
for _n, _c, _t in STAGES:
    FIRST[_n] = _u
    _u += _c
N_UNITS = _u
STAGE_TILES = {name: tiles for name, _, tiles in STAGES}
RAW_SLOTS, SPLIT_SLOTS = 4, 2
COPY_ROWS = 28
N_COPIES = (PAST - DEC_SEQ) // COPY_ROWS


def tiles_of(u):
    for name, count, tiles in STAGES:
        if u < FIRST[name] + count:
            return tiles
    raise ValueError(u)


def spread(ap, axis, n):
    a = ap.unsqueeze(axis)
    shape = list(a.shape)
    shape[axis] = n
    return a.broadcast_to(shape)


class Steps:

    def __init__(self, eng, sem):
        self.eng, self.sem, self.n = eng, sem, 0

    def done(self, instruction):
        instruction.then_inc(self.sem, 1)
        self.n += 1
        self.eng.wait_ge(self.sem, self.n)


def build_program(nc, x_t, p_t, cache_a, cache_b, page_table, ln, kidx_g, kidx_b, w, rel_bias,
                  rel_rows, consts, onehots, patterns, mask_new, toeplitz, y_t, kv_a_t, a_sample, kv_b_t, ki_b):
    ctx = ExitStack()
    with ctx:
        SBUF_FROM, SBUF_TO = 16512, 229344
        place = {"at": SBUF_FROM}

        def sb(name, shape, dt=F32, at=None):
            size = int(np.prod(shape[1:])) * 4
            if at is None:
                at = place["at"]
                place["at"] += (size + 31) // 32 * 32
                assert place["at"] <= SBUF_TO, (name, place["at"])
            return nc.alloc_sbuf_tensor_at(name, list(shape), dt, offset=at)

        XH = sb("x_high", [128, KD, T], F32R)
        XL = sb("x_rest", [128, KD, T], F32R)
        RAW = sb("w_raw", [128, RAW_SLOTS, UNIT_TILES, 128])
        split_at = place["at"]
        WH = sb("w_high", [128, SPLIT_SLOTS, UNIT_TILES, 128], F32R)
        WL = sb("w_rest", [128, SPLIT_SLOTS, UNIT_TILES, 128], F32R)
        h_at = place["at"]
        HH = sb("hidden_high", [128, KF, T], F32R)
        HL = sb("hidden_rest", [128, KF, T], F32R)
        h_end = y_at = place["at"]
        Y = sb("y", [128, KD, T])
        CP = sb("consts_sb", [128, 352])
        BIAS_A = sb("bias_a", [128, KEYS_A])
        BIAS_N = sb("bias_a_new", [128, 4, NDEC])
        RELB = sb("rel_b", [128, DEC_BATCH, HEADS_B, 4])
        LN = sb("ln_sb", [128, 6, KD])
        KIDX_GB = sb("kidx_gb", [128, 2, HD])
        ONES = sb("ones", [128, 128])
        PAGE_IDS = sb("page_ids", [1, DEC_BATCH * PAGES], I32)
        SMALL = sb("small", [128, 96])
        e_at = place["at"]

        IDENT = CP[:, 0:128]
        MASK_NEW_IX = CP[0:32, 128:160]
        SEL_HEAD = CP[64:72, 160:288]
        SEL_QUERY = CP[0:32, 160:288]
        WMASK = CP[:, 288:352].rearrange("p (k c) -> p k c", k=2)

        SG = sb("silu_gate", [128, 2, T], at=y_at)
        HF = sb("hidden", [128, 2, T], at=y_at + 2 * T * 4)
        P_RAW = sb("p_raw", [128, KP, T], at=y_at + 4 * T * 4)
        SUM = sb("sum_acc", [128, T], at=e_at)
        PH = sb("p_high", [128, KP, T], F32R, at=e_at + T * 4)
        PL = sb("p_rest", [128, KP, T], F32R, at=e_at + 3 * T * 4)
        OH = sb("onehots_sb", [128, 24, 128], at=h_at)
        TP = sb("toeplitz_sb", [34, 640], at=h_at + 12288)
        RELC = sb("rel_sb", [34, 16], at=h_at + 16384)
        RELREP = sb("rel_rep", [128, 16], at=h_at + 16512)
        RELA = sb("rel_a", [128, 2, 16, 4], at=h_at + 16640)
        LNC = sb("patterns_sb", [4, 1024], at=h_at + 20480)
        MNEW = sb("mask_new_sb", [128, 4, NDEC], at=h_at + 24576)
        REV = sb("rev_sb", [16, 640], at=e_at + 4096)
        ln_at = h_end - (4 + KD) * T * 4
        MEAN = sb("mean", [128, T], at=ln_at)
        RSTD = sb("rstd", [128, T], at=ln_at + T * 4)
        SQ = sb("squares", [128, KD, T], at=ln_at + 4 * T * 4)
        XN = sb("x_new", [128, 2, T], at=ln_at + 2 * T * 4)
        PROJ = sb("proj", [128, N_PROJ, T], at=h_at)
        vp_at = h_at + N_PROJ * T * 4
        VP = sb("v_prompt", [128, QB_BLOCKS, WIDTH_A], at=vp_at)
        wk_at = vp_at + QB_BLOCKS * WIDTH_A * 4
        TOE = sb("bias_toeplitz", [128, 2, SEQ], at=wk_at)
        PTS = sb("probs_t", [128, 2, SEQ], at=wk_at + 10240)
        MSK = sb("topk_work", [128, 3, SEQ], at=wk_at + 14336)
        TM = sb("bias_masked", [128, 2, SEQ], at=wk_at + 20480)
        KIT = sb("kidx_t", [128, T], at=wk_at + 24576)
        assert wk_at + 24576 + T * 4 <= h_end
        LP = [sb(f"logits{i}", [128, SEQ], at=wk_at + 4096 + 2048 * i if i < 3 else wk_at + 24576) for i in range(4)]
        KI0 = sb("kidx_wi_tok", [128, 5, 72], at=wk_at + 20480)
        KIN = sb("kidx_norm", [128, 5, 128], at=wk_at + 20480 + 1440)
        RL = sb("idx_relu", [128, 2, SEQ], at=wk_at + 10240)
        KIPT = sb("kidx_pages_t", [128, 2, 4, 128], at=wk_at + 4096)
        RLD = sb("idx_relu_dec", [128, 2, 2, 128], at=wk_at + 8192)
        KNEW = sb("k_a_new_tok", [NDEC, WIDTH_A], at=y_at)
        VNEW = sb("v_a_new_tok", [NDEC, WIDTH_A], at=y_at + 3072)
        QIB = sb("q_idx_blocks", [128, 4, 64], at=y_at + 6144)
        WB = sb("w_idx_blocks", [128, 2, 32], at=y_at + 7168)
        PG = sb("idx_pages_ring", [128, 4, DEC_BATCH, HD], at=y_at + 7680)
        OT = sb("attn_out_t", [128, KD, T], at=y_at)
        OH_ = sb("attn_out_high", [128, KD, T], F32R, at=h_at)
        OL_ = sb("attn_out_rest", [128, KD, T], F32R, at=h_at + KD * T * 4)
        SC = sb("idx_scores", [NDEC, PAST + NDEC], at=e_at)
        KB2 = sb("k_b_high_half", [128, T], at=e_at + 8320)
        assert e_at + 10496 <= SBUF_TO and e_at + 5 * T * 4 <= SBUF_TO, SBUF_TO - e_at
        AR = sb("cache_a_ring", [128, 4, WIDTH_A], at=split_at)
        KTA = sb("k_a_t", [128, 2, WIDTH_A], at=split_at + 12288)
        KTB = sb("k_b_t", [128, 2, 512], at=split_at + 12288)
        KC = [sb("k_b_pages0", [128, DEC_BATCH, HD], at=split_at + 18432),
              sb("k_b_pages1", [128, DEC_BATCH, HD], at=e_at + 8320)]
        PTA = sb("probs_a_t", [128, 2, 8, 128], at=split_at + 12288)
        VBT = sb("kv_b_tok", [128, QB_BLOCKS, 128], at=split_at + 18432)
        VBN = sb("kv_b_new_tok", [NDEC, 128], at=split_at + 20480)
        assert split_at + 20992 <= h_at
        raw_at = SBUF_FROM + 2 * KD * T * 4
        QBLKA = sb("q_a_blocks", [128, 6, DEC_BATCH * 48 + 16], at=raw_at)
        QBLKB = sb("q_b_blocks", [128, 4, 32], at=raw_at + 9600)
        KNT = sb("k_a_new_t", [128, 6, NDEC], at=raw_at + 10112)
        OHB = sb("onehots_b", [128, 17, 128], at=raw_at + 11264)
        PTB = sb("probs_b_t", [128, 17, 128], at=raw_at + 11264)
        AV = [AR[:, k, :] for k in range(4)] + [
            sb(f"values_a{k}", [128, WIDTH_A], at=raw_at + 3072 * k)[:] for k in range(3)]
        KVP = sb("kv_b_pages", [128, DEC_BATCH * PAGES, 128], at=h_at)
        STA = sb("logits_a", [128, 4, ALL_A], at=h_at + 65536)
        STB = sb("logits_b", [128, PAST + NDEC], at=h_at + 65536 + 14848)
        OA = sb("out_a", [128, WIDTH_A], at=h_at + 65536 + 23168)
        OB = sb("out_b", [128, 128], at=h_at + 65536 + 26240)
        VN2 = sb("v_a_new", [NDEC, WIDTH_A], at=h_at + 65536 + 26752)
        assert h_at + 65536 + 26752 + 3072 <= h_end
        SM_MINS, SM_MIN, SM_DEN, SM_BMAX, SM_BSUM = 64, 76, 80, 84, 90

        BANK = [ctx.enter_context(nc.psum_tensor(f"bank{i}", [128, 512], F32)) for i in range(8)]
        REV_COPIES = 64
        REV_DRAM = nc.dram_tensor("rev_bias", [16, REV_COPIES, 640], F32, kind="Internal").ap()
        TOE_IN = 16 * (128 // REV_COPIES)

        names = """setup_in ids_in ln_in ones_done relt_done tables_ps tables_out rev_in rev_out
            xh_ready x_ready hi_ready lo_ready unit_used
            silu_done h_done hh_done hl_done y_part y_full sum_done
            mean_ps mean_sb centred squared sq_added sq_used var_sb std_sb zed xn_done xh_ln
            p_in gate_sig y_final
            proj_a proj_d kiw_ps ki_var ki_std kin_done kit_ps kit_sb kb2_done tr_ps tr_a tr_d qblocks_done
            ix_ps ix_relu ix_acc wsel_ps wsel_done kp_t kp_sb kp_sc kp_relu kp_sum kp_row ix_causal
            topk_prompt_done sc_ps logits_done exp_done den_done probs_done pt_ps pt_sb pv_done o_sb tm_done
            new_rows_out proj_out copy_done
            oh_in vnew_in
            ka_t ka_sb ka_sc ka_logits expa_done
            topk_dec_done kc_ready kc_ready_d kb_t kb_sb kb_sc b_logits b_max b_exp
            pt_ps2 pt_a pt_d vb_all ob_sb oa_sb ob_t va_used va_pair ot_done o_tail
            oh_ready o_ready dve_step""".split()
        S = {n: ctx.enter_context(nc.semaphore(n)) for n in names}
        raw_loaded = [ctx.enter_context(nc.semaphore(f"raw_loaded{i}")) for i in range(RAW_SLOTS)]
        toe_in = [ctx.enter_context(nc.semaphore(f"toe_in{i}")) for i in range(2)]
        ar_in = [ctx.enter_context(nc.semaphore(f"ar_in{i}")) for i in range(4)]
        pg_in = [ctx.enter_context(nc.semaphore(f"pg_in{i}")) for i in range(4)]
        av_in = [ctx.enter_context(nc.semaphore(f"av_in{i}")) for i in range(KEY_BLOCKS_A)]
        kv_in = [ctx.enter_context(nc.semaphore(f"kv_in{i}")) for i in range(8)]
        x_in = [ctx.enter_context(nc.semaphore(f"x_in{i}")) for i in range(2)]
        y_out = [ctx.enter_context(nc.semaphore(f"y_out{i}")) for i in range(2)]

        block = ctx.enter_context(nc.Block())
        UP_ITERS = KF // 2
        SCORE_BANK = [BANK[0], BANK[1], BANK[6], BANK[7]]
        N_STEPS = 4 * (HEADS_A + HEADS_B)

        def raw_slot(u0, j):
            return (u0 + j) % RAW_SLOTS

        def half(t, k, n):
            a, b = HALVES[n]
            return t[:, k, a:b]

        TR_FROM, TR_IN_SLOTS, TR_GROUPS = 8, 9, 11

        def tr_bank(g):
            return BANK[5] if g < TR_IN_SLOTS else BANK[4 + 2 * (g - TR_IN_SLOTS)]

        def tr_copies(g):
            bank = tr_bank(g)
            if g < 6:
                return [(VP[:, :, :].rearrange("p a n -> p (a n)")[:, 512 * g:512 * g + 512], bank[:, :])]
            if g == 6:
                return [(KNEW[:, 0:512], bank[0:32, :])]
            if g == 7:
                return [(KNEW[:, 512:768], bank[0:32, 0:256]), (VNEW[:, 0:256], bank[0:32, 256:512])]
            if g == 8:
                return [(VNEW[:, 256:768], bank[0:32, :])]
            if g == 9:
                return [(VBT[:, :, :].rearrange("p a n -> p (a n)"), bank[:, :])]
            return [(VBN[:, 0:HD], bank[0:32, HD:128]), (VBN[:, HD:128], bank[0:32, HD:128])]

        IDX_FROM, N_PT = 9, 13
        PT_DONE_A = [(9 + 2 * a + 1) // 2 for a in range(3)]
        PT_DONE_D = [(9 + 2 * a) // 2 for a in range(3)]

        def pt_group(i):
            if 2 <= i < 7:
                return "b", i - 2, 0
            j = i if i < 2 else i - 5
            return "a", j // 2, j % 2

        def pt_copies(i):
            which, q, part = pt_group(i)
            bank = BANK[5 + i % 2]
            if which == "b":
                if q == 4:
                    return [(PTB[0:32, 16, :], bank[0:32, 0:128])]
                return [(PTB[:, 4 * q:4 * q + 4, :].rearrange("p g n -> p (g n)"), bank[:, :])]
            if part == 0:
                return [(PTA[:, q % 2, 0:4, :].rearrange("p g n -> p (g n)"), bank[:, :])]
            return [(PTA[:, q % 2, 4:7, :].rearrange("p g n -> p (g n)"), bank[:, 0:384]),
                    (PTA[0:32, q % 2, 7, :], bank[0:32, 384:512])]

        def load_kv_page(eng, q):
            g, b = q // DEC_BATCH, q % DEC_BATCH
            page = eng.value_load(PAGE_IDS[0:1, b * PAGES + g:b * PAGES + g + 1], min_val=0, max_val=cache_b.shape[0] - 1)
            eng.dma_start(KVP[:, q, :], cache_b[bass.ds(page, 1), :, 0:2 * HD].rearrange("o p n -> (o p) n")
                          ).then_inc(kv_in[g // 4 + 4 * (q % 2)], 16)

        @block.sync
        def _(sp):
            def cache_copy(q):
                sp.dma_start(
                    a_sample[:, bass.ds(q * COPY_ROWS, COPY_ROWS), :].rearrange("b r n -> r b n"),
                    cache_a[:, bass.ds(q * COPY_ROWS + DEC_SEQ, COPY_ROWS), :].rearrange("b r n -> r b n"),
                ).then_inc(S["copy_done"], 16)

            def load_unit(name, i, j, free=True):
                u0, n_tiles = FIRST[name], STAGE_TILES[name]
                slot = raw_slot(u0, j)
                if free:
                    sp.wait_ge(S["lo_ready"], u0 + i * 4 + j - 3)
                sp.dma_start(RAW[:, slot, 0:n_tiles, :],
                             w[name][bass.ds(i * 4 + j, 1)].rearrange("o p t n -> (o p) t n")
                             ).then_inc(raw_loaded[slot], 16)

            def load_stage(name, first, iters, copies=0, copy0=0):
                with sp.Fori(first, iters) as i:
                    for j in range(4):
                        load_unit(name, i, j)
                        if j < copies:
                            cache_copy(i * copies + (j + copy0))

            load_unit("wi1", 0, 0, free=False)
            for k in range(0, KD, 4):
                sp.dma_start(Y[:, k:k + 4, :], x_t[:, k:k + 4, :]).then_inc(x_in[k // 4], 16)
            load_unit("wi1", 0, 1, free=False)
            sp.dma_start(RELC[0:32, :], rel_bias).then_inc(S["setup_in"], 16)
            sp.dma_start(RELC[32:34, :], rel_rows).then_inc(S["setup_in"], 16)
            for t in range(4):
                sp.dma_start(RELREP[32 * t:32 * t + 32, :], rel_bias).then_inc(S["setup_in"], 16)
            sp.dma_start(CP[:], consts).then_inc(S["setup_in"], 16)
            sp.dma_start(TP[:], toeplitz).then_inc(S["setup_in"], 16)
            sp.dma_start(OH[:], onehots).then_inc(S["setup_in"], 16)
            sp.dma_start(LNC[:], patterns).then_inc(S["setup_in"], 16)
            sp.dma_start(MNEW[:], mask_new).then_inc(S["setup_in"], 16)
            for j in range(2, 4):
                load_unit("wi1", 0, j, free=False)
            sp.dma_start(LN[:], ln).then_inc(S["ln_in"], 16)
            sp.dma_start(KIDX_GB[:, 0, :], kidx_g.partition_broadcast(128)).then_inc(S["ln_in"], 16)
            sp.dma_start(KIDX_GB[:, 1, :], kidx_b.partition_broadcast(128)).then_inc(S["ln_in"], 16)
            sp.dma_start(PAGE_IDS[:], page_table.rearrange("b g -> (b g)").unsqueeze(0)).then_inc(S["ids_in"], 16)
            sp.wait_ge(S["rev_in"], 1)
            sp.dma_start(REV_DRAM, spread(REV[:], 1, REV_COPIES)).then_inc(S["rev_out"], 16)
            load_stage("wi1", 1, UP_ITERS, copies=2, copy0=-2)
            load_stage("wo1", 0, 4, copies=3, copy0=20)

            def load_idx_pages(g):
                if g == 0:
                    sp.wait_ge(S["ids_in"], 16)
                    sp.wait_ge(S["x_ready"], 2 * KD)
                if g >= 4:
                    sp.wait_ge(S["kp_t"], g - 3)
                for b in range(DEC_BATCH):
                    page = sp.value_load(PAGE_IDS[0:1, b * PAGES + g:b * PAGES + g + 1],
                                         min_val=0, max_val=cache_b.shape[0] - 1)
                    sp.dma_start(PG[:, g % 4, b, :],
                                 cache_b[bass.ds(page, 1), :, 2 * HD:3 * HD].rearrange("o p n -> (o p) n")
                                 ).then_inc(pg_in[g % 4], 16)

            for c in range(N_PROJ):
                load_unit("w_in", c // 4, c % 4)
                if 4 <= c < 8:
                    load_idx_pages(c - 4)
                elif 11 <= c < 7 + PAGES:
                    load_idx_pages(c - 7)
                if c == 3:
                    for q in range(32, 36):
                        cache_copy(q)
                elif 8 <= c < 11:
                    cache_copy(28 + c)
                elif c == 24:
                    sp.wait_ge(S["proj_a"], C_QA)
                    sp.wait_ge(S["proj_d"], C_QA)
                    sp.dma_start(kv_a_t.rearrange("c p n -> p c n"), PROJ[:, C_KA:C_KA + 12, 0:SEQ]
                                 ).then_inc(S["proj_out"], 16)
                    sp.dma_start(kv_b_t, PROJ[:, C_KV, :]).then_inc(S["proj_out"], 16)
            sp.dma_start(ki_b, KIN[:, :, 0:HD]).then_inc(S["proj_out"], 16)
            sp.wait_ge(S["tr_a"], 5)
            sp.wait_ge(S["tr_d"], 4)
            for b in range(DEC_BATCH):
                for kv, t in ((0, KNEW), (1, VNEW)):
                    sp.dma_start(a_sample[b, PAST - DEC_SEQ:PAST, kv * WIDTH_A:(kv + 1) * WIDTH_A],
                                 t[4 * b:4 * b + 4, :]).then_inc(S["new_rows_out"], 16)
            sp.wait_ge(S["unit_used"], FIRST["w_out"])

            def load_rows(n, kv):
                b, k = n // 7, n % 7
                if kv == 0:
                    dst, sem = AR[:, n % 4, :], ar_in[n % 4]
                    if n >= 4:
                        sp.wait_ge(S["ka_t"], n - 3)
                else:
                    dst, sem = AV[k], av_in[k]
                    if n >= 7:
                        sp.wait_ge(S["va_used"], n - 6)
                    elif n < 4:
                        sp.wait_ge(S["ka_t"], 53 + n)
                    else:
                        sp.wait_ge(S["ka_sc"], 56)
                cols = slice(kv * WIDTH_A, (kv + 1) * WIDTH_A)
                if k < STRIDED_BLOCKS:
                    src = cache_a[b, 512 * k:512 * k + 512, cols].rearrange("(j r) n -> j r n", r=16)[:, 0:4, :]
                else:
                    r0 = PAST - 512 + 128 * (k - STRIDED_BLOCKS)
                    src = cache_a[b, r0:r0 + 128, cols]
                sp.dma_start(dst, src).then_inc(sem, 16)

            for n in range(4):
                load_rows(n, 0)
            sp.wait_ge(S["lo_ready"], FIRST["w_out"])
            sp.dma_start(OHB[:], onehots[:, KEY_BLOCKS_A:24, :]).then_inc(S["oh_in"], 16)
            sp.wait_ge(S["proj_out"], 48)
            sp.wait_ge(S["new_rows_out"], 16 * 2 * DEC_BATCH)
            sp.wait_ge(S["o_sb"], 8)
            sp.dma_start(VN2[:], a_sample[:, PAST - DEC_SEQ:PAST, WIDTH_A:2 * WIDTH_A]).then_inc(S["vnew_in"], 16)
            page_at = 0
            for n in range(4, 56):
                load_rows(n, 0)
                while page_at < min(64, (5 * (n - 3) + 3) // 4):
                    load_kv_page(sp, 2 * page_at)
                    page_at += 1
            for n in range(7):
                load_rows(n, 1)
            sp.wait_ge(S["vb_all"], 1)
            for j in (0, 1):
                load_unit("w_out", 0, j, free=False)
            for n in range(7, 56):
                load_rows(n, 1)
            sp.wait_ge(S["b_logits"], 5)
            sp.wait_ge(S["va_used"], 56)
            for j in (2, 3):
                load_unit("w_out", 0, j, free=False)

            for j in range(4):
                load_unit("w_out", 1, j)
            load_stage("wi2", 0, UP_ITERS, copies=2, copy0=39)
            sp.dma_start(P_RAW[:], p_t).then_inc(S["p_in"], 16)
            load_stage("wo2", 0, 4, copies=3, copy0=61)
            load_stage("gate", 0, 2)
            for m in range(KD):
                sp.wait_ge(S["y_final"], m + 1)
                sp.dma_start(y_t[m], HF[:, m % 2, :]).then_inc(y_out[m % 2], 16)
            for s in y_out:
                sp.wait_ge(s, 16 * KD // 2)
            sp.wait_ge(S["proj_out"], 48)
            sp.wait_ge(S["new_rows_out"], 16 * 2 * DEC_BATCH)
            sp.wait_ge(S["copy_done"], 16 * N_COPIES)

        @block.gpsimd
        def _(pool):
            def rest(name, i, j):
                u0, tiles = FIRST[name], STAGE_TILES[name]
                slot, s = raw_slot(u0, j), (u0 + j) % 2
                pool.wait_ge(S["hi_ready"], u0 + i * 4 + j + 1)
                nc.gpsimd.tensor_tensor(WL[:, s, 0:tiles, :], RAW[:, slot, 0:tiles, :],
                                        WH[:, s, 0:tiles, :].bitcast(F32), ALU.subtract
                                        ).then_inc(S["lo_ready"], 1)

            def rests(name, first, iters):
                with pool.Fori(first, iters) as i:
                    for j in range(4):
                        rest(name, i, j)

            def x_rest(k, new):
                nc.gpsimd.tensor_tensor(XL[:, k, :], new, XH[:, k, :].bitcast(F32), ALU.subtract
                                        ).then_inc(S["x_ready"], 1)

            def ln_rest(which, nxt):
                for j in range(2):
                    rest(nxt, 0, j)
                for m in range(1, 4):
                    pool.wait_ge(S["squared"], KD * which + m + 1)
                    if m > 1:
                        pool.wait_ge(S["sq_added"], 3 * which + m - 1)
                    nc.gpsimd.tensor_tensor(SQ[:, 0, :], SQ[:, 0, :], SQ[:, m, :], ALU.add).then_inc(S["sq_added"], 1)
                for m in range(KD):
                    pool.wait_ge(S["xh_ln"], KD * which + m + 1)
                    pool.wait_ge(S["xn_done"], KD * which + m + 1)
                    x_rest(m, XN[:, m % 2, :])
                for j in range(2, 4):
                    rest(nxt, 0, j)

            nc.gpsimd.memset(ONES[:], 1.0 / D_MODEL).then_inc(S["ones_done"], 1)
            rest("wi1", 0, 0)
            for k in range(KD):
                pool.wait_ge(S["xh_ready"], k + 1)
                x_rest(k, Y[:, k, :])
            for j in range(1, 4):
                rest("wi1", 0, j)
            rests("wi1", 1, UP_ITERS)
            rests("wo1", 0, 4)
            ln_rest(0, "w_in")
            def causal(i):
                pool.wait_ge(S["ix_acc"], IDX_HEADS * i)
                d = MSK[:, i - 1, 128 * i:128 * i + 128]
                nc.gpsimd.affine_select(out=d, in_=d, compare_op=ALU.is_ge, fill=NEG, base=0,
                                        pattern=[[-1, 128]], channel_multiplier=1
                                        ).then_inc(S["ix_causal"], 1)

            pool.wait_ge(S["rev_out"], 16)

            def load_bias(h):
                for p in range(0, 128, REV_COPIES):
                    rows = bass.AP(REV_DRAM.tensor, 640 * REV_COPIES * h + 127 - p, [[639, REV_COPIES], [1, SEQ]])
                    pool.dma_start(TOE[p:p + REV_COPIES, h % 2, :], rows).then_inc(toe_in[h % 2], 16)

            for c in range(4, N_PROJ):
                rest("w_in", c // 4, c % 4)
                if c in (8, 9):
                    load_bias(c - 8)
                if c in (13, 16, 19):
                    causal((c - 10) // 3)

            def mask_bias(h, i):
                n = 3 * (h - HEADS_A) + i - 1
                if n == 0:
                    pool.wait_ge(S["topk_prompt_done"], 3)
                    pool.wait_ge(S["proj_out"], 48)
                pool.wait_ge(toe_in[h % 2], TOE_IN * (h // 2 + 1))
                if n >= 2:
                    hh, ii = HEADS_A + (n - 2) // 3, (n - 2) % 3 + 1
                    pool.wait_ge(S["logits_done"], 4 * hh + ii + 1)
                nk = 128 * (i + 1)
                nc.gpsimd.tensor_tensor(TM[:, n % 2, 0:nk], TOE[:, h % 2, SEQ - nk:SEQ],
                                        MSK[:, i - 1, 0:nk], ALU.add).then_inc(S["tm_done"], 1)

            for n in range(N_STEPS):
                h, i = n // 4, n % 4
                if i == 3 and h + 2 < HEADS_A + HEADS_B:
                    pool.wait_ge(S["logits_done"], 4 * (h + 1))
                    load_bias(h + 2)
                m = n + 2
                if 4 * HEADS_A <= m < N_STEPS and m % 4:
                    mask_bias(m // 4, m % 4)

            pool.wait_ge(S["ids_in"], 16)
            pool.wait_ge(S["proj_out"], 48)
            pool.wait_ge(S["o_sb"], 8)
            for q in range(1, DEC_BATCH * PAGES, 2):
                load_kv_page(pool, q)
            for g in range(PAGES):
                if g % 4 == 0:
                    for queue in range(2):
                        pool.wait_ge(kv_in[g // 4 + 4 * queue], 16 * 2 * DEC_BATCH)
                if g >= 2:
                    pool.wait_ge(S["kb_t"], g - 1)
                nc.gpsimd.tensor_copy(KC[g % 2][:, 0:4, :], KVP[:, DEC_BATCH * g:DEC_BATCH * g + 4, 0:HD]
                                      ).then_inc(S["kc_ready"], 1)

            for c in range(KD):
                pool.wait_ge(S["oh_ready"], c + 1)
                nc.gpsimd.tensor_tensor(OL_[:, c, 0:SEQ], OT[:, c, 0:SEQ], OH_[:, c, 0:SEQ].bitcast(F32), ALU.subtract
                                        ).then_inc(S["o_ready"], 1)
            rest("w_out", 0, 0)
            pool.wait_ge(S["o_tail"], 1)
            nc.gpsimd.tensor_tensor(OL_[:, :, SEQ:T], OT[:, :, SEQ:T], OH_[:, :, SEQ:T].bitcast(F32), ALU.subtract
                                    ).then_inc(S["o_ready"], 1)
            for j in range(1, 4):
                rest("w_out", 0, j)
            rests("w_out", 1, 2)
            ln_rest(1, "wi2")
            rests("wi2", 1, UP_ITERS)
            rests("wo2", 0, 4)
            ln_rest(2, "gate")
            rests("gate", 1, 2)

        @block.scalar
        def _(act):
            def high(u0, i, j, tiles):
                slot, s = raw_slot(u0, j), (u0 + j) % 2
                act.wait_ge(raw_loaded[slot], (i + (u0 + j) // 4) * 16 + 16)
                if not (isinstance(i, int) and u0 + 4 * i + j < 2):
                    act.wait_ge(S["unit_used"], u0 + i * 4 + j - 1)
                nc.scalar.activation(WH[:, s, 0:tiles, :], RAW[:, slot, 0:tiles, :], ACT.Copy
                                     ).then_inc(S["hi_ready"], 1)

            def high_of(u):
                high(u % 4, u // 4, 0, tiles_of(u))

            def up_stage(which):
                name = ("wi1", "wi2")[which]
                u0 = FIRST[name]

                def pair(i, split):
                    for s in range(2):
                        for j in (2 * s + 2, 2 * s + 3):
                            split(i, j)
                        if not (isinstance(i, int) and i == 0 and which == 0):
                            act.wait_ge(S["h_done"], 22 * which + i * 2 + s - 1)
                        act.wait_ge(S["unit_used"], u0 + i * 4 + 2 * s + 1)
                        for n in range(2):
                            last = nc.scalar.activation(half(SG, s, n), BANK[4 * s + n][:, 0:HALF], ACT.Silu)
                        last.then_inc(S["silu_done"], 1)

                pair(0, lambda i, j: high(u0, i, j, 8))
                with act.Fori(1, UP_ITERS - 1) as i:
                    pair(i, lambda i, j: high(u0, i, j, 8))
                pair(UP_ITERS - 1, lambda i, j: high_of(u0 + 4 * i + j))

            def layer_norm(which):
                act.wait_ge(S["mean_ps"], which + 1)
                for n, (a, b) in enumerate(HALVES):
                    last = nc.scalar.activation(MEAN[:, a:b], BANK[4 + n][:, 0:HALF], ACT.Copy)
                last.then_inc(S["mean_sb"], 1)
                for m in range(KD):
                    act.wait_ge(S["centred"], KD * which + m + 1)
                    nc.scalar.activation(SQ[:, m, :], Y[:, m, :], ACT.Square).then_inc(S["squared"], 1)
                act.wait_ge(S["var_sb"], which + 1)
                nc.scalar.activation(RSTD[:], RSTD[:], ACT.Sqrt).then_inc(S["std_sb"], 1)
                if which == 0:
                    act.wait_ge(S["ln_in"], 48)
                for m in range(KD):
                    act.wait_ge(S["zed"], KD * which + m + 1)
                    g, b = LN[:, 2 * which, m:m + 1], LN[:, 2 * which + 1, m:m + 1]
                    nc.scalar.activation(XH[:, m, :], Y[:, m, :], ACT.Identity, bias=b, scale=g
                                         ).then_inc(S["xh_ln"], 1)

            high_of(0)
            high_of(1)
            up_stage(0)
            for m in range(KD):
                high_of(FIRST["wo1"] + 2 * m + 2)
                high_of(FIRST["wo1"] + 2 * m + 3)
            layer_norm(0)

            def project(c):
                u0 = FIRST["w_in"]
                if c + 2 < N_PROJ:
                    high(u0, (c + 2) // 4, (c + 2) % 4, 8)
                act.wait_ge(S["unit_used"], u0 + c + 1)
                nc.scalar.activation(PROJ[:, c, 0:HALF], BANK[2 * (c % 2)][:, 0:HALF], ACT.Copy,
                                     scale=HD ** -0.5 if c >= C_QA else 1.0).then_inc(S["proj_a"], 1)

            def relu_prompt(n):
                nk = 128 * (n // IDX_HEADS + 2)
                act.wait_ge(S["ix_ps"], n + 1)
                if n >= 2:
                    act.wait_ge(S["ix_acc"], n - 1)
                nc.scalar.activation(RL[:, n % 2, 0:nk], BANK[5][:, 0:nk], ACT.Relu).then_inc(S["ix_relu"], 1)

            def relu_dec(g):
                act.wait_ge(S["kp_sc"], g + 1)
                if g >= 2:
                    act.wait_ge(S["kp_sum"], g - 1)
                nk = 128 if g < PAGES else NDEC
                src = BANK[6][:, 0:256].rearrange("p (a k) -> p a k", a=2)[:, :, 0:nk]
                nc.scalar.activation(RLD[:, g % 2, :, 0:nk], src, ACT.Relu).then_inc(S["kp_relu"], 1)

            def token_major(g):
                act.wait_ge(S["tr_ps"], g + 1)
                for dst, src in tr_copies(g):
                    last = nc.scalar.activation(dst, src, ACT.Copy)
                last.then_inc(S["tr_a"], 1)

            for c in range(7):
                project(c)
            act.wait_ge(S["ki_var"], 1)
            nc.scalar.activation(SMALL[:, 10:15], SMALL[:, 10:15], ACT.Sqrt).then_inc(S["ki_std"], 1)
            for c in range(7, IDX_FROM):
                project(c)
            act.wait_ge(S["kit_ps"], 1)
            nc.scalar.activation(KIT[:, 0:SEQ], BANK[5][:, 0:SEQ], ACT.Copy)
            nc.scalar.activation(KIT[:, SEQ:T], BANK[6][:, 0:32], ACT.Copy).then_inc(S["kit_sb"], 1)
            for s in range(PAGES + 3):
                if s < PAGES:
                    act.wait_ge(S["kp_t"], s + 1)
                    if s >= 2:
                        act.wait_ge(S["kp_sc"], s - 1)
                    nc.scalar.activation(KIPT[:, s % 2, :, :].rearrange("p a k -> p (a k)"), BANK[4][:, :],
                                         ACT.Copy).then_inc(S["kp_sb"], 1)
                if s < 8:
                    relu_prompt(3 * s)
                if 1 <= s < PAGES + 2:
                    relu_dec(s - 1)
                if s < 8:
                    relu_prompt(3 * s + 1)
                    relu_prompt(3 * s + 2)
                if 0 <= s - TR_FROM < TR_IN_SLOTS and (s - TR_FROM) % 2 == 0:
                    token_major(s - TR_FROM)
                if IDX_FROM + s < N_PROJ:
                    project(IDX_FROM + s)
            token_major(10)

            for n in range(N_STEPS + 3):
                if n < N_STEPS:
                    nk = 128 * (n % 4 + 1)
                    act.wait_ge(S["logits_done"], n + 1)
                    l = LP[n % 4][:, 0:nk]
                    nc.scalar.activation(l, l, ACT.Exp, bias=SMALL[:, 32 + n % 4:33 + n % 4], scale=-1.0,
                                         accum_out=SMALL[:, 36 + n % 4:37 + n % 4]).then_inc(S["exp_done"], 1)
                if n >= 3:
                    k = n - 3
                    nk = 128 * (k % 4 + 1)
                    act.wait_ge(S["pt_ps"], k + 1)
                    if k >= 2:
                        act.wait_ge(S["pv_done"], k - 1)
                    nc.scalar.activation(PTS[:, k % 2, 0:nk], BANK[2 + k % 2][:, 0:nk], ACT.Copy
                                         ).then_inc(S["pt_sb"], 1)
                if 1 <= n < N_STEPS + 1:
                    k = n - 1
                    act.wait_ge(S["den_done"], k + 1)
                    l = LP[k % 4][:, 0:128 * (k % 4 + 1)]
                    nc.scalar.activation(l, l, ACT.Copy, scale=SMALL[:, 40 + k % 4:41 + k % 4]).then_inc(S["probs_done"], 1)

            def exp_a(a):
                act.wait_ge(S["ka_logits"], a + 1)
                nc.scalar.activation(STA[:, a, :], STA[:, a, :], ACT.Exp, bias=SMALL[:, SM_MIN + a:SM_MIN + a + 1],
                                     scale=-1.0, accum_out=SMALL[:, SM_DEN + a:SM_DEN + a + 1]
                                     ).then_inc(S["expa_done"], 1)

            for n in range(56):
                act.wait_ge(S["ka_t"], n + 1)
                if n >= 2:
                    act.wait_ge(S["ka_sc"], n - 1)
                b0 = 2 * (n % 2)
                nc.scalar.activation(KTA[:, n % 2, 0:512], BANK[b0][:, :], ACT.Copy)
                nc.scalar.activation(KTA[:, n % 2, 512:768], BANK[b0 + 1][:, 0:256], ACT.Copy
                                     ).then_inc(S["ka_sb"], 1)
                if n >= 20 and (n - 20) % 14 == 0:
                    exp_a((n - 20) // 14)
            for g in range(PAGES):
                act.wait_ge(S["kb_t"], g + 1)
                if g >= 2:
                    act.wait_ge(S["kb_sc"], g - 1)
                nc.scalar.activation(KTB[:, g % 2, :], BANK[5 + g % 2][:, :], ACT.Copy).then_inc(S["kb_sb"], 1)
                if g == 2:
                    exp_a(3)
            act.wait_ge(S["b_max"], 1)
            for j in range(5):
                nk = 512 if j < 4 else NDEC
                last = nc.scalar.activation(STB[:, 512 * j:512 * j + nk], BANK[j][:, 0:nk], ACT.Exp,
                                            bias=SMALL[:, SM_BMAX + 5:SM_BMAX + 6], scale=1.0,
                                            accum_out=SMALL[:, SM_BSUM + j:SM_BSUM + j + 1])
            last.then_inc(S["b_exp"], 1)
            for i in range(0, N_PT, 2):
                act.wait_ge(S["pt_ps2"], i + 1)
                for dst, src in pt_copies(i):
                    last = nc.scalar.activation(dst, src, ACT.Copy)
                last.then_inc(S["pt_a"], 1)

            act.wait_ge(S["va_pair"], 4)
            act.wait_ge(S["vb_all"], 1)
            for j in range(2):
                high_of(FIRST["w_out"] + j)
            for m in range(KD):
                high_of(FIRST["w_out"] + m + 2)
            layer_norm(1)
            up_stage(1)
            for m in range(KD):
                high_of(FIRST["wo2"] + 2 * m + 2)
                high_of(FIRST["wo2"] + 2 * m + 3)
            layer_norm(2)
            for m in range(KD):
                if m < KD - 2:
                    high_of(FIRST["gate"] + m + 2)
                s = m % 2
                act.wait_ge(S["unit_used"], FIRST["gate"] + m + 1)
                if m >= 2:
                    act.wait_ge(S["y_final"], m - 1)
                for n in range(2):
                    last = nc.scalar.activation(half(SG, s, n), BANK[4 * s + n][:, 0:HALF], ACT.Sigmoid)
                last.then_inc(S["gate_sig"], 1)

        @block.vector
        def _(dve):
            own = Steps(dve, S["dve_step"])
            v = nc.vector

            for k in range(KD):
                if k % 4 == 0:
                    dve.wait_ge(x_in[k // 4], 16)
                v.tensor_copy(XH[:, k, :], Y[:, k, :]).then_inc(S["xh_ready"], 1)
            v.memset(RELA[:], 0.0)
            own.done(v.memset(RELB[:], 0.0))
            dve.wait_ge(S["setup_in"], 16 * 11)
            for t in range(4):
                rel = RELREP[32 * t:32 * t + 32, :]
                v.tensor_copy(RELA[32 * t:32 * t + 32, :, 0:HEADS_A, t], spread(rel[:, 0:HEADS_A], 1, 2))
                last = v.tensor_copy(RELB[32 * t:32 * t + 32, :, :, t], spread(rel[:, HEADS_A:16], 1, DEC_BATCH))
            last.then_inc(S["relt_done"], 1)
            dve.wait_ge(S["tables_ps"], 1)
            v.tensor_copy(REV[:, 0:512], BANK[6][0:16, :])
            v.tensor_copy(REV[:, 512:640], BANK[7][0:16, 0:128]).then_inc(S["rev_in"], 1)
            v.tensor_copy(BIAS_A[:, 0:512], BANK[4][:, :])
            v.tensor_copy(BIAS_A[:, 512:KEYS_A], BANK[5][:, 0:KEYS_A - 512])
            v.tensor_tensor(BIAS_N[:], spread(BANK[5][:, 384:416], 1, 4), MNEW[:], ALU.add).then_inc(S["tables_out"], 1)

            def up_stage(which):
                u0 = FIRST[("wi1", "wi2")[which]]
                with dve.Fori(0, UP_ITERS) as i:
                    for s in range(2):
                        done = i * 2 + (22 * which + s + 1)
                        c = i * 2 + s
                        dve.wait_ge(S["silu_done"], done)
                        dve.wait_ge(S["unit_used"], u0 + i * 4 + 2 * s + 2)
                        for n in range(2):
                            last = v.scalar_tensor_tensor(half(HF, s, n), half(SG, s, n), 0.5,
                                                          BANK[4 * s + 2 + n][:, 0:HALF], ALU.mult, ALU.mult)
                        last.then_inc(S["h_done"], 1)
                        dve.wait_ge(S["h_done"], done)
                        v.tensor_copy(HH[:, bass.ds(c, 1), :], HF[:, s:s + 1, :]).then_inc(S["hh_done"], 1)
                        dve.wait_ge(S["hh_done"], done)
                        v.tensor_tensor(HL[:, bass.ds(c, 1), :], HF[:, s:s + 1, :],
                                        HH[:, bass.ds(c, 1), :].bitcast(F32), ALU.subtract
                                        ).then_inc(S["hl_done"], 1)

            def down_stage(which):
                name = ("wo1", "w_out", "wo2")[which]
                u0, per = FIRST[name], (2, 1, 2)[which]
                own.done(v.memset(SUM[:], 0.0))
                with dve.Fori(0, KD // 2) as i:
                    for s in range(2):
                        done = i * 2 + (KD * which + s + 1)
                        m = i * 2 + s
                        dve.wait_ge(S["unit_used"], u0 + i * (2 * per) + per * (s + 1))
                        for n, (a, b) in enumerate(HALVES):
                            last = v.scalar_tensor_tensor(
                                Y[:, bass.ds(m, 1), a:b], XH[:, bass.ds(m, 1), a:b].bitcast(F32), ALPHA,
                                BANK[2 * s + n][:, 0:HALF].unsqueeze(1), ALU.mult, ALU.add)
                        last.then_inc(S["y_part"], 1)
                        dve.wait_ge(S["y_part"], done)
                        v.scalar_tensor_tensor(Y[:, bass.ds(m, 1), :], XL[:, bass.ds(m, 1), :].bitcast(F32), ALPHA,
                                               Y[:, bass.ds(m, 1), :], ALU.mult, ALU.add).then_inc(S["y_full"], 1)
                        dve.wait_ge(S["y_full"], done)
                        v.tensor_tensor(SUM[:].unsqueeze(1), SUM[:].unsqueeze(1), Y[:, bass.ds(m, 1), :], ALU.add
                                        ).then_inc(S["sum_done"], 1)
                        dve.wait_ge(S["sum_done"], done)

            def layer_norm(which):
                dve.wait_ge(S["mean_sb"], which + 1)
                for m in range(KD):
                    v.tensor_tensor(Y[:, m, :], Y[:, m, :], MEAN[:], ALU.subtract).then_inc(S["centred"], 1)
                dve.wait_ge(S["sq_used"], which + 1)
                for n, (a, b) in enumerate(HALVES):
                    last = v.tensor_scalar_add(RSTD[:, a:b], BANK[6 + n][:, 0:HALF], LN_EPS)
                last.then_inc(S["var_sb"], 1)
                dve.wait_ge(S["std_sb"], which + 1)
                own.done(v.reciprocal(RSTD[:], RSTD[:]))
                if which == 0:
                    dve.wait_ge(S["ln_in"], 48)
                for m in range(KD + 1):
                    if m < KD:
                        v.tensor_tensor(Y[:, m, :], Y[:, m, :], RSTD[:], ALU.mult).then_inc(S["zed"], 1)
                    if m >= 1:
                        k = m - 1
                        dve.wait_ge(S["zed"], KD * which + k + 1)
                        if k >= 2 or which:
                            dve.wait_ge(S["x_ready"], KD * (which + 1) + k - 1)
                        g, b = LN[:, 2 * which, k:k + 1], LN[:, 2 * which + 1, k:k + 1]
                        v.tensor_scalar(XN[:, k % 2, :], Y[:, k, :], g, b, ALU.mult, ALU.add).then_inc(S["xn_done"], 1)

            up_stage(0)
            dve.wait_ge(S["rev_out"], 16)
            down_stage(0)
            layer_norm(0)

            def project(c):
                dve.wait_ge(S["unit_used"], FIRST["w_in"] + c + 1)
                v.tensor_scalar_mul(PROJ[:, c, HALF:T], BANK[2 * (c % 2) + 1][:, 0:HALF],
                                    HD ** -0.5 if c >= C_QA else 1.0).then_inc(S["proj_d"], 1)

            for c in range(7):
                project(c)
            own.done(v.memset(KI0[:], 0.0))
            dve.wait_ge(S["kiw_ps"], 1)
            v.tensor_copy(KI0[:, 0:4, :].rearrange("p a n -> p (a n)"), BANK[4][:, 0:288])
            own.done(v.tensor_copy(KI0[0:32, 4, :], BANK[4][0:32, 288:360]))
            for k in range(5):
                last = v.bn_stats(SMALL[:, 16 + 6 * k:22 + 6 * k], KI0[:, k, 0:HD])
            own.done(last)
            for k in range(5):
                last = v.bn_aggr(SMALL[:, 2 * k:2 * k + 2], SMALL[:, 16 + 6 * k:22 + 6 * k])
            own.done(last)
            v.tensor_scalar_add(SMALL[:, 10:15], SMALL[:, 1:10:2], LN_EPS).then_inc(S["ki_var"], 1)
            dve.wait_ge(S["ki_std"], 1)
            own.done(v.reciprocal(SMALL[:, 10:15], SMALL[:, 10:15]))
            for k in range(5):
                last = v.tensor_scalar(KIN[:, k, 0:HD], KI0[:, k, 0:HD], SMALL[:, 2 * k:2 * k + 1],
                                       SMALL[:, 10 + k:11 + k], ALU.subtract, ALU.mult)
            own.done(last)
            own.done(v.tensor_tensor(KIN[:, :, 0:HD], KIN[:, :, 0:HD], spread(KIDX_GB[:, 0, :], 1, 5), ALU.mult))
            own.done(v.tensor_tensor(KIN[:, :, 0:HD], KIN[:, :, 0:HD], spread(KIDX_GB[:, 1, :], 1, 5), ALU.add))
            v.tensor_copy(KIN[:, :, HD:128], KIN[:, :, 0:HD]).then_inc(S["kin_done"], 1)
            own.done(v.tensor_scalar_mul(KI0[:, :, HD:HD + 8], KI0[:, :, HD:HD + 8], IDX_SCALE))
            own.done(v.memset(QIB[:], 0.0))
            for h2 in range(2):
                lo = slice(64 * h2, 64 * h2 + 64)
                for b2 in range(2):
                    up = slice(64 * b2, 64 * b2 + 64)
                    qi = PROJ[lo, C_QI:C_QI + 4, SEQ:T].rearrange("p c (a b t) -> p a c b t", b=2, t=4)[:, :, :, b2, :]
                    last = v.tensor_copy(QIB[up, :, :].rearrange("p a (b c h t) -> p a b c h t", b=2, c=4, h=2)
                                         [:, :, b2, :, h2, :], qi)
            last.then_inc(S["qblocks_done"], 1)
            for c in range(7, IDX_FROM):
                project(c)
            dve.wait_ge(S["wsel_ps"], 1)
            v.tensor_tensor(WB[:], spread(BANK[7][:, 0:32], 1, 2), WMASK, ALU.mult).then_inc(S["wsel_done"], 1)

            def index_sum(n):
                i, h = n // IDX_HEADS + 1, n % IDX_HEADS
                nk = 128 * (i + 1)
                dve.wait_ge(S["ix_relu"], n + 1)
                weight = KI0[:, i, HD + h:HD + h + 1]
                if h == 0:
                    last = v.tensor_scalar_mul(MSK[:, i - 1, 0:nk], RL[:, n % 2, 0:nk], weight)
                else:
                    dve.wait_ge(S["ix_acc"], n)
                    last = v.scalar_tensor_tensor(MSK[:, i - 1, 0:nk], RL[:, n % 2, 0:nk], weight,
                                                  MSK[:, i - 1, 0:nk], ALU.mult, ALU.add)
                last.then_inc(S["ix_acc"], 1)

            def index_row(g):
                dve.wait_ge(S["kp_sum"], g + 1)
                if g < PAGES:
                    last = v.tensor_copy(SC[:, 128 * g:128 * g + 128], BANK[7][0:32, 0:128])
                else:
                    last = v.tensor_tensor(SC[:, PAST:PAST + NDEC], BANK[7][0:32, 0:NDEC], MASK_NEW_IX, ALU.add)
                last.then_inc(S["kp_row"], 1)

            def take_eight(scores, top):
                own.done(v.max(top, scores))
                own.done(v.match_replace(scores, top, scores, TAKEN))

            def taken_to_mask(scores):
                return v.tensor_scalar(scores, scores, TAKEN_LIMIT, NEG, ALU.is_ge, ALU.mult)

            def prompt_round(n):
                b, first = n // (TOPK_PROMPT // 8), n % (TOPK_PROMPT // 8) == 0
                if first:
                    dve.wait_ge(S["ix_causal"], b + 1)
                scores = MSK[:, b, 0:128 * (b + 2)]
                take_eight(scores, SMALL[:, 16:24])
                if n % (TOPK_PROMPT // 8) == TOPK_PROMPT // 8 - 1:
                    taken_to_mask(scores).then_inc(S["topk_prompt_done"], 1)

            def token_major(g):
                dve.wait_ge(S["tr_ps"], g + 1)
                for dst, src in tr_copies(g):
                    last = v.tensor_copy(dst, src)
                last.then_inc(S["tr_d"], 1)

            PROMPT_ROUNDS = [0, 0, 0, 0, 5, 6, 5, 4, 4, 4, 4, 4, 4, 4, 4]
            rounds = 0
            for s in range(PAGES + 3):
                if s >= 2:
                    index_row(s - 2)
                if s < 8:
                    for n in range(3 * s, 3 * s + 3):
                        index_sum(n)
                if IDX_FROM + s < N_PROJ:
                    project(IDX_FROM + s)
                if 0 <= s - TR_FROM < TR_IN_SLOTS and (s - TR_FROM) % 2:
                    token_major(s - TR_FROM)
                for _ in range(PROMPT_ROUNDS[s] if s < len(PROMPT_ROUNDS) else 0):
                    prompt_round(rounds)
                    rounds += 1
            token_major(9)
            v.tensor_copy(KB2[0:64, SEQ:T], PROJ[0:64, C_KV, SEQ:T])
            v.tensor_copy(KB2[64:128, :], PROJ[0:64, C_KV, :]).then_inc(S["kb2_done"], 1)

            def decode_queries():
                dve.wait_ge(S["lo_ready"], FIRST["w_out"])
                v.memset(QBLKA[:], 0.0)
                own.done(v.memset(QBLKB[:], 0.0))
                v.tensor_copy(KNT[:], PROJ[:, C_KA:C_KA + 6, SEQ:T])
                for h2 in range(2):
                    lo = slice(64 * h2, 64 * h2 + 64)
                    for c in range(6):
                        col = 8 * c + 4 * h2
                        v.tensor_copy(QBLKA[lo, c, 0:384].rearrange("p (b r) -> p b r", b=DEC_BATCH)[:, :, col:col + 4],
                                      PROJ[lo, C_QA + c, SEQ:T].rearrange("p (b t) -> p b t", t=4))
                    for b2 in range(2):
                        up = slice(64 * b2, 64 * b2 + 64)
                        qb = PROJ[lo, C_QB:C_QB + 2, SEQ:T].rearrange("p c (a b t) -> p a c b t", b=2, t=4)[:, :, :, b2, :]
                        last = v.tensor_copy(QBLKB[up, :, :].rearrange("p a (b c h t) -> p a b c h t", b=2, c=2, h=2)
                                             [:, :, b2, :, h2, :], qb)
                last.then_inc(S["qblocks_done"], 1)

            def invert(n):
                dve.wait_ge(S["exp_done"], n + 1)
                c = n % 4
                v.reciprocal(SMALL[:, 40 + c:41 + c], SMALL[:, 36 + c:37 + c]).then_inc(S["den_done"], 1)

            def take_out(q):
                dve.wait_ge(S["pv_done"], 8 * q + 8)
                v.tensor_copy(OT[:, q, 0:SEQ], BANK[4 + q % 2][:, :]).then_inc(S["o_sb"], 1)

            dec_rounds = 0
            for n in range(N_STEPS):
                h, i = n // 4, n % 4
                nk = 128 * (i + 1)
                dve.wait_ge(S["sc_ps"], n + 1)
                if n >= 4:
                    dve.wait_ge(S["pt_ps"], n - 3)
                if h < HEADS_A or i == 0:
                    dve.wait_ge(toe_in[h % 2], TOE_IN * (h // 2 + 1))
                    bias = TOE[:, h % 2, SEQ - nk:SEQ]
                else:
                    t = 3 * (h - HEADS_A) + i - 1
                    dve.wait_ge(S["tm_done"], t + 1)
                    bias = TM[:, t % 2, 0:nk]
                v.tensor_tensor_reduce(out=LP[n % 4][:, 0:nk], in0=SCORE_BANK[n % 4][:, 0:nk], in1=bias, scale=-1.0,
                                       scalar=3.0e38, op0=ALU.add, op1=ALU.min,
                                       accum_out=SMALL[:, 32 + i:33 + i]).then_inc(S["logits_done"], 1)
                if n >= 1:
                    invert(n - 1)
                if n == 12:
                    dve.wait_ge(S["new_rows_out"], 16 * 2 * DEC_BATCH)
                if n >= 12 and (n - 12) % 8 == 0:
                    take_out((n - 12) // 8)
                if n % 4 == 0:
                    own.done(v.max(SMALL[0:32, 24:32], SC[:]))
                elif n % 4 == 2:
                    own.done(v.match_replace(SC[:], SMALL[0:32, 24:32], SC[:], TAKEN))
                    dec_rounds += 1
                if n == 20:
                    decode_queries()
            invert(N_STEPS - 1)
            take_out(7)

            for a in range(4):
                while dec_rounds < TOPK_DEC // 8 - 4 * (3 - a):
                    take_eight(SC[:], SMALL[0:32, 24:32])
                    dec_rounds += 1
                if a == 3:
                    taken_to_mask(SC[:]).then_inc(S["topk_dec_done"], 1)
                dve.wait_ge(S["ka_sc"], 14 * (a + 1))
                lo_bank, hi_bank = BANK[4 + 2 * (a % 2)], BANK[5 + 2 * (a % 2)]
                for j, (src, bias, c0, c1) in enumerate((
                        (lo_bank[:, :], BIAS_A[:, 0:512], 0, 512),
                        (hi_bank[:, 0:384], BIAS_A[:, 512:KEYS_A], 512, KEYS_A),
                        (hi_bank[:, 384:416], BIAS_N[:, a, :], KEYS_A, ALL_A))):
                    last = v.tensor_tensor_reduce(out=STA[:, a, c0:c1], in0=src, in1=bias, scale=-1.0,
                                                  scalar=3.0e38, op0=ALU.add, op1=ALU.min,
                                                  accum_out=SMALL[:, SM_MINS + 3 * a + j:SM_MINS + 3 * a + j + 1])
                own.done(last)
                v.tensor_reduce(SMALL[:, SM_MIN + a:SM_MIN + a + 1], SMALL[:, SM_MINS + 3 * a:SM_MINS + 3 * a + 3],
                                AX.X, ALU.min).then_inc(S["ka_logits"], 1)
            for g in range(PAGES):
                if g % 4 == 0:
                    for queue in range(2):
                        dve.wait_ge(kv_in[g // 4 + 4 * queue], 16 * 2 * DEC_BATCH)
                if g >= 2:
                    dve.wait_ge(S["kb_t"], g - 1)
                v.tensor_copy(KC[g % 2][:, 4:8, :], KVP[:, DEC_BATCH * g + 4:DEC_BATCH * g + 8, 0:HD]
                              ).then_inc(S["kc_ready_d"], 1)
            dve.wait_ge(S["expa_done"], 4)
            own.done(v.reciprocal(SMALL[:, SM_DEN:SM_DEN + 4], SMALL[:, SM_DEN:SM_DEN + 4]))
            for j in range(5):
                nk = 512 if j < 4 else NDEC
                dve.wait_ge(S["b_logits"], j + 1)
                last = v.tensor_reduce(SMALL[:, SM_BMAX + j:SM_BMAX + j + 1], BANK[j][:, 0:nk], AX.X, ALU.max)
            own.done(last)
            own.done(v.tensor_reduce(SMALL[:, SM_BMAX + 5:SM_BMAX + 6], SMALL[:, SM_BMAX:SM_BMAX + 5], AX.X, ALU.max))
            v.tensor_scalar_mul(SMALL[:, SM_BMAX + 5:SM_BMAX + 6], SMALL[:, SM_BMAX + 5:SM_BMAX + 6], -1.0
                                ).then_inc(S["b_max"], 1)
            dve.wait_ge(S["b_exp"], 1)
            own.done(v.tensor_reduce(SMALL[:, SM_BMAX:SM_BMAX + 1], SMALL[:, SM_BSUM:SM_BSUM + 5], AX.X, ALU.add))
            own.done(v.reciprocal(SMALL[:, SM_BMAX:SM_BMAX + 1], SMALL[:, SM_BMAX:SM_BMAX + 1]))

            def pt_out(i):
                dve.wait_ge(S["pt_ps2"], i + 1)
                for dst, src in pt_copies(i):
                    last = v.tensor_copy(dst, src)
                last.then_inc(S["pt_d"], 1)

            for i in (1, 3, 5):
                pt_out(i)
            dve.wait_ge(S["vb_all"], 1)
            v.tensor_scalar_mul(OB[:], BANK[7][:, 0:128], SMALL[:, SM_BMAX:SM_BMAX + 1]).then_inc(S["ob_sb"], 1)
            dve.wait_ge(S["ob_t"], 1)
            for b2 in range(2):
                up = slice(64 * b2, 64 * b2 + 64)
                for h2 in range(2):
                    lo = slice(64 * h2, 64 * h2 + 64)
                    last = v.tensor_copy(
                        OT[lo, 6:8, SEQ:T].rearrange("p c (a b t) -> p c a b t", b=2, t=4)[:, :, :, b2, :],
                        BANK[4][up, 0:128].rearrange("p (a b c h t) -> p c a b h t", a=4, b=2, c=2, h=2)[:, :, :, b2, h2, :])
            last.then_inc(S["ot_done"], 1)
            for c in range(KD):
                v.tensor_copy(OH_[:, c, 0:SEQ], OT[:, c, 0:SEQ]).then_inc(S["oh_ready"], 1)
            pt_out(7)
            for a in range(4):
                if a < 3:
                    if a > 0:
                        pt_out(7 + 2 * a)
                dve.wait_ge(S["va_pair"], a + 1)
                if a > 0:
                    dve.wait_ge(S["ob_t"], a + 1)
                rden = SMALL[:, SM_DEN + a:SM_DEN + a + 1]
                v.tensor_scalar_mul(OA[:, 0:384], BANK[2 * (a % 2)][:, 0:384], rden)
                v.tensor_scalar_mul(OA[:, 384:768], BANK[2 * (a % 2) + 1][:, 0:384], rden).then_inc(S["oa_sb"], 1)
                dve.wait_ge(S["ob_t"], a + 2)
                for c in range(6):
                    bank, col = (BANK[7], 128 * c) if c < 4 else (BANK[4], 128 * (c - 4))
                    for h2 in range(2):
                        lo = slice(64 * h2, 64 * h2 + 64)
                        q = 8 * c + 4 * h2
                        last = v.tensor_copy(OT[lo, c, SEQ + 8 * a:SEQ + 8 * a + 8].rearrange("p (b t) -> p b t", t=4),
                                             bank[lo, col:col + 128].rearrange("p (b r) -> p b r", b=2)[:, :, q:q + 4])
                last.then_inc(S["ot_done"], 1)
            dve.wait_ge(S["ot_done"], 5)
            v.tensor_copy(OH_[:, :, SEQ:T], OT[:, :, SEQ:T]).then_inc(S["o_tail"], 1)
            dve.wait_ge(S["o_ready"], KD + 1)

            down_stage(1)
            layer_norm(1)
            up_stage(1)
            dve.wait_ge(S["p_in"], 16)
            own.done(v.tensor_copy(PH[:], P_RAW[:]))
            own.done(v.tensor_tensor(PL[:], P_RAW[:], PH[:].bitcast(F32), ALU.subtract))
            down_stage(2)
            layer_norm(2)
            for m in range(KD):
                s = m % 2
                dve.wait_ge(S["gate_sig"], m + 1)
                if m >= 2:
                    dve.wait_ge(y_out[s], 16 * (m // 2))
                for n in range(2):
                    last = v.tensor_tensor(half(HF, s, n), half(SG, s, n), BANK[4 * s + 2 + n][:, 0:HALF], ALU.mult)
                own.done(last)
                own.done(v.tensor_tensor(HF[:, s, :], HF[:, s, :], XH[:, m, :].bitcast(F32), ALU.add))
                v.tensor_tensor(HF[:, s, :], HF[:, s, :], XL[:, m, :].bitcast(F32), ALU.add).then_inc(S["y_final"], 1)

        @block.tensor
        def _(pe):
            mm = nc.tensor.matmul

            def tile(banks, s, j, xh, xl, start, stop):
                wh, wl = WH[:, s, j, :], WL[:, s, j, :]
                for n in range(2):
                    mm(banks[n][:, 0:HALF], wh, xh[n], start=start, stop=False)
                for n in range(2):
                    mm(banks[n][:, 0:HALF], wh, xl[n], start=False, stop=False)
                for n in range(2):
                    last = mm(banks[n][:, 0:HALF], wl, xh[n], start=False, stop=stop)
                return last

            def unit(u0, i, j, banks, high, low, k0, count, first, last_tile, ready=None, between=None):
                s = (u0 + j) % 2
                pe.wait_ge(S["lo_ready"], u0 + i * 4 + j + 1)
                for t in range(count):
                    if ready is not None:
                        pe.wait_ge(S["x_ready"], ready + t + 1)
                    k = k0 + t
                    last = tile(banks, s, t, [half(high, k, n) for n in range(2)], [half(low, k, n) for n in range(2)],
                                first and t == 0, last_tile and t == count - 1)
                    if between is not None and t < count - 1:
                        between(t)
                return last

            def up_stage(which):
                u0 = FIRST[("wi1", "wi2")[which]]

                def pair(i, ready=None):
                    for s in range(2):
                        if not (isinstance(i, int) and i == 0 and which == 0):
                            pe.wait_ge(S["h_done"], 22 * which + i * 2 + s - 1)
                        if isinstance(i, int) and which == 0 and s == 1:
                            pe.wait_ge(S["tables_out"], 1)
                        for j in (2 * s, 2 * s + 1):
                            banks = BANK[4 * s + 2 * (j % 2):4 * s + 2 * (j % 2) + 2]
                            unit(u0, i, j, banks, XH, XL, 0, KD, True, True, ready if j == 0 else None
                                 ).then_inc(S["unit_used"], 1)
                            if isinstance(i, int) and which == 0 and j == 0:
                                bias_tables()

                pair(0, ready=KD * 2 * which)
                with pe.Fori(1, UP_ITERS) as i:
                    pair(i)

            def down_stage(which):
                name, order = ("wo1", "wo2")[which], (0, 2)[which]
                u0 = FIRST[name]
                pe.wait_ge(S["hl_done"], KF * (which + 1) - 1)

                def last_chunk(t):
                    if t == UNIT_TILES - 2:
                        pe.wait_ge(S["hl_done"], KF * (which + 1))

                def pair(i):
                    for s in range(2):
                        if not (isinstance(i, int) and i == 0 and which == 0):
                            pe.wait_ge(S["y_part"], KD * order + i * 2 + s - 1)
                        for part in range(2):
                            unit(u0, i, 2 * s + part, BANK[2 * s:2 * s + 2], HH, HL, UNIT_TILES * part, UNIT_TILES,
                                 part == 0, part == 1,
                                 between=last_chunk if isinstance(i, int) and s == 0 and part == 1 else None
                                 ).then_inc(S["unit_used"], 1)

                pair(0)
                with pe.Fori(1, KD // 2) as i:
                    pair(i)

            def layer_norm(which):
                if which == 0:
                    pe.wait_ge(S["ones_done"], 1)
                pe.wait_ge(S["sum_done"], KD * (which + 1))
                for n, (a, b) in enumerate(HALVES):
                    last = mm(BANK[4 + n][:, 0:HALF], ONES[:], SUM[:, a:b], start=True, stop=True)
                last.then_inc(S["mean_ps"], 1)
                order = [4, 5, 6, 0, 7]
                for m in order:
                    if m == 0:
                        pe.wait_ge(S["sq_added"], 3 * (which + 1))
                    else:
                        pe.wait_ge(S["squared"], KD * which + m + 1)
                    for n in range(2):
                        last = mm(BANK[6 + n][:, 0:HALF], ONES[:], half(SQ, m, n), start=m == order[0], stop=m == order[-1])
                last.then_inc(S["sq_used"], 1)

            def bias_tables():
                pe.wait_ge(S["setup_in"], 16 * 11)
                mm(BANK[6][0:16, :], RELC[:], TP[:, 0:512], start=True, stop=True)
                mm(BANK[7][0:16, 0:128], RELC[:], TP[:, 512:640], start=True, stop=True)
                pe.wait_ge(S["relt_done"], 1)
                rela = RELA[:].rearrange("p b h t -> p (b h t)")
                for bank, c0, c1 in ((BANK[4], 0, 512), (BANK[5], 512, KEYS_A)):
                    mm(bank[:, 0:c1 - c0], rela, OH[:].rearrange("p k n -> p (k n)")[:, c0:c1], start=True, stop=False)
                    mm(bank[:, 0:c1 - c0], LNC[:, KEYS_A:1024], LNC[:, c0:c1], start=False, stop=True)
                mm(BANK[5][:, 384:416], rela, OH[:, BLK_NEW, 0:32], start=True, stop=True).then_inc(S["tables_ps"], 1)

            up_stage(0)
            down_stage(0)
            layer_norm(0)

            def project(c, ready=None, between=None):
                if c >= 2:
                    pe.wait_ge(S["proj_a"], c - 1)
                    pe.wait_ge(S["proj_d"], c - 1)
                unit(FIRST["w_in"], c // 4, c % 4, BANK[2 * (c % 2):2 * (c % 2) + 2], XH, XL, 0, KD, True, True,
                     ready, between).then_inc(S["unit_used"], 1)

            tr = nc.tensor.transpose
            for c in range(7):
                project(c, ready=KD if c == 0 else None)
            pe.wait_ge(S["proj_a"], C_IDX + 1)
            pe.wait_ge(S["proj_d"], C_IDX + 1)
            for k in range(5):
                n = 128 if k < 4 else NDEC
                last = tr(BANK[4][0:n, 72 * k:72 * k + 72], PROJ[0:72, C_IDX, 128 * k:128 * k + n], IDENT[0:72, 0:72])
            last.then_inc(S["kiw_ps"], 1)
            mm(BANK[7][:, 0:32], SEL_HEAD, PROJ[64:72, C_IDX, SEQ:T], start=True, stop=True).then_inc(S["wsel_ps"], 1)
            for c in range(7, IDX_FROM):
                project(c)
            pe.wait_ge(S["kin_done"], 1)
            for k in range(4):
                tr(BANK[5][:, 128 * k:128 * k + 128], KIN[:, k, :], IDENT)
            tr(BANK[6][:, 0:32], KIN[0:32, 4, :], IDENT[0:32, 0:32]).then_inc(S["kit_ps"], 1)
            pe.wait_ge(S["wsel_done"], 1)
            pe.wait_ge(S["qblocks_done"], 1)
            pe.wait_ge(S["kit_sb"], 1)

            def index_prompt(n):
                i, h = n // IDX_HEADS + 1, n % IDX_HEADS
                nk = 128 * (i + 1)
                if n >= 1:
                    pe.wait_ge(S["ix_relu"], n)
                lo = slice(64 * (h % 2), 64 * (h % 2) + 64)
                mm(BANK[5][:, 0:nk], PROJ[lo, C_QI + h // 2, 128 * i:128 * i + 128], KIT[lo, 0:nk],
                   start=True, stop=True).then_inc(S["ix_ps"], 1)

            def index_transposes(g):
                pe.wait_ge(pg_in[g % 4], 128 * (g // 4 + 1))
                if g >= 1:
                    pe.wait_ge(S["kp_sb"], g)
                for p in range(4):
                    last = tr(BANK[4][:, 128 * p:128 * p + 128],
                              PG[:, g % 4, 2 * p:2 * p + 2, :].rearrange("p b n -> p (b n)"), IDENT)
                last.then_inc(S["kp_t"], 1)

            def index_scores(g):
                if g < PAGES:
                    pe.wait_ge(S["kp_sb"], g + 1)
                if g >= 1:
                    pe.wait_ge(S["kp_relu"], g)
                nk = 128 if g < PAGES else NDEC
                for p in range(4):
                    keys = KIPT[:, g % 2, p, :] if g < PAGES else KIT[:, SEQ:T]
                    last = mm(BANK[6][64 * (p % 2):64 * (p % 2) + 64, 128 * (p // 2):128 * (p // 2) + nk],
                              QIB[:, p, :], keys, start=True, stop=True)
                last.then_inc(S["kp_sc"], 1)

            def index_sum(g):
                pe.wait_ge(S["kp_relu"], g + 1)
                if g >= 1:
                    pe.wait_ge(S["kp_row"], g)
                nk = 128 if g < PAGES else NDEC
                for a in range(2):
                    last = mm(BANK[7][0:32, 0:nk], WB[:, a, :], RLD[:, g % 2, a, 0:nk], start=a == 0, stop=a == 1)
                last.then_inc(S["kp_sum"], 1)

            def token_major(g):
                if g == 0:
                    pe.wait_ge(S["ix_relu"], 3 * IDX_HEADS)
                elif g < TR_IN_SLOTS:
                    pe.wait_ge(S["tr_a"] if g % 2 else S["tr_d"], (g + 1) // 2)
                if g == 1:
                    pe.wait_ge(S["proj_a"], C_VA + 6)
                    pe.wait_ge(S["proj_d"], C_VA + 6)
                for q in range(4):
                    if g < 6:
                        blk, c = (4 * g + q) // 6, (4 * g + q) % 6
                        src, n = PROJ[:, C_VA + c, 128 * blk:128 * blk + 128], 128
                    elif g < 9:
                        src, n = PROJ[:, C_KA + 4 * (g - 6) + q, SEQ:T], NDEC
                    elif g == 9:
                        src, n = PROJ[:, C_KV, 128 * q:128 * q + 128], 128
                    elif q == 0:
                        src, n = PROJ[:, C_KV, SEQ:T], NDEC
                    else:
                        break
                    last = tr(tr_bank(g)[0:n, 128 * q:128 * q + 128], src, IDENT)
                last.then_inc(S["tr_ps"], 1)

            for s in range(PAGES + 3):
                def between(t):
                    if t == 0 and s >= 2:
                        index_sum(s - 2)
                    if t == 3 and 1 <= s < PAGES + 2:
                        index_scores(s - 1)
                    if t in (1, 4, 6) and s < 8:
                        index_prompt(3 * s + (1, 4, 6).index(t))
                    if t == 5 and 0 <= s - TR_FROM < TR_IN_SLOTS:
                        token_major(s - TR_FROM)

                if s < PAGES:
                    index_transposes(s)
                if IDX_FROM + s < N_PROJ:
                    project(IDX_FROM + s, between=between)
                else:
                    for t in range(KD - 1):
                        between(t)

            pe.wait_ge(S["proj_a"], N_PROJ)
            pe.wait_ge(S["proj_d"], N_PROJ)
            pe.wait_ge(S["kp_row"], PAGES + 1)
            token_major(9)
            token_major(10)
            pe.wait_ge(S["tr_a"], 6)
            pe.wait_ge(S["tr_d"], 5)
            pe.wait_ge(S["kb2_done"], 1)

            def scores(n):
                h, i = n // 4, n % 4
                if n >= 4:
                    pe.wait_ge(S["logits_done"], n - 3)
                nk = 128 * (i + 1)
                base = 64 * (h % 2)
                lo = slice(base, base + 64)
                if h < HEADS_A:
                    keys = PROJ[lo, C_KA + h // 2, 0:nk]
                else:
                    keys = KB2[lo, 0:nk] if base else PROJ[lo, C_KV, 0:nk]
                mm(SCORE_BANK[n % 4][:, 0:nk], PROJ[lo, C_QA + h // 2, 128 * i:128 * i + 128], keys,
                   start=True, stop=True).then_inc(S["sc_ps"], 1)

            def transposed(n):
                pe.wait_ge(S["probs_done"], n + 1)
                if n >= 2:
                    pe.wait_ge(S["pt_sb"], n - 1)
                for j in range(n % 4 + 1):
                    last = tr(BANK[2 + n % 2][:, 128 * j:128 * j + 128], LP[n % 4][:, 128 * j:128 * j + 128], IDENT)
                last.then_inc(S["pt_ps"], 1)

            def values(n):
                h, i = n // 4, n % 4
                q, base = h // 2, 64 * (h % 2)
                if n % 8 == 0 and q >= 2:
                    pe.wait_ge(S["o_sb"], q - 1)
                pe.wait_ge(S["pt_sb"], n + 1)
                for j in range(i + 1):
                    val = VP[:, j, 64 * h:64 * h + 64] if h < HEADS_A else VBT[:, j, HD:128]
                    last = mm(BANK[4 + q % 2][base:base + 64, 128 * i:128 * i + 128], val,
                              PTS[:, n % 2, 128 * j:128 * j + 128], start=j == 0, stop=j == i)
                last.then_inc(S["pv_done"], 1)

            for n in range(N_STEPS + 4):
                if n < N_STEPS:
                    scores(n)
                if 3 <= n < N_STEPS + 3:
                    transposed(n - 3)
                if n >= 4:
                    values(n - 4)

            pe.wait_ge(S["o_sb"], 8)
            pe.wait_ge(S["qblocks_done"], 2)

            def key_scores_a(n):
                b, k = n // 7, n % 7
                a, rows = b // 2, slice(64 * (b % 2), 64 * (b % 2) + 64)
                banks = BANK[4 + 2 * (a % 2):6 + 2 * (a % 2)]
                pe.wait_ge(S["ka_sb"], n + 1)
                if k == 0 and b % 2 == 0 and a >= 2:
                    pe.wait_ge(S["ka_logits"], a - 1)
                for c in range(6):
                    last = mm(banks[k // 4][rows, 128 * (k % 4):128 * (k % 4) + 128], QBLKA[:, c, 48 * b:48 * b + 64],
                              KTA[:, n % 2, 128 * c:128 * c + 128], start=c == 0, stop=c == 5)
                if k == 6:
                    for c in range(6):
                        last = mm(banks[1][rows, 384:416], QBLKA[:, c, 48 * b:48 * b + 64], KNT[:, c, :],
                                  start=c == 0, stop=c == 5)
                last.then_inc(S["ka_sc"], 1)

            for n in range(57):
                if n < 56:
                    pe.wait_ge(ar_in[n % 4], 16 * (n // 4 + 1))
                    if n >= 2:
                        pe.wait_ge(S["ka_sb"], n - 1)
                    for c in range(6):
                        last = tr(BANK[2 * (n % 2) + c // 4][:, 128 * (c % 4):128 * (c % 4) + 128],
                                  AR[:, n % 4, 128 * c:128 * c + 128], IDENT)
                    last.then_inc(S["ka_t"], 1)
                if n >= 1:
                    key_scores_a(n - 1)

            pe.wait_ge(S["oh_in"], 16)
            relb = RELB[:].rearrange("p b h t -> p (b h t)")
            for j in range(5):
                nk = 512 if j < 4 else NDEC
                if j == 4:
                    pe.wait_ge(S["ka_logits"], 3)
                mm(BANK[j][:, 0:nk], relb, OHB[:].rearrange("p k n -> p (k n)")[:, 512 * j:512 * j + nk],
                   start=True, stop=False, skip_group_check=True)
            mm(BANK[4][:, 0:32], QBLKB[:].rearrange("p a n -> p (a n)"), KB2[:, SEQ:T], start=False, stop=False,
               skip_group_check=True)
            for g in range(PAGES + 1):
                if g < PAGES:
                    pe.wait_ge(S["kc_ready"], g + 1)
                    pe.wait_ge(S["kc_ready_d"], g + 1)
                    if g < 2:
                        pe.wait_ge(S["ka_logits"], 3 + g)
                    else:
                        pe.wait_ge(S["kb_sb"], g - 1)
                    for p in range(4):
                        last = tr(BANK[5 + g % 2][:, 128 * p:128 * p + 128],
                                  KC[g % 2][:, 2 * p:2 * p + 2, :].rearrange("p b n -> p (b n)"), IDENT)
                    last.then_inc(S["kb_t"], 1)
                if g >= 1:
                    m = g - 1
                    pe.wait_ge(S["kb_sb"], m + 1)
                    for p in range(4):
                        last = mm(BANK[m // 4][32 * p:32 * p + 32, 128 * (m % 4):128 * (m % 4) + 128], QBLKB[:, p, :],
                                  KTB[:, m % 2, 128 * p:128 * p + 128], start=False, stop=False, skip_group_check=True)
                    last.then_inc(S["kb_sc"], 1)
            pe.wait_ge(S["topk_dec_done"], 1)
            for j in range(5):
                nk = 512 if j < 4 else NDEC
                mm(BANK[j][:, 0:nk], SEL_QUERY, SC[:, 512 * j:512 * j + nk], start=False, stop=True,
                   skip_group_check=True).then_inc(S["b_logits"], 1)

            def pt_transposes(i):
                which, q, part = pt_group(i)
                if i >= 2:
                    pe.wait_ge(S["pt_a"] if i % 2 == 0 else S["pt_d"], i // 2)
                if which == "a":
                    pe.wait_ge(S["expa_done"], q + 1)
                for j in range(4 if which == "a" or q < 4 else 1):
                    k = 4 * (part if which == "a" else q) + j
                    n = 128
                    if which == "a":
                        c0 = 128 * k
                        if k == 7:
                            n = NDEC
                        src = STA[:, q, c0:c0 + n]
                    else:
                        if k == 16:
                            n = NDEC
                        src = STB[:, 128 * k:128 * k + n]
                    last = tr(BANK[5 + i % 2][0:n, 128 * j:128 * j + 128], src, IDENT)
                last.then_inc(S["pt_ps2"], 1)

            pe.wait_ge(S["kb_sb"], PAGES)
            for i in range(2):
                pt_transposes(i)
            pe.wait_ge(S["b_exp"], 1)
            for i in range(2, 7):
                pt_transposes(i)
            pe.wait_ge(S["pt_a"], 4)
            pe.wait_ge(S["pt_d"], 3)
            for g in range(PAGES + 1):
                for p in range(4):
                    if g < PAGES:
                        val, probs = KVP[:, DEC_BATCH * g + 2 * p:DEC_BATCH * g + 2 * p + 2, HD:2 * HD], PTB[:, g, 32 * p:32 * p + 32]
                    else:
                        val, probs = VBN[:], PTB[0:32, g, 32 * p:32 * p + 32]
                    last = mm(BANK[7][32 * p:32 * p + 32, 0:128], probs, val, start=g == 0, stop=g == PAGES,
                              skip_group_check=True)
            last.then_inc(S["vb_all"], 1)

            pe.wait_ge(S["vnew_in"], 16)

            def out_transposes_a(a):
                pe.wait_ge(S["oa_sb"], a + 1)
                pe.wait_ge(S["ot_done"], a + 1)
                for c in range(6):
                    bank, col = (BANK[7], 128 * c) if c < 4 else (BANK[4], 128 * (c - 4))
                    last = tr(bank[:, col:col + 128], OA[:, 128 * c:128 * c + 128], IDENT)
                last.then_inc(S["ob_t"], 1)

            for a in range(4):
                if a >= 2:
                    pe.wait_ge(S["oa_sb"], a - 1)
                for b in (2 * a, 2 * a + 1):
                    rows = slice(64 * (b % 2), 64 * (b % 2) + 64)
                    for k in range(8):
                        if k < 7:
                            pe.wait_ge(av_in[k], 16 * (b + 1))
                        for q in range(2):
                            if k < 7:
                                probs, val = PTA[:, a % 2, k, rows], AV[k][:, 384 * q:384 * q + 384]
                            else:
                                probs, val = PTA[0:32, a % 2, 7, rows], VN2[:, 384 * q:384 * q + 384]
                            last = mm(BANK[2 * (a % 2) + q][rows, 0:384], probs, val, start=k == 0, stop=k == 7)
                        if k < 7:
                            last.then_inc(S["va_used"], 1)
                        elif b % 2:
                            last.then_inc(S["va_pair"], 1)
                        if b % 2 == 0 and k == 1 and a < 3:
                            for i in (7 + 2 * a, 8 + 2 * a):
                                pt_transposes(i)
                        if b % 2 == 0 and k == 3:
                            if a == 0:
                                pe.wait_ge(S["ob_sb"], 1)
                                tr(BANK[4][:, 0:128], OB[:], IDENT).then_inc(S["ob_t"], 1)
                            else:
                                out_transposes_a(a - 1)
                if a < 3:
                    pe.wait_ge(S["pt_a"], PT_DONE_A[a])
                    pe.wait_ge(S["pt_d"], PT_DONE_D[a])
            out_transposes_a(3)

            u0 = FIRST["w_out"]
            pe.wait_ge(S["o_ready"], KD + 1)
            for i in range(2):
                for j in range(4):
                    s = j % 2
                    pe.wait_ge(S["y_part"], KD + i * 4 + j - 1) 
                    unit(u0, i, j, BANK[2 * s:2 * s + 2], OH_, OL_, 0, KD, True, True).then_inc(S["unit_used"], 1)
            layer_norm(1)
            up_stage(1)
            down_stage(1)
            layer_norm(2)
            u0 = FIRST["gate"]
            for m in range(KD):
                s = m % 2
                if m >= 2:
                    pe.wait_ge(S["y_final"], m - 1)
                unit(u0, 0, m, BANK[4 * s:4 * s + 2], XH, XL, 0, KD, True, True, KD * 3 if m == 0 else None)
                for t in range(KP):
                    last = tile(BANK[4 * s + 2:4 * s + 4], (u0 + m) % 2, KD + t, [half(PH, t, n) for n in range(2)],
                                [half(PL, t, n) for n in range(2)], t == 0, t == KP - 1)
                last.then_inc(S["unit_used"], 1)


def bucket(d):
    d = np.maximum(d, 0)
    exact = BUCKETS // 2
    scaled = np.log(np.maximum(d, 1) / exact) / log(REL_MAX / exact)
    large = exact + np.floor(scaled * (BUCKETS - exact) + 1e-9).astype(int)
    return np.where(d < exact, d, np.minimum(large, BUCKETS - 1))


def log_count(d):
    count = sum(((d >= 0) & (d <= window) & (d % dil == 0)).astype(int) for window, dil in PATTERNS)
    return np.where(count > 0, np.log(np.maximum(count, 1)), NEG)


def shape_constants():
    p = np.arange(128)
    rows = [16 * (32 * k + p // 4) + p % 4 for k in range(STRIDED_BLOCKS)]
    rows += [PAST - 512 + 128 * k + p for k in range(4)]
    t = np.arange(4)
    patterns = np.zeros((4, 1024), np.float32)
    patterns[:, 0:KEYS_A] = log_count(PAST + t[:, None] - np.concatenate(rows)[None, :])
    patterns[:, KEYS_A:] = (p % 4)[None, :] == t[:, None]
    kb, kt = np.arange(32) // 4, np.arange(32) % 4
    batch = 2 * np.arange(4)[None, :, None] + (p // 64)[:, None, None]
    mask_new = np.where(batch == kb, log_count((p % 4)[:, None, None] - kt), NEG).astype(np.float32)
    consts = np.zeros((128, 352), np.float32)
    consts[:, 0:128] = np.eye(128)
    own = kb[:, None] == kb[None, :]
    consts[0:32, 128:160] = np.where(own & (kt[None, :] <= kt[:, None]), 0.0, NEG)
    consts[64:72, 160:288] = (p % 32 // 4)[None, :] == np.arange(8)[:, None]
    consts[0:32, 160:288] = (4 * (p // 16) + p % 4)[None, :] == np.arange(32)[:, None]
    for a in range(2):
        q = np.arange(32)
        consts[:, 288 + 32 * a:320 + 32 * a] = IDX_SCALE * (
            (q // 4 == 4 * a + p[:, None] // 32) & (q % 4 == p[:, None] % 4))
    onehots = np.zeros((128, 24, 128), np.float32)
    keys = rows + [128 * g + p for g in range(PAGES)]
    for k, r in enumerate(keys):
        for step in range(4):
            onehots[32 * step + bucket(PAST + step - r), k, p] = 1.0
    for step in range(4):
        onehots[32 * step + bucket(step - kt), BLK_NEW, np.arange(32)] = 1.0
    toeplitz = np.zeros((34, 640), np.float32)
    d = 511 - np.arange(640)
    toeplitz[bucket(d), np.arange(640)] = 1.0
    toeplitz[32] = log_count(d)
    toeplitz[33] = np.where(d >= 0, 0.0, NEG)
    rel_rows = np.zeros((2, 16), np.float32)
    rel_rows[0, :HEADS_A] = 1.0
    rel_rows[1, HEADS_A:] = 1.0
    return consts, onehots, patterns, mask_new, toeplitz, rel_rows


def kernel(x_prompt, x_sample, cache_a_kv, cache_b, page_table, p_prompt, p_sample, ln_g, ln_b,
           ffn1_wi, ffn1_wo, w_in, kidx_ln_g, kidx_ln_b, w_out, ffn2_wi, ffn2_wo, ple_proj, ple_gate,
           rel_bias):
    import concourse.bacc as bacc
    from concourse.bass_utils import run_bass_kernel_spmd

    def features(a, b, chunks):
        both = np.concatenate([np.asarray(a).reshape(SEQ, -1), np.asarray(b).reshape(NDEC, -1)])
        return np.ascontiguousarray(both.T.reshape(chunks, 128, T).transpose(1, 0, 2))

    def units(a, tiles, count, parts=1):
        a = np.asarray(a).reshape(parts, tiles, 128, count, 128)
        return a.transpose(3, 0, 2, 1, 4).reshape(count * parts, 128, tiles, 128)

    def up_units(a):
        u = units(a, KD, 2 * KF)
        return np.ascontiguousarray(u.reshape(2, KF, 128, KD, 128).transpose(1, 0, 2, 3, 4)).reshape(2 * KF, 128, KD, 128)

    wa, wb, wi_ = WIDTH_A, HEADS_B * HD, IDX_HEADS * HD
    w_in0 = np.asarray(w_in)[0]
    at = np.cumsum([0, wa, wa, wa, wb, HD, HD, wi_, HD, IDX_HEADS])
    qa, ka, va, qb, kb, vb, qi, ki, wi = (w_in0[:, at[n]:at[n + 1]] for n in range(9))
    pad = np.zeros((D_MODEL, 128 - HD - IDX_HEADS), w_in0.dtype)
    w_proj = np.concatenate([qi, ki, wi, pad, kb, vb, ka, va, qa, qb], axis=1)
    gate = units(np.asarray(ple_gate)[0], KD, KD)
    ple = units(np.asarray(ple_proj)[0], KP, KD)
    w = {
        "wi1": up_units(np.asarray(ffn1_wi)[0]),
        "wo1": units(np.asarray(ffn1_wo)[0], UNIT_TILES, KD, 2),
        "w_in": units(w_proj, KD, N_PROJ),
        "w_out": units(np.asarray(w_out)[0], KD, KD),
        "wi2": up_units(np.asarray(ffn2_wi)[0]),
        "wo2": units(np.asarray(ffn2_wo)[0], UNIT_TILES, KD, 2),
        "gate": np.concatenate([gate, ple], axis=2),
    }
    ln = np.stack([np.asarray(ln_g)[0], np.asarray(ln_b)[0]], axis=1).reshape(6, KD, 128).transpose(2, 0, 1)
    consts, onehots, patterns, mask_new, toeplitz, rel_rows = shape_constants()
    n_pool = np.asarray(cache_b).shape[1]
    arrays = {
        "x_t": features(x_prompt, x_sample, KD),
        "p_t": features(p_prompt, p_sample, KP),
        "cache_a": np.asarray(cache_a_kv).reshape(DEC_BATCH, PAST, 2 * WIDTH_A),
        "cache_b": np.asarray(cache_b).reshape(n_pool, PAGE, ROW_B),
        "page_table": np.asarray(page_table),
        "ln": ln,
        "kidx_g": np.asarray(kidx_ln_g)[0],
        "kidx_b": np.asarray(kidx_ln_b)[0],
        "rel_bias": np.asarray(rel_bias),
        "rel_rows": rel_rows, "consts": consts, "onehots": onehots,
        "patterns": patterns, "mask_new": mask_new, "toeplitz": toeplitz,
    }
    arrays.update({"w_" + name: a for name, a in w.items()})
    arrays = {name: np.ascontiguousarray(a) for name, a in arrays.items()}
    outs = {
        "y_t": (KD, 128, T), "kv_a_t": (12, 128, SEQ), "a_sample": (DEC_BATCH, PAST, 2 * WIDTH_A),
        "kv_b_t": (128, T), "ki_b": (128, 5, HD),
    }
    nc = bacc.Bacc("TRN2", target_bir_lowering=False, num_devices=1)
    ins = {name: nc.dram_tensor("in_" + name, a.shape, mybir.dt.from_np(a.dtype), kind="ExternalInput").ap()
           for name, a in arrays.items()}
    res = {name: nc.dram_tensor("out_" + name, shape, F32, kind="ExternalOutput").ap() for name, shape in outs.items()}
    weights = {name: ins.pop("w_" + name) for name in w}
    build_program(nc, w=weights, **ins, **res)
    r = run_bass_kernel_spmd(nc, [{"in_" + name: a for name, a in arrays.items()}], core_ids=[0]).results[0]

    y = r["out_y_t"].transpose(2, 0, 1).reshape(T, D_MODEL)
    kv = r["out_kv_a_t"].reshape(2, HEADS_A, HD, SEQ).transpose(3, 0, 1, 2)
    row_b = np.concatenate([r["out_kv_b_t"].T, r["out_ki_b"].transpose(1, 0, 2).reshape(640, HD)[:T]], axis=1)
    return (
        y[:SEQ].reshape(1, SEQ, D_MODEL), y[SEQ:].reshape(DEC_BATCH, DEC_SEQ, D_MODEL),
        kv.reshape(1, 1, SEQ, 2, HEADS_A, HD),
        r["out_a_sample"].reshape(1, DEC_BATCH, PAST, 2, HEADS_A, HD),
        row_b[:SEQ].reshape(1, 1, SEQ, ROW_B), row_b[SEQ:].reshape(1, DEC_BATCH, DEC_SEQ, ROW_B),
    )
```
